# Optimizing a Trainium2 kernel written in Bass

```python
import jax, jax.numpy as jnp
from jax import lax
import numpy as np

D_MODEL = 1024
BATCH = 1
SEQ = 256
DEPTH = 2

CONV_WIDTH = D_MODEL // 2
CONV_GROUPS = 8
CONV_K = 3
HEAD_DIM = 64
ATT_WIDTH = D_MODEL - CONV_WIDTH
ATT_HEADS = ATT_WIDTH // HEAD_DIM
IN_WIDTH = 3 * CONV_WIDTH + 3 * ATT_WIDTH
MOBA_BLOCK = 256
MOBA_TOPK = 3
QUERY_CHUNK = 32
ROPE_THETA = 10000.0
N_GROUPS = 4
EXPERTS_PER_GROUP = 4
N_EXPERTS = N_GROUPS * EXPERTS_PER_GROUP
TOP_K_IN_GROUP = 2
D_FF_EXPERT = D_MODEL // 4
EPS = 1e-6
NEG = -1e30

kernel_name = "hymba_conv_moba_hmoe_adaln"

def rmsnorm(x, g):
    xf = x.astype(jnp.float32)
    y = xf * lax.rsqrt(jnp.mean(xf * xf, axis=-1, keepdims=True) + EPS)
    return (y * g.astype(jnp.float32)).astype(x.dtype)

def rope(x, positions):
    dh = x.shape[-1]
    inv_freq = ROPE_THETA ** (-jnp.arange(0, dh, 2, dtype=jnp.float32) / dh)
    ang = positions[:, None, :, None].astype(jnp.float32) * inv_freq
    cos, sin = jnp.cos(ang), jnp.sin(ang)
    xf = x.astype(jnp.float32)
    x1, x2 = xf[..., : dh // 2], xf[..., dh // 2:]
    out = jnp.concatenate([x1 * cos - x2 * sin, x2 * cos + x1 * sin], axis=-1)
    return out.astype(x.dtype)

def short_conv_mixer(u_b, u_c, u_h, conv_w):
    gated = u_c * u_h
    rhs = conv_w.reshape(CONV_K, 1, CONV_WIDTH).astype(gated.dtype)
    conv = lax.conv_general_dilated(
        gated, rhs, window_strides=(1,), padding=[(CONV_K - 1, 0)],
        dimension_numbers=("NWC", "WIO", "NWC"), feature_group_count=CONV_WIDTH)
    return u_b * conv

def moba_attention(q, k, v):
    B, H, S, dh = q.shape
    nb = -(-S // MOBA_BLOCK)
    s_pad = nb * MOBA_BLOCK
    pad = [(0, 0), (0, 0), (0, s_pad - S), (0, 0)]
    kb = jnp.pad(k, pad).reshape(B, H, nb, MOBA_BLOCK, dh)
    vb = jnp.pad(v, pad).reshape(B, H, nb, MOBA_BLOCK, dh)
    kmean = jnp.mean(kb.astype(jnp.float32), axis=3)
    n_sel = max(1, min(MOBA_TOPK, nb - 1))
    scale = HEAD_DIM ** -0.5
    n_chunks = S // QUERY_CHUNK
    gather = jax.vmap(jax.vmap(lambda blocks, ix: blocks[ix]))
    blk = jnp.arange(nb)

    def chunk(ci):
        start = ci * QUERY_CHUNK
        qc = lax.dynamic_slice_in_dim(q, start, QUERY_CHUNK, axis=2)
        own = start // MOBA_BLOCK
        qpos = start + jnp.arange(QUERY_CHUNK)
        kpos = own * MOBA_BLOCK + jnp.arange(MOBA_BLOCK)
        k_own = lax.dynamic_index_in_dim(kb, own, axis=2, keepdims=False)
        v_own = lax.dynamic_index_in_dim(vb, own, axis=2, keepdims=False)
        s_own = jnp.einsum("bhqd,bhkd->bhqk", qc, k_own,
                           preferred_element_type=jnp.float32) * scale
        s_own = jnp.where(kpos[None, :] <= qpos[:, None], s_own, NEG)
        gscore = jnp.einsum("bhqd,bhnd->bhqn", qc.astype(jnp.float32), kmean)
        gscore = jnp.where(blk < own, gscore, NEG)
        _, sel = lax.top_k(gscore, n_sel)
        valid = sel < own
        k_sel = gather(kb, sel)
        v_sel = gather(vb, sel)
        s_sel = jnp.einsum("bhqd,bhqnkd->bhqnk", qc, k_sel,
                           preferred_element_type=jnp.float32) * scale
        s_sel = jnp.where(valid[..., None], s_sel, NEG)
        n_l = n_sel * MOBA_BLOCK
        s_all = jnp.concatenate(
            [s_sel.reshape(B, H, QUERY_CHUNK, n_l), s_own], axis=-1)
        p = jax.nn.softmax(s_all, axis=-1)
        p_sel = p[..., :n_l].reshape(B, H, QUERY_CHUNK, n_sel, MOBA_BLOCK).astype(v.dtype)
        p_own = p[..., n_l:].astype(v.dtype)
        out = (jnp.einsum("bhqnk,bhqnkd->bhqd", p_sel, v_sel)
               + jnp.einsum("bhqk,bhkd->bhqd", p_own, v_own))
        return out.astype(q.dtype)

    outs = lax.map(chunk, jnp.arange(n_chunks))
    return outs.transpose(1, 2, 0, 3, 4).reshape(B, H, S, dh)

def hier_moe(h, w_rg, b_rg, w_re, b_re, w_gate, w_up, w_down):
    B, S, D = h.shape
    n = B * S
    t = h.reshape(n, D)
    tok = jnp.arange(n)
    g_logits = (t @ w_rg).astype(jnp.float32) + b_rg.astype(jnp.float32)
    g_prob = jax.nn.softmax(g_logits, axis=-1)
    g_sel = jnp.argmax(g_logits, axis=-1)
    p_group = g_prob[tok, g_sel]
    e_logits = ((t @ w_re).astype(jnp.float32) + b_re.astype(jnp.float32)
                ).reshape(n, N_GROUPS, EXPERTS_PER_GROUP)
    e_in = e_logits[tok, g_sel]
    top_v, top_i = lax.top_k(e_in, TOP_K_IN_GROUP)
    w_sel = jax.nn.softmax(top_v, axis=-1) * p_group[:, None]
    expert_ids = g_sel[:, None] * EXPERTS_PER_GROUP + top_i
    combine = jnp.sum(jax.nn.one_hot(expert_ids, N_EXPERTS, dtype=jnp.float32)
                      * w_sel[..., None], axis=1)
    hid = (jax.nn.silu(jnp.einsum("nd,edf->nef", t, w_gate))
           * jnp.einsum("nd,edf->nef", t, w_up))
    y = jnp.einsum("nef,efd->nd", hid * combine[:, :, None].astype(hid.dtype), w_down)
    return y.reshape(B, S, D)

def setup_inputs(seed: int = 0) -> dict:
    key = jax.random.key(seed)
    ks = jax.random.split(key, 24)
    f32 = jnp.float32
    D, L = D_MODEL, DEPTH

    def nrm(k, shape, s):
        return jax.random.normal(k, shape, f32) * s

    x = jax.random.normal(ks[0], (BATCH, SEQ, D), f32)
    c = jax.random.normal(ks[1], (BATCH, D), f32)
    offset = jax.random.randint(ks[2], (BATCH, 1), 0, 4096, dtype=jnp.int32)
    positions = offset + jnp.arange(SEQ, dtype=jnp.int32)[None, :]
    return {
        "x": x,
        "c": c,
        "positions": positions,
        "norm1_g": 1.0 + nrm(ks[3], (L, D), 0.02),
        "norm2_g": 1.0 + nrm(ks[4], (L, D), 0.02),
        "w_ada": nrm(ks[5], (L, D, 6 * D), 0.5 * D ** -0.5),
        "b_ada": nrm(ks[6], (L, 6 * D), 0.02),
        "w_in": nrm(ks[7], (L, D, IN_WIDTH), D ** -0.5),
        "conv_w": nrm(ks[8], (L, CONV_K, CONV_WIDTH), CONV_K ** -0.5),
        "q_norm_g": 1.0 + nrm(ks[9], (L, HEAD_DIM), 0.02),
        "k_norm_g": 1.0 + nrm(ks[10], (L, HEAD_DIM), 0.02),
        "conv_out_g": 1.0 + nrm(ks[11], (L, CONV_WIDTH), 0.02),
        "attn_out_g": 1.0 + nrm(ks[12], (L, ATT_WIDTH), 0.02),
        "w_out": nrm(ks[13], (L, D, D), D ** -0.5),
        "w_router_group": nrm(ks[14], (L, D, N_GROUPS), D ** -0.5),
        "b_router_group": nrm(ks[15], (L, N_GROUPS), 0.01),
        "w_router_expert": nrm(ks[16], (L, D, N_EXPERTS), D ** -0.5),
        "b_router_expert": nrm(ks[17], (L, N_EXPERTS), 0.01),
        "w_gate": nrm(ks[18], (L, N_EXPERTS, D, D_FF_EXPERT), D ** -0.5),
        "w_up": nrm(ks[19], (L, N_EXPERTS, D, D_FF_EXPERT), D ** -0.5),
        "w_down": nrm(ks[20], (L, N_EXPERTS, D_FF_EXPERT, D), D_FF_EXPERT ** -0.5),
    }

def reference(x, c, positions, norm1_g, norm2_g, w_ada, b_ada, w_in, conv_w,
              q_norm_g, k_norm_g, conv_out_g, attn_out_g, w_out,
              w_router_group, b_router_group, w_router_expert, b_router_expert,
              w_gate, w_up, w_down):
    B, S, D = x.shape
    cw, aw = CONV_WIDTH, ATT_WIDTH
    split_at = [cw, 2 * cw, 3 * cw, 3 * cw + aw, 3 * cw + 2 * aw]
    c_act = jax.nn.silu(c)

    def heads(u):
        return u.reshape(B, S, ATT_HEADS, HEAD_DIM).transpose(0, 2, 1, 3)

    for l in range(DEPTH):
        mod = (c_act @ w_ada[l] + b_ada[l])[:, None, :]
        shift1, scale1, gate1, shift2, scale2, gate2 = jnp.split(mod, 6, axis=-1)

        h = rmsnorm(x, norm1_g[l]) * (1.0 + scale1) + shift1
        u = h @ w_in[l]
        u_b, u_c, u_h, u_q, u_k, u_v = jnp.split(u, split_at, axis=-1)
        y_conv = short_conv_mixer(u_b, u_c, u_h, conv_w[l])
        q = rope(rmsnorm(heads(u_q), q_norm_g[l]), positions)
        k = rope(rmsnorm(heads(u_k), k_norm_g[l]), positions)
        v = heads(u_v)
        y_att = moba_attention(q, k, v).transpose(0, 2, 1, 3).reshape(B, S, aw)
        y_mix = jnp.concatenate(
            [rmsnorm(y_conv, conv_out_g[l]), rmsnorm(y_att, attn_out_g[l])], axis=-1)
        x = x + gate1 * (y_mix @ w_out[l])

        h2 = rmsnorm(x, norm2_g[l]) * (1.0 + scale2) + shift2
        x = x + gate2 * hier_moe(h2, w_router_group[l], b_router_group[l],
                                 w_router_expert[l], b_router_expert[l],
                                 w_gate[l], w_up[l], w_down[l])
    return x


_drawn_inputs = setup_inputs


def setup_inputs(seed=0):
    import zlib

    import numpy as np

    out = dict(_drawn_inputs(seed))
    spreads = {}
    factors = {'norm1_g': 4.453,
     'norm2_g': 4.272,
     'q_norm_g': 8.0,
     'k_norm_g': 8.0,
     'conv_out_g': 6.026,
     'attn_out_g': 6.671,
     'b_router_group': 6.695,
     'b_router_expert': 8.0}
    for name, (base, spread) in spreads.items():
        noise = np.random.default_rng([zlib.crc32(name.encode()), seed]).standard_normal(out[name].shape)
        drawn = base * np.exp(spread * noise) if base else spread * noise
        out[name] = __import__('jax').numpy.asarray(drawn.astype(out[name].dtype))
    for name, factor in factors.items():
        out[name] = (out[name] * factor).astype(out[name].dtype)
    return out
```

```python
from contextlib import ExitStack

import concourse.bass as bass
import numpy as np
from concourse import mybir

ALU = mybir.AluOpType
ACT = mybir.ActivationFunctionType
AX = mybir.AxisListType
F32 = mybir.dt.float32
F32R = mybir.dt.float32r
I32 = mybir.dt.int32

P = 128
EPS = 1e-6
NEG = -1e30
ROPE_THETA = 10000.0
TOP_MAGIC = 12582912.0
TWO_PI_A = 6.28125
TWO_PI_B = 0.00193500518798828125
TWO_PI_C = 2 * np.pi - TWO_PI_A - TWO_PI_B
PI_IN = 3.1415925
RING = 4
PASSES = ((0, 0), (0, 1), (1, 0))


def trunk(nc, x, c, positions, norm1_g, norm2_g, w_ada, b_ada, w_in, conv_w, q_norm_g, k_norm_g,
          conv_out_g, attn_out_g, w_out, w_rg, b_rg, w_re, b_re, w_gate, w_up, w_down, out):
    _, S, D = x.shape
    L = norm1_g.shape[0]
    CW = conv_out_g.shape[1]
    AW = attn_out_g.shape[1]
    HD = q_norm_g.shape[1]
    H = AW // HD
    NE, _, F = w_gate.shape[1:]
    NG = w_rg.shape[2]
    EG = NE // NG
    NR = NG + NE
    T = S // P
    KD = D // P
    KC = CW // P
    HH = HD // 2
    SCALE = float(HD) ** -0.5
    assert (S, D, CW, AW, HD, F) == (256, 1024, 512, 512, 64, 256)
    UL = 16 + 3 * NE
    NU = L * UL

    x_v = x.rearrange("a (t p) d -> (a p) t d", p=P)
    out_v = out.rearrange("a (t p) d -> (a p) t d", p=P)
    win_v = w_in.rearrange("l (p k) n -> l p k n", k=KD)
    wout_v = w_out.rearrange("l (s p k) n -> l s p k n", s=2, k=KC)
    ada_v = w_ada.rearrange("l (p k) n -> l p k n", k=KD)
    gate_v = w_gate.rearrange("l e (p k) f -> l e p k f", k=KD)
    up_v = w_up.rearrange("l e (p k) f -> l e p k f", k=KD)
    down_v = w_down.rearrange("l e (p k) d -> l e p k d", k=2)
    IN_ORDER = (3, 4, 5, 0, 1, 2)

    with ExitStack() as ctx:
        def sb(name, shape, dt=F32):
            return ctx.enter_context(nc.sbuf_tensor(name, shape, dt))

        def sem(name):
            return ctx.enter_context(nc.semaphore(name))

        ps = ctx.enter_context(nc.psum_tensor("ps", [P, 8, 512], F32))

        raw = sb("raw", [P, RING, 2048])
        whi = sb("whi", [P, RING, 2048], F32R)
        wlo = sb("wlo", [P, RING, 2048], F32R)
        ada_raw = sb("ada_raw", [P, 2, 4, 512])
        ada_bias = sb("ada_bias", [P, 512])
        mod_rows = sb("mod_rows", [P, D])
        gates = sb("gates", [P, 2, D])
        res = sb("res", [P, T, D])
        act_hi = sb("act_hi", [P, KD, S], F32R)
        act_lo = sb("act_lo", [P, KD, S], F32R)
        tokmaj = sb("tokmaj", [P, T, D])
        qkT = sb("qkT", [P, 2, H // 2, S])
        v_sb = sb("v_sb", [P, T, AW])
        cb = sb("cb", [P, KC, S])
        cc = sb("cc", [P, KC, S])
        cg = sb("cg", [P, KC, S + 2])
        work = sb("work", [P, 2, 4, 384])
        wflat = work[:, :, :, :].rearrange("p a b c -> p (a b c)")
        hf = wflat[:, 0:KD * S].rearrange("p (k s) -> p k s", k=KD)
        ident = sb("ident", [P, P])
        ones = sb("ones", [P, P])
        rowsel = sb("rowsel", [P, P])
        mask = sb("mask", [P, 384])
        c_col = sb("c_col", [P, KD])
        c_rep = sb("c_rep", [P, KD, 32])
        g_norm = sb("g_norm", [P, 2, L, KD])
        g_qk = sb("g_qk", [P, L, 2, HD])
        g_conv = sb("g_conv", [P, L, KC])
        g_attn = sb("g_attn", [P, L, KC])
        w_conv = sb("w_conv", [P, L, 3, KC])
        r_w = wflat[:, 0:L * KD * NR].rearrange("p (l k n) -> p l k n", l=L, k=KD)
        r_hi = sb("r_hi", [P, L, KD, NR], F32R)
        r_lo = sb("r_lo", [P, L, KD, NR], F32R)
        r_b = sb("r_b", [P, L, NR])
        pos_i = sb("pos_i", [P, T], I32)
        pos_f = sb("pos_f", [P, T])
        invf = sb("invf", [P, HH])
        ang = wflat[:, 512:512 + 3 * T * HH].rearrange("p (a t d) -> p a t d", a=3, t=T)
        sincos = sb("sincos", [P, 2, T, HH])
        trig = sb("trig", [P, 2, T, 2, HD])
        mod_t = sb("mod_t", [P, 2, 2, KD])
        stat = sb("stat", [P, 64])
        rt = sb("rt", [P, 10, T, NR])
        rank = sb("rank", [P, NE])
        combine = sb("combine", [P, T, NE])
        sil = wflat[:, 0:T * F].rearrange("p (t f) -> p t f", t=T)
        hid = wflat[:, T * F:2 * T * F].rearrange("p (t f) -> p t f", t=T)
        hidT_hi = sb("hidT_hi", [P, 2, S], F32R)
        hidT_lo = sb("hidT_lo", [P, 2, S], F32R)

        par_in = sem("par_in")
        raw_full = [sem(f"raw_full{r}") for r in range(RING)]
        ada_full = [sem(f"ada_full{r}") for r in range(2)]
        bias_full = sem("bias_full")
        out_done = sem("out_done")
        hi_done = sem("hi_done")
        lo_done = sem("lo_done")
        unit_used = sem("unit_used")
        const_ready = sem("const_ready")
        rowsel_ready = sem("rowsel_ready")
        crep_ready = sem("crep_ready")
        ada_used = sem("ada_used")
        acc_done = sem("acc_done")
        mod_evac = sem("mod_evac")
        mod_used = sem("mod_used")
        mod_ready = sem("mod_ready")
        gate_done = sem("gate_done")
        gate_evac = sem("gate_evac")
        rstd_sum = sem("rstd_sum")
        rstd_root = sem("rstd_root")
        xn_ready = sem("xn_ready")
        xT_done = sem("xT_done")
        hf_ready = sem("hf_ready")
        act_ready = sem("act_ready")
        proj_evac = sem("proj_evac")
        qk_sum = sem("qk_sum")
        qk_root = sem("qk_root")
        rope_done = sem("rope_done")
        qkT_done = sem("qkT_done")
        qkT_ready = sem("qkT_ready")
        gated_done = sem("gated_done")
        scores_done = sem("scores_done")
        max_ready = sem("max_ready")
        exp_done = sem("exp_done")
        pT_done = sem("pT_done")
        pT_ready = sem("pT_ready")
        pv_done = sem("pv_done")
        yconv_ready = sem("yconv_ready")
        csq_ready = sem("csq_ready")
        csum_done = sem("csum_done")
        croot = sem("croot")
        ymc_ready = sem("ymc_ready")
        yatt_raw = sem("yatt_raw")
        yatt_sum = sem("yatt_sum")
        yatt_root = sem("yatt_root")
        yatt_ready = sem("yatt_ready")
        yT_done = sem("yT_done")
        yf_ready = sem("yf_ready")
        yma_ready = sem("yma_ready")
        logit_done = sem("logit_done")
        rexp_in = sem("rexp_in")
        rexp_out = sem("rexp_out")
        rw_ready = sem("rw_ready")
        gu_done = sem("gu_done")
        sil_done = sem("sil_done")
        hid_ready = sem("hid_ready")
        hidT_done = sem("hidT_done")
        hidT_hi_done = sem("hidT_hi_done")
        hidT_ready = sem("hidT_ready")
        res_ready = sem("res_ready")
        act_step = sem("act_step")
        dve_step = sem("dve_step")
        pool_step = sem("pool_step")

        block = ctx.enter_context(nc.Block())
        NPAR = 11 + 3 * L

        @block.sync
        def _(sp):
            def raw_slot(n):
                if n >= RING:
                    sp.wait_ge(lo_done, n - RING + 1)
                return raw[:, n % RING, :]

            def ada_half(a):
                l, h = a // 2, a % 2
                for b in range(6):
                    B = 6 * a + b
                    cols = slice((h * 6 + b) * 512, (h * 6 + b + 1) * 512)
                    for u in range(2):
                        if B >= 1:
                            sp.wait_ge(ada_used, 2 * (B - 1) + u + 1)
                        sp.dma_start(ada_raw[:, u, :, :], ada_v[l, :, 4 * u:4 * u + 4, cols]
                                     ).then_inc(ada_full[u], 16)
                    if B >= 1:
                        sp.wait_ge(acc_done, B)
                    else:
                        sp.wait_ge(const_ready, 1)
                    sp.dma_start(ada_bias[0:1, :], b_ada[l:l + 1, cols]
                                 ).then_inc(bias_full, 16)

            ada_half(0)
            for l in range(L):
                n0 = l * UL
                for i in range(12):
                    blk, half = IN_ORDER[i // 2], i % 2
                    sp.dma_start(raw_slot(n0 + i).rearrange("p (k n) -> p k n", k=4),
                                 win_v[l, :, 4 * half:4 * half + 4, blk * 512:(blk + 1) * 512]
                                 ).then_inc(raw_full[(n0 + i) % RING], 16)
                for i in range(4):
                    sp.dma_start(raw_slot(n0 + 12 + i).rearrange("p (k n) -> p k n", k=2),
                                 wout_v[l, i // 2, :, 2 * (i % 2):2 * (i % 2) + 2, :]
                                 ).then_inc(raw_full[(n0 + 12 + i) % RING], 16)
                ada_half(2 * l + 1)
                if l + 1 < L:
                    ada_half(2 * l + 2)
                for e in range(NE):
                    n = n0 + 16 + 3 * e
                    for half in range(2):
                        slot = raw_slot(n + half).rearrange("p (g k f) -> p g k f", g=2, k=4)
                        for g, w in enumerate((gate_v, up_v)):
                            sp.dma_start(slot[:, g, :, :], w[l, e, :, 4 * half:4 * half + 4, :]
                                         ).then_inc(raw_full[(n + half) % RING], 8 * 2)
                    sp.dma_start(raw_slot(n + 2).rearrange("p (k n) -> p k n", k=2), down_v[l, e]
                                 ).then_inc(raw_full[(n + 2) % RING], 16)
            sp.wait_ge(res_ready, 2 * L)
            sp.dma_start(out_v, res[:, :, :]).then_inc(out_done, 16)
            sp.wait_ge(out_done, 16)

        def raw_landed(n):
            total = 0
            for m in range(n % RING, n + 1, RING):
                i = m % UL - 16
                total += 32 if i >= 0 and i % 3 < 2 else 16
            return total

        @block.gpsimd
        def _(pool):
            pool.memset(ident[:, :], 0.0).then_inc(pool_step, 1)
            pool.memset(mask[:, :], 0.0).then_inc(pool_step, 1)
            pool.memset(ones[:, :], 1.0)
            for i in range(HH):
                pool.memset(invf[:, i:i + 1],
                            float(np.float32(ROPE_THETA) ** (-np.float32(2 * i) / np.float32(HD))))
            for i in range(NE):
                pool.memset(rank[:, i:i + 1], float(NE - i))
            pool.memset(cg[:, :, 0:2], 0.0)
            pool.memset(ada_bias[:, :], 0.0).then_inc(const_ready, 1)
            pool.wait_ge(pool_step, 1)
            pool.affine_select(out=ident[:, :], in_=ident[:, :], compare_op=ALU.not_equal, fill=1.0,
                               base=0, pattern=[[-1, P]], channel_multiplier=1).then_inc(const_ready, 1)
            pool.wait_ge(pool_step, 2)
            for a in (0, 256):
                last = pool.affine_select(out=mask[:, a:a + P], in_=mask[:, a:a + P], compare_op=ALU.is_ge,
                                          fill=NEG, base=0, pattern=[[-1, P]], channel_multiplier=1)
            last.then_inc(const_ready, 1)

        @block.scalar
        def _(act):
            steps = [0]

            def link(ins):
                steps[0] += 1
                ins.then_inc(act_step, 1)
                act.wait_ge(act_step, steps[0])

            def load(dst, src):
                act.dma_start(dst, src).then_inc(par_in, 16)

            load(c_col[:, :], c.rearrange("a (p k) -> (a p) k", k=KD))
            load(res[:, :, :], x_v)
            with nc.allow_non_contiguous_dma(reason="256 positions, one to a partition"):
                load(pos_i[:, :], positions.rearrange("a (t p) -> (a p) t", p=P))
            load(g_norm[:, 0, :, :], norm1_g.rearrange("l (p k) -> p l k", k=KD))
            load(g_norm[:, 1, :, :], norm2_g.rearrange("l (p k) -> p l k", k=KD))
            load(g_qk[:, :, 0, :], q_norm_g.partition_broadcast(P))
            load(g_qk[:, :, 1, :], k_norm_g.partition_broadcast(P))
            load(g_conv[:, :, :], conv_out_g.rearrange("l (p k) -> p l k", k=KC))
            load(g_attn[:, :, :], attn_out_g.rearrange("l (p k) -> p l k", k=KC))
            for l in range(L):
                load(w_conv[:, l, :, :], conv_w[l].rearrange("r (p k) -> p r k", k=KC))
            load(r_b[:, :, 0:NG], b_rg.partition_broadcast(P))
            load(r_b[:, :, NG:NR], b_re.partition_broadcast(P))
            for l in range(L):
                load(r_w[:, l, :, 0:NG], w_rg[l].rearrange("(p k) n -> p k n", k=KD))
            for l in range(L):
                load(r_w[:, l, :, NG:NR], w_re[l].rearrange("(p k) n -> p k n", k=KD))

            def split(n):
                act.wait_ge(raw_full[n % RING], raw_landed(n))
                if n >= RING:
                    act.wait_ge(unit_used, n - RING + 1)
                act.activation(whi[:, n % RING, :], raw[:, n % RING, :], ACT.Copy).then_inc(hi_done, 1)

            def ahead(n):
                if n < NU:
                    split(n)

            def ada_block(a, b):
                B = 6 * a + b
                act.wait_ge(acc_done, B + 1)
                if b in (2, 4):
                    act.wait_ge(mod_used, 2 * a + b // 2)
                act.activation(mod_rows[:, (b % 2) * 512:(b % 2 + 1) * 512], ps[:, 4 + b % 2, :],
                               ACT.Copy).then_inc(mod_evac, 1)
                if b == 5:
                    if a >= 2:
                        act.wait_ge(res_ready, a - 1)
                    for n in range(2):
                        act.wait_ge(gate_done, 2 * a + n + 1)
                        act.activation(gates[:, a % 2, n * 512:(n + 1) * 512], ps[:, 7, :],
                                       ACT.Copy).then_inc(gate_evac, 1)

            def norm_root(m):
                act.wait_ge(rstd_sum, m + 1)
                act.activation(stat[:, 2:4], stat[:, 0:2], ACT.Sqrt, scale=1.0 / D,
                               bias=eps_col).then_inc(rstd_root, 1)

            def norm_evac(m):
                act.wait_ge(mod_ready, m + 1)
                for bank in range(4):
                    act.wait_ge(xT_done, 4 * m + bank + 1)
                    for j in (2 * bank, 2 * bank + 1):
                        ins = act.activation(hf[:, j, :], ps[:, bank, (j % 2) * S:(j % 2 + 1) * S],
                                             ACT.Identity, scale=mod_t[:, m % 2, 1, j:j + 1],
                                             bias=mod_t[:, m % 2, 0, j:j + 1])
                    ins.then_inc(hf_ready, 1)

            act.wait_ge(par_in, 16)
            act.wait_ge(par_in, 16 * NPAR)
            eps_col = stat[:, 63:64]
            act.wait_ge(crep_ready, 1)
            link(act.activation(stat[:, 40:40 + KD], c_col[:, :], ACT.Silu))
            act.activation(c_rep[:, :, :], stat[:, 40:40 + KD].unsqueeze(2).to_broadcast([P, KD, 32]),
                           ACT.Copy).then_inc(crep_ready, 1)
            act.wait_ge(crep_ready, 3)
            act.activation(sincos[:, :, :, :], ang[:, 0:2, :, :], ACT.Sin).then_inc(crep_ready, 1)
            for b in range(6):
                ada_block(0, b)
            for n in range(RING):
                split(n)
            for l in range(L):
                n0 = l * UL
                m = 2 * l
                norm_root(m)
                norm_evac(m)
                split(n0 + 4)
                split(n0 + 5)
                for w in range(2):
                    act.wait_ge(unit_used, n0 + 2 * w + 2)
                    for t in range(T):
                        ins = act.activation(tokmaj[:, t, w * AW:(w + 1) * AW], ps[:, 4 + 2 * w + t, :],
                                             ACT.Copy)
                    ins.then_inc(proj_evac, 1)
                    if w == 0:
                        split(n0 + 6)
                        split(n0 + 7)
                act.wait_ge(unit_used, n0 + 6)
                act.activation(v_sb[:, :, :], ps[:, 0:2, :], ACT.Copy).then_inc(proj_evac, 1)
                split(n0 + 8)
                split(n0 + 9)
                act.wait_ge(qk_sum, l + 1)
                act.activation(stat[:, 4:36], stat[:, 4:36], ACT.Sqrt, scale=1.0 / HD,
                               bias=eps_col).then_inc(qk_root, 1)
                act.wait_ge(unit_used, n0 + 8)
                act.activation(cb[:, :, :], ps[:, 2:4, :].rearrange("p a (b s) -> p (a b) s", s=S),
                               ACT.Copy).then_inc(proj_evac, 1)
                split(n0 + 10)
                split(n0 + 11)
                act.wait_ge(unit_used, n0 + 10)
                act.activation(cc[:, :, :], ps[:, 4:6, :].rearrange("p a (b s) -> p (a b) s", s=S),
                               ACT.Copy).then_inc(proj_evac, 1)
                for w in range(2):
                    act.wait_ge(qkT_done, 2 * l + w + 1)
                    act.activation(qkT[:, w, :, :],
                                   ps[:, 2 * w:2 * w + 2, :].rearrange("p a (b s) -> p (a b) s", s=S),
                                   ACT.Copy).then_inc(qkT_ready, 1)
                split(n0 + 12)
                split(n0 + 13)

                def exps(g):
                    act.wait_ge(max_ready, 2 * l + g + 1)
                    for h in range(4):
                        for t in range(T):
                            cols = slice(0, P) if t == 0 else slice(P, 384)
                            col = 16 * g + 4 * t + h
                            ins = act.activation(work[:, g, h, cols], work[:, g, h, cols], ACT.Exp,
                                                 bias=stat[:, 4 + col:5 + col],
                                                 accum_out=stat[:, 12 + col:13 + col])
                    ins.then_inc(exp_done, 1)

                a = 2 * l + 1
                exps(0)
                split(n0 + 14)
                split(n0 + 15)
                for b in range(6):
                    ada_block(a, b)
                exps(1)
                for g in range(2):
                    act.wait_ge(pT_done, 2 * l + g + 1)
                    act.activation(work[:, g, :, :], ps[:, 4 * g:4 * g + 4, 0:384], ACT.Copy
                                   ).then_inc(pT_ready, 1)
                act.wait_ge(yconv_ready, l + 1)
                act.activation(cb[:, :, :], cc[:, :, :], ACT.Square).then_inc(csq_ready, 1)
                act.wait_ge(csum_done, l + 1)
                act.activation(cb[:, 0, :], ps[:, 2, 0:S], ACT.Sqrt, scale=1.0 / CW,
                               bias=eps_col).then_inc(croot, 1)
                act.wait_ge(yatt_sum, l + 1)
                act.activation(stat[:, 2:4], stat[:, 0:2], ACT.Sqrt, scale=1.0 / AW,
                               bias=eps_col).then_inc(yatt_root, 1)
                act.wait_ge(yT_done, l + 1)
                for j in range(KC):
                    ins = act.activation(hf[:, KC + j, :], ps[:, j // 2, (j % 2) * S:(j % 2 + 1) * S],
                                         ACT.Copy, scale=g_attn[:, l, j:j + 1])
                ins.then_inc(yf_ready, 1)
                m = 2 * l + 1
                norm_root(m)
                norm_evac(m)
                if l + 1 < L:
                    for b in range(6):
                        ada_block(2 * l + 2, b)
                for n in range(4):
                    split(n0 + 16 + n)
                act.wait_ge(rexp_in, 2 * l + 1)
                act.activation(rt[:, 8, :, 0:NG], rt[:, 8, :, 0:NG], ACT.Exp).then_inc(rexp_out, 1)
                act.wait_ge(rexp_in, 2 * l + 2)
                act.activation(stat[:, 36:38], stat[:, 36:38], ACT.Exp).then_inc(rexp_out, 1)
                for e in range(NE):
                    E = l * NE + e
                    for t in range(T):
                        if t == 0:
                            act.wait_ge(gu_done, E + 1)
                        else:
                            act.wait_ge(unit_used, n0 + 16 + 3 * e + 2)
                        if E > 0:
                            act.wait_ge(hid_ready, T * (E - 1) + t + 1)
                        act.activation(sil[:, t, :], ps[:, 4 + t, 0:F], ACT.Silu).then_inc(sil_done, 1)
                    ahead(n0 + 16 + 3 * e + 4)
                    ahead(n0 + 16 + 3 * e + 5)
                    act.wait_ge(hidT_done, E + 1)
                    act.activation(hidT_hi[:, :, :], ps[:, 6, :].rearrange("p (k s) -> p k s", k=2),
                                   ACT.Copy).then_inc(hidT_hi_done, 1)
                    ahead(n0 + 16 + 3 * e + 6)

        @block.vector
        def _(dve):
            steps = [0]

            def link(ins):
                steps[0] += 1
                ins.then_inc(dve_step, 1)
                dve.wait_ge(dve_step, steps[0])

            def split(n):
                dve.wait_ge(hi_done, n + 1)
                dve.tensor_tensor(wlo[:, n % RING, :], raw[:, n % RING, :],
                                  whi[:, n % RING, :].bitcast(F32), ALU.subtract).then_inc(lo_done, 1)

            def ahead(n):
                if n < NU:
                    split(n)

            dve.memset(stat[:, 63:64], EPS).then_inc(crep_ready, 1)
            link(dve.memset(rowsel[:, :], 0.0))
            for q in range(4):
                last = dve.memset(rowsel[32 * q:32 * q + 1, :], 1.0)
            last.then_inc(rowsel_ready, 1)
            dve.wait_ge(par_in, 16 * NPAR)
            link(dve.tensor_copy(pos_f[:, :], pos_i[:, :]))
            dve.wait_ge(const_ready, 1)
            for t in range(T):
                last = dve.tensor_scalar(ang[:, 0, t, :], invf[:, :], pos_f[:, t:t + 1], None, ALU.mult)
            link(last)
            link(dve.tensor_scalar(ang[:, 1, :, :], ang[:, 0, :, :], 1.0 / (2 * np.pi), TOP_MAGIC,
                                   ALU.mult, ALU.add))
            link(dve.tensor_scalar(ang[:, 2, :, :], ang[:, 1, :, :], -TOP_MAGIC, None, ALU.add))
            for part in (TWO_PI_A, TWO_PI_B, TWO_PI_C):
                link(dve.scalar_tensor_tensor(out=ang[:, 0, :, :], in0=ang[:, 2, :, :], scalar=-float(part),
                                              in1=ang[:, 0, :, :], op0=ALU.mult, op1=ALU.add))
            link(dve.tensor_scalar(ang[:, 1, :, :], ang[:, 0, :, :], float(np.pi / 2), None, ALU.add))
            link(dve.tensor_scalar(ang[:, 2, :, :], ang[:, 1, :, :], float(np.pi), None, ALU.is_gt))
            link(dve.scalar_tensor_tensor(out=ang[:, 1, :, :], in0=ang[:, 2, :, :], scalar=-float(2 * np.pi),
                                          in1=ang[:, 1, :, :], op0=ALU.mult, op1=ALU.add))
            dve.wait_ge(crep_ready, 2)
            dve.tensor_scalar(ang[:, 0:2, :, :], ang[:, 0:2, :, :], PI_IN, -PI_IN, ALU.min, ALU.max
                              ).then_inc(crep_ready, 1)
            link(dve.tensor_copy(r_hi[:, :, :, :], r_w[:, :, :, :]))
            link(dve.tensor_tensor(r_lo[:, :, :, :], r_w[:, :, :, :], r_hi[:, :, :, :].bitcast(F32),
                                   ALU.subtract))
            dve.wait_ge(crep_ready, 4)

            def modulation(a):
                l, h = a // 2, a % 2
                dve.wait_ge(mod_used, 2 * a + 2)
                if a >= 2:
                    dve.wait_ge(hf_ready, 4 * (a - 1))
                link(dve.tensor_copy(mod_t[:, h, 0, :], ps[:, 6, 0:KD]))
                dve.scalar_tensor_tensor(out=mod_t[:, h, 1, :], in0=ps[:, 6, KD:2 * KD], scalar=1.0,
                                         in1=g_norm[:, h, l, :], op0=ALU.add, op1=ALU.mult
                                         ).then_inc(mod_ready, 1)

            def token_norm(m):
                for t in range(T):
                    ins = dve.tensor_tensor_reduce(out=tokmaj[:, t, :], in0=res[:, t, :], in1=res[:, t, :],
                                                   scale=1.0, scalar=0.0, op0=ALU.mult, op1=ALU.add,
                                                   accum_out=stat[:, t:t + 1])
                ins.then_inc(rstd_sum, 1)
                dve.wait_ge(rstd_root, m + 1)
                link(dve.reciprocal(stat[:, 0:2], stat[:, 2:4]))
                for t in range(T):
                    dve.tensor_scalar(tokmaj[:, t, :], res[:, t, :], stat[:, t:t + 1], None, ALU.mult
                                      ).then_inc(xn_ready, 1)

            def activation_parts(m):
                for bank in range(4):
                    dve.wait_ge(hf_ready, 4 * m + bank + 1)
                    js = slice(2 * bank, 2 * bank + 2)
                    link(dve.tensor_copy(act_hi[:, js, :], hf[:, js, :]))
                    dve.tensor_tensor(act_lo[:, js, :], hf[:, js, :], act_hi[:, js, :].bitcast(F32),
                                      ALU.subtract).then_inc(act_ready, 1)

            def residual(l, h, banks):
                dve.wait_ge(gate_evac, 2 * (2 * l + h) + 2)
                for t in range(T):
                    link(dve.tensor_tensor(tokmaj[:, t, :].rearrange("p (a b) -> p a b", a=2),
                                           ps[:, banks + 2 * t:banks + 2 * t + 2, :],
                                           gates[:, h, :].rearrange("p (a b) -> p a b", a=2), ALU.mult))
                    ins = dve.tensor_tensor(res[:, t, :], res[:, t, :], tokmaj[:, t, :], ALU.add)
                    if t == T - 1:
                        ins.then_inc(res_ready, 1)
                        dve.wait_ge(res_ready, 2 * l + h + 1)
                    else:
                        link(ins)

            modulation(0)
            for n in range(RING):
                split(n)
            for l in range(L):
                n0 = l * UL
                token_norm(2 * l)
                activation_parts(2 * l)
                for w in range(2):
                    for s in range(2):
                        for half in range(2):
                            hs = slice(half * HH, half * HH + HH)
                            ins = dve.tensor_tensor(
                                trig[:, s, :, w, hs], sincos[:, 1 - s, :, :],
                                g_qk[:, l, w, hs].unsqueeze(1).to_broadcast([P, T, HH]), ALU.mult)
                link(ins)
                split(n0 + 4)
                split(n0 + 5)
                split(n0 + 6)
                split(n0 + 7)
                dve.wait_ge(proj_evac, 5 * l + 2)
                for t in range(T):
                    link(dve.tensor_tensor(wflat[:, t * 1024:(t + 1) * 1024], tokmaj[:, t, :],
                                           tokmaj[:, t, :], ALU.mult))
                dve.tensor_reduce(stat[:, 4:36], wflat[:, 0:2048].rearrange("p (h d) -> p h d", d=HD),
                                  AX.X, ALU.add).then_inc(qk_sum, 1)
                split(n0 + 8)
                split(n0 + 9)
                dve.wait_ge(qk_root, l + 1)
                link(dve.reciprocal(stat[:, 4:36], stat[:, 4:36]))
                for t in range(T):
                    qk = tokmaj[:, t, :].rearrange("p (h d) -> p h d", d=HD)
                    link(dve.tensor_tensor(qk, qk, stat[:, 4 + 16 * t:20 + 16 * t].unsqueeze(2)
                                           .to_broadcast([P, 2 * H, HD]), ALU.mult))
                    parts = [wflat[:, s * 1024:(s + 1) * 1024] for s in range(2)]
                    for s in range(2):
                        for w in range(2):
                            ins = dve.tensor_tensor(
                                parts[s][:, w * AW:(w + 1) * AW].rearrange("p (h d) -> p h d", d=HD),
                                tokmaj[:, t, w * AW:(w + 1) * AW].rearrange("p (h d) -> p h d", d=HD),
                                trig[:, s, t, w, :].unsqueeze(1).to_broadcast([P, H, HD]), ALU.mult)
                    link(ins)
                    xc, xs = (q.rearrange("p (h a d) -> p h a d", a=2, d=HH) for q in parts)
                    q4 = tokmaj[:, t, :].rearrange("p (h a d) -> p h a d", a=2, d=HH)
                    dve.tensor_tensor(q4[:, :, 0, :], xc[:, :, 0, :], xs[:, :, 1, :], ALU.subtract)
                    ins = dve.tensor_tensor(q4[:, :, 1, :], xc[:, :, 1, :], xs[:, :, 0, :], ALU.add)
                    ins.then_inc(rope_done, 1)
                    dve.wait_ge(rope_done, T * l + t + 1)
                split(n0 + 10)
                split(n0 + 11)
                dve.wait_ge(proj_evac, 5 * l + 5)
                dve.wait_ge(unit_used, n0 + 12)
                dve.tensor_tensor(cg[:, :, 2:S + 2], cc[:, :, :],
                                  ps[:, 6:8, :].rearrange("p a (b s) -> p (a b) s", s=S), ALU.mult
                                  ).then_inc(gated_done, 1)
                split(n0 + 12)
                split(n0 + 13)

                def softmax_max(g):
                    dve.wait_ge(scores_done, 2 * l + g + 1)
                    link(dve.scalar_tensor_tensor(out=work[:, g, :, :], in0=ps[:, 4 * g:4 * g + 4, 0:384],
                                                  scalar=SCALE,
                                                  in1=mask[:, :].unsqueeze(1).to_broadcast([P, 4, 384]),
                                                  op0=ALU.mult, op1=ALU.add))
                    for t in range(T):
                        cols = slice(0, P) if t == 0 else slice(P, 384)
                        ins = dve.tensor_reduce(stat[:, 4 + 16 * g + 4 * t:8 + 16 * g + 4 * t],
                                                work[:, g, :, cols], AX.X, ALU.max, negate=True)
                    ins.then_inc(max_ready, 1)

                softmax_max(0)
                split(n0 + 14)
                split(n0 + 15)
                dve.wait_ge(gated_done, l + 1)
                for j in range(KC):
                    taps = [w_conv[:, l, k, j:j + 1] for k in range(3)]
                    link(dve.tensor_scalar(cc[:, j, :], cg[:, j, 0:S], taps[0], None, ALU.mult))
                    for k in (1, 2):
                        link(dve.scalar_tensor_tensor(out=cc[:, j, :], in0=cg[:, j, k:k + S], scalar=taps[k],
                                                      in1=cc[:, j, :], op0=ALU.mult, op1=ALU.add))
                dve.tensor_tensor(cc[:, :, :], cc[:, :, :], cb[:, :, :], ALU.mult).then_inc(yconv_ready, 1)
                modulation(2 * l + 1)
                softmax_max(1)
                dve.wait_ge(croot, l + 1)
                link(dve.reciprocal(cb[:, 1, :], cb[:, 0, :]))
                for j in range(KC):
                    ins = dve.scalar_tensor_tensor(out=cc[:, j, :], in0=cc[:, j, :],
                                                   scalar=g_conv[:, l, j:j + 1], in1=cb[:, 1, :],
                                                   op0=ALU.mult, op1=ALU.mult)
                link(ins)
                link(dve.tensor_copy(act_hi[:, 0:KC, :], cc[:, :, :]))
                dve.tensor_tensor(act_lo[:, 0:KC, :], cc[:, :, :], act_hi[:, 0:KC, :].bitcast(F32),
                                  ALU.subtract).then_inc(ymc_ready, 1)
                dve.wait_ge(exp_done, 2 * l + 2)
                sums = stat[:, 12:36].rearrange("p (a b) -> p a b", b=8)[:, 0:3:2, :]
                link(dve.reciprocal(sums, sums))
                dve.wait_ge(pv_done, l + 1)
                for t in range(T):
                    for g in range(2):
                        ins = dve.tensor_tensor(
                            tokmaj[:, t, g * 256:(g + 1) * 256].rearrange("p (h d) -> p h d", d=HD),
                            ps[:, t, g * 256:(g + 1) * 256].rearrange("p (h d) -> p h d", d=HD),
                            stat[:, 12 + 16 * g + 4 * t:16 + 16 * g + 4 * t].unsqueeze(2)
                            .to_broadcast([P, 4, HD]), ALU.mult)
                link(ins)
                for t in range(T):
                    ins = dve.tensor_tensor_reduce(out=tokmaj[:, t, AW:2 * AW], in0=tokmaj[:, t, 0:AW],
                                                   in1=tokmaj[:, t, 0:AW], scale=1.0, scalar=0.0,
                                                   op0=ALU.mult, op1=ALU.add, accum_out=stat[:, t:t + 1])
                ins.then_inc(yatt_sum, 1)
                dve.wait_ge(yatt_root, l + 1)
                link(dve.reciprocal(stat[:, 0:2], stat[:, 2:4]))
                for t in range(T):
                    ins = dve.tensor_scalar(tokmaj[:, t, 0:AW], tokmaj[:, t, 0:AW], stat[:, t:t + 1], None,
                                            ALU.mult)
                ins.then_inc(yatt_ready, 1)
                dve.wait_ge(yf_ready, l + 1)
                link(dve.tensor_copy(act_hi[:, KC:KD, :], hf[:, KC:KD, :]))
                dve.tensor_tensor(act_lo[:, KC:KD, :], hf[:, KC:KD, :], act_hi[:, KC:KD, :].bitcast(F32),
                                  ALU.subtract).then_inc(yma_ready, 1)
                dve.wait_ge(unit_used, n0 + 16)
                residual(l, 0, 4)
                token_norm(2 * l + 1)
                activation_parts(2 * l + 1)
                if l + 1 < L:
                    modulation(2 * l + 2)
                for n in range(4):
                    split(n0 + 16 + n)
                dve.wait_ge(logit_done, l + 1)
                lg = rt[:, 0, :, :]
                link(dve.tensor_tensor(lg, ps[:, 0, 0:T * NR].rearrange("p (t n) -> p t n", t=T),
                                       r_b[:, l, :].unsqueeze(1).to_broadcast([P, T, NR]), ALU.add))

                def col(i):
                    return stat[:, i:i + T]

                def wide(ap, n):
                    return ap.unsqueeze(2).to_broadcast([P, T, n])

                def first_max(values, n, top, onehot):
                    link(dve.tensor_reduce(top, values, AX.X, ALU.max))
                    link(dve.tensor_tensor(onehot, values, wide(top, n), ALU.is_equal))
                    link(dve.tensor_tensor(onehot, onehot, rank[:, NE - n:NE].unsqueeze(1)
                                           .to_broadcast([P, T, n]), ALU.mult))
                    link(dve.tensor_reduce(col(50), onehot, AX.X, ALU.max))
                    link(dve.tensor_tensor(onehot, onehot, wide(col(50), n), ALU.is_equal))

                glog, elog = lg[:, :, 0:NG], lg[:, :, NG:NR]
                goh, oh1, oh2, em = (rt[:, i, :, 0:n] for i, n in ((1, NG), (2, NE), (3, NE), (4, NE)))
                first_max(glog, NG, col(52), goh)
                dve.tensor_tensor(rt[:, 8, :, 0:NG], glog, wide(col(52), NG), ALU.subtract
                                  ).then_inc(rexp_in, 1)
                link(dve.tensor_scalar(rt[:, 5, :, 0:NG], goh, -1.0, -NEG, ALU.add, ALU.mult))
                for t in range(T):
                    e4 = [rt[:, i, t, 0:NE].rearrange("p (g e) -> p g e", e=EG) for i in (4,)][0]
                    link(dve.tensor_tensor(e4, rt[:, 0, t, NG:NR].rearrange("p (g e) -> p g e", e=EG),
                                           rt[:, 1, t, 0:NG].unsqueeze(2).to_broadcast([P, NG, EG]),
                                           ALU.mult))
                    link(dve.tensor_tensor(e4, e4, rt[:, 5, t, 0:NG].unsqueeze(2)
                                           .to_broadcast([P, NG, EG]), ALU.add))
                first_max(em, NE, col(54), oh1)
                link(dve.scalar_tensor_tensor(out=em, in0=oh1, scalar=10 * NEG, in1=em, op0=ALU.mult,
                                              op1=ALU.add))
                first_max(em, NE, col(56), oh2)
                dve.tensor_tensor(stat[:, 36:38], col(56), col(54), ALU.subtract).then_inc(rexp_in, 1)
                dve.wait_ge(rexp_out, 2 * l + 1)
                link(dve.tensor_reduce(col(58), rt[:, 8, :, 0:NG], AX.X, ALU.add))
                dve.wait_ge(rexp_out, 2 * l + 2)
                link(dve.tensor_scalar(col(60), stat[:, 36:38], 1.0, None, ALU.add))
                link(dve.tensor_tensor(col(60), col(60), col(58), ALU.mult))
                link(dve.reciprocal(col(60), col(60)))
                link(dve.tensor_tensor(stat[:, 38:40], stat[:, 36:38], col(60), ALU.mult))
                link(dve.tensor_tensor(oh1, oh1, wide(col(60), NE), ALU.mult))
                link(dve.tensor_tensor(oh2, oh2, wide(stat[:, 38:40], NE), ALU.mult))
                link(dve.tensor_tensor(combine[:, :, :], oh1, oh2, ALU.add))
                for e in range(NE):
                    E = l * NE + e
                    for t in range(T):
                        dve.wait_ge(sil_done, T * E + t + 1)
                        if E > 0:
                            dve.wait_ge(hidT_done, E)
                        dve.scalar_tensor_tensor(out=hid[:, t, :], in0=ps[:, 4 + t, F:2 * F],
                                                 scalar=combine[:, t, e:e + 1], in1=sil[:, t, :],
                                                 op0=ALU.mult, op1=ALU.mult).then_inc(hid_ready, 1)
                    ahead(n0 + 16 + 3 * e + 4)
                    ahead(n0 + 16 + 3 * e + 5)
                    dve.wait_ge(hidT_hi_done, E + 1)
                    dve.tensor_tensor(hidT_lo[:, :, :], ps[:, 6, :].rearrange("p (k s) -> p k s", k=2),
                                      hidT_hi[:, :, :].bitcast(F32), ALU.subtract).then_inc(hidT_ready, 1)
                    ahead(n0 + 16 + 3 * e + 6)
                dve.wait_ge(unit_used, n0 + UL)
                residual(l, 1, 0)

        @block.tensor
        def _(pe):
            def wait_unit(n):
                pe.wait_ge(lo_done, n + 1)
                r = n % RING
                return whi[:, r, :], wlo[:, r, :]

            def ada_half(a):
                for b in range(6):
                    B = 6 * a + b
                    bank = 4 + b % 2
                    if b >= 2:
                        pe.wait_ge(mod_evac, B - 1)
                    for k in range(KD):
                        if k % 4 == 0:
                            pe.wait_ge(ada_full[k // 4], 16 * (B + 1))
                        q = k % 4
                        ins = pe.matmul(ps[32 * q:32 * q + 32, bank, :], c_rep[:, k, :],
                                        ada_raw[:, k // 4, k % 4, :], start=(k < 4), stop=(k >= 4 and q > 0),
                                        skip_group_check=True)
                        if k % 4 == 3:
                            ins.then_inc(ada_used, 1)
                    pe.wait_ge(bias_full, 16 * (B + 1))
                    pe.matmul(ps[0:32, bank, :], ones[:, 0:32], ada_bias[:, :], start=False, stop=True,
                              skip_group_check=True).then_inc(acc_done, 1)
                    if b % 2 == 0:
                        continue
                    v = b // 2
                    pe.wait_ge(mod_evac, B + 1)
                    if v < 2:
                        for j in range(KD):
                            ins = pe.matmul(ps[:, 6, v * KD + j:v * KD + j + 1], mod_rows[:, j::KD],
                                            rowsel[:, 0:1], start=True, stop=True)
                            if j == KD - 1:
                                ins.then_inc(mod_used, 1)
                    else:
                        for n in range(2):
                            if n == 1:
                                pe.wait_ge(gate_evac, 2 * a + 1)
                            pe.matmul(ps[:, 7, :], rowsel[:, :], mod_rows[:, n * 512:(n + 1) * 512],
                                      start=True, stop=True).then_inc(gate_done, 1)

            def transposes(m):
                pe.wait_ge(xn_ready, T * (m + 1))
                for bank in range(4):
                    for j in (2 * bank, 2 * bank + 1):
                        for t in range(T):
                            ins = pe.transpose(ps[:, bank, (j % 2) * S + t * P:(j % 2) * S + (t + 1) * P],
                                               tokmaj[:, t, j::KD], ident[:, :])
                    ins.then_inc(xT_done, 1)

            acts = (act_hi, act_lo)

            pe.wait_ge(const_ready, 3)
            pe.wait_ge(rowsel_ready, 1)
            pe.wait_ge(crep_ready, 2)
            ada_half(0)
            for l in range(L):
                n0 = l * UL
                transposes(2 * l)
                for i in range(3):
                    bank = (4, 6, 0)[i]
                    for half in range(2):
                        w = wait_unit(n0 + 2 * i + half)
                        pe.wait_ge(act_ready, 4 * 2 * l + (4 if i else 2 * half + 2))
                        for kk in range(4):
                            k = 4 * half + kk
                            for t in range(T):
                                for p, (pa, pw) in enumerate(PASSES):
                                    ins = pe.matmul(ps[:, bank + t, :], acts[pa][:, k, t * P:(t + 1) * P],
                                                    w[pw][:, kk * 512:(kk + 1) * 512],
                                                    start=(k == 0 and p == 0), stop=(k == KD - 1 and p == 2))
                        ins.then_inc(unit_used, 1)

                def conv_block(i, bank):
                    for half in range(2):
                        w = wait_unit(n0 + 6 + 2 * i + half)
                        for kk in range(4):
                            k = 4 * half + kk
                            for j in range(KC):
                                for p, (pa, pw) in enumerate(PASSES):
                                    ins = pe.matmul(ps[:, bank + j // 2, (j % 2) * S:(j % 2 + 1) * S],
                                                    w[pw][:, kk * 512 + j:(kk + 1) * 512:KC],
                                                    acts[pa][:, k, :], start=(k == 0 and p == 0 and j % 2 == 0),
                                                    stop=(k == KD - 1 and p == 2), skip_group_check=True)
                        ins.then_inc(unit_used, 1)

                conv_block(0, 2)
                pe.wait_ge(proj_evac, 5 * l + 1)
                conv_block(1, 4)
                pe.wait_ge(rope_done, T * (l + 1))
                for w in range(2):
                    pe.wait_ge(proj_evac, 5 * l + 3 + w)
                    for cpair in range(H // 2):
                        for t in range(T):
                            a0 = (cpair % 2) * S + t * P
                            ins = pe.transpose(ps[:, 2 * w + cpair // 2, a0:a0 + P],
                                               tokmaj[:, t, w * AW + cpair * P:w * AW + (cpair + 1) * P],
                                               ident[:, :])
                    ins.then_inc(qkT_done, 1)
                pe.wait_ge(proj_evac, 5 * l + 2)
                conv_block(2, 6)

                def scores(g):
                    for hh in range(4):
                        h = 4 * g + hh
                        rows = slice((h % 2) * HD, (h % 2) * HD + HD)
                        for t in range(T):
                            cols = slice(0, P) if t == 0 else slice(P, 384)
                            ins = pe.matmul(ps[:, 4 * g + hh, cols], qkT[rows, 0, h // 2, t * P:(t + 1) * P],
                                            qkT[rows, 1, h // 2, 0:(t + 1) * P], start=True, stop=True)
                    ins.then_inc(scores_done, 1)

                pe.wait_ge(qkT_ready, 2 * l + 2)
                scores(0)
                pe.wait_ge(proj_evac, 5 * l + 5)
                pe.wait_ge(gated_done, l + 1)
                ada_half(2 * l + 1)
                pe.wait_ge(gate_evac, 2 * (2 * l + 1) + 2)
                pe.wait_ge(mod_ready, 2 * l + 2)
                scores(1)
                for g in range(2):
                    pe.wait_ge(exp_done, 2 * l + g + 1)
                    for hh in range(4):
                        for q in range(3):
                            ins = pe.transpose(ps[:, 4 * g + hh, q * P:(q + 1) * P],
                                               work[:, g, hh, q * P:(q + 1) * P], ident[:, :])
                    ins.then_inc(pT_done, 1)
                for g in range(2):
                    if g == 0:
                        pe.wait_ge(pT_ready, 2 * l + 1)
                    else:
                        pe.wait_ge(pT_ready, 2 * l + 2)
                    for hh in range(4):
                        h = 4 * g + hh
                        vs = slice(h * HD, (h + 1) * HD)
                        pe.matmul(ps[:, 0, vs], work[:, g, hh, 0:P], v_sb[:, 0, vs], start=True, stop=True)
                        pe.matmul(ps[:, 1, vs], work[:, g, hh, P:2 * P], v_sb[:, 0, vs], start=True, stop=False)
                        ins = pe.matmul(ps[:, 1, vs], work[:, g, hh, 2 * P:3 * P], v_sb[:, 1, vs],
                                        start=False, stop=True)
                ins.then_inc(pv_done, 1)
                pe.wait_ge(csq_ready, l + 1)
                for j in range(KC):
                    ins = pe.matmul(ps[:, 2, 0:S], ones[:, :], cb[:, j, :], start=(j == 0), stop=(j == KC - 1))
                ins.then_inc(csum_done, 1)

                def out_proj(s):
                    for half in range(2):
                        w = wait_unit(n0 + 12 + 2 * s + half)
                        for kk in range(2):
                            k = 4 * s + 2 * half + kk
                            for t in range(T):
                                for p, (pa, pw) in enumerate(PASSES):
                                    for n in range(2):
                                        c0 = kk * D + n * 512
                                        ins = pe.matmul(ps[:, 4 + 2 * t + n, :],
                                                        acts[pa][:, k, t * P:(t + 1) * P],
                                                        w[pw][:, c0:c0 + 512], start=(k == 0 and p == 0),
                                                        stop=(k == KD - 1 and p == 2))
                        ins.then_inc(unit_used, 1)

                pe.wait_ge(ymc_ready, l + 1)
                out_proj(0)
                pe.wait_ge(yatt_ready, l + 1)
                for j in range(KC):
                    for t in range(T):
                        a0 = (j % 2) * S + t * P
                        ins = pe.transpose(ps[:, j // 2, a0:a0 + P], tokmaj[:, t, j:AW:KC], ident[:, :])
                ins.then_inc(yT_done, 1)
                pe.wait_ge(yma_ready, l + 1)
                out_proj(1)
                transposes(2 * l + 1)
                pe.wait_ge(act_ready, 4 * (2 * l + 2))
                rw = (r_hi, r_lo)
                for t in range(T):
                    for k in range(KD):
                        for p, (pa, pw) in enumerate(PASSES):
                            ins = pe.matmul(ps[:, 0, t * NR:(t + 1) * NR], acts[pa][:, k, t * P:(t + 1) * P],
                                            rw[pw][:, l, k, :], start=(k == 0 and p == 0),
                                            stop=(k == KD - 1 and p == 2))
                ins.then_inc(logit_done, 1)
                if l + 1 < L:
                    ada_half(2 * l + 2)
                    pe.wait_ge(gate_evac, 2 * (2 * l + 2) + 2)
                    pe.wait_ge(mod_ready, 2 * l + 3)

                def gate_up(e, t):
                    E = l * NE + e
                    n = n0 + 16 + 3 * e
                    if e > 0:
                        pe.wait_ge(hid_ready, T * (E - 1) + t + 1)
                    for half in range(2):
                        w = wait_unit(n + half)
                        for kk in range(4):
                            k = 4 * half + kk
                            for p, (pa, pw) in enumerate(PASSES):
                                ins = pe.matmul(
                                    ps[:, 4 + t, :], acts[pa][:, k, t * P:(t + 1) * P],
                                    w[pw].rearrange("p (g k f) -> p g k f", g=2, k=4)[:, :, kk, :],
                                    start=(k == 0 and p == 0), stop=(k == KD - 1 and p == 2))
                        if t == T - 1:
                            ins.then_inc(unit_used, 1)
                    if t == 0:
                        ins.then_inc(gu_done, 1)

                def hid_transpose(e):
                    E = l * NE + e
                    pe.wait_ge(hid_ready, T * (E + 1))
                    if E > 0:
                        pe.wait_ge(hidT_ready, E)
                    for kk in range(2):
                        for t in range(T):
                            ins = pe.transpose(ps[:, 6, kk * S + t * P:kk * S + (t + 1) * P],
                                               hid[:, t, kk::2], ident[:, :])
                    ins.then_inc(hidT_done, 1)

                def down(e):
                    E = l * NE + e
                    w = wait_unit(n0 + 16 + 3 * e + 2)
                    pe.wait_ge(hidT_ready, E + 1)
                    hT = (hidT_hi, hidT_lo)
                    for kk in range(2):
                        for t in range(T):
                            for p, (pa, pw) in enumerate(PASSES):
                                for n in range(2):
                                    c0 = kk * D + n * 512
                                    ins = pe.matmul(ps[:, 2 * t + n, :], hT[pa][:, kk, t * P:(t + 1) * P],
                                                    w[pw][:, c0:c0 + 512],
                                                    start=(e == 0 and kk == 0 and p == 0),
                                                    stop=(e == NE - 1 and kk == 1 and p == 2))
                    return ins

                for e in range(NE):
                    gate_up(e, 0)
                    gate_up(e, 1)
                    hid_transpose(e)
                    down(e).then_inc(unit_used, 1)


_INS = ["x", "c", "positions", "norm1_g", "norm2_g", "w_ada", "b_ada", "w_in", "conv_w", "q_norm_g",
        "k_norm_g", "conv_out_g", "attn_out_g", "w_out", "w_router_group", "b_router_group",
        "w_router_expert", "b_router_expert", "w_gate", "w_up", "w_down"]


def kernel(**inputs):
    import concourse.bacc as _bacc
    from concourse.bass_utils import run_bass_kernel_spmd as _run

    nc = _bacc.Bacc("TRN2", target_bir_lowering=False, num_devices=1, dynamic_dma_scratch_size=4096)
    arrays, args = {}, []
    for name in _INS:
        a = np.ascontiguousarray(inputs[name])
        arrays[f"in_{name}_dram"] = a
        args.append(nc.dram_tensor(f"in_{name}_dram", a.shape, mybir.dt.from_np(a.dtype),
                                   kind="ExternalInput").ap())
    shape = tuple(inputs["x"].shape)
    args.append(nc.dram_tensor("out_0_dram", shape, F32, kind="ExternalOutput").ap())
    trunk(nc, *args)
    r = _run(nc, [arrays], core_ids=[0])
    return r.results[0]["out_0_dram"]
```

```python
from contextlib import ExitStack

import concourse.bass as bass
import numpy as np
from concourse import mybir

ALU = mybir.AluOpType
ACT = mybir.ActivationFunctionType
AX = mybir.AxisListType
F32 = mybir.dt.float32
F32R = mybir.dt.float32r
I32 = mybir.dt.int32

P = 128
EPS = 1e-6
NEG = -1e30
ROPE_THETA = 10000.0
TOP_MAGIC = 12582912.0
TWO_PI_A = 6.28125
TWO_PI_B = 0.00193500518798828125
TWO_PI_C = 2 * np.pi - TWO_PI_A - TWO_PI_B
PI_IN = 3.1415925
BIG = 4096.0
RING = 4
PASSES = ((0, 0), (0, 1), (1, 0))


def trunk(nc, x, c, positions, norm1_g, norm2_g, w_ada, b_ada, w_in, conv_w, q_norm_g, k_norm_g,
          conv_out_g, attn_out_g, w_out, w_rg, b_rg, w_re, b_re, w_gate, w_up, w_down, out):
    _, S, D = x.shape
    L = norm1_g.shape[0]
    CW = conv_out_g.shape[1]
    AW = attn_out_g.shape[1]
    HD = q_norm_g.shape[1]
    H = AW // HD
    NE, _, F = w_gate.shape[1:]
    NG = w_rg.shape[2]
    EG = NE // NG
    NR = NG + NE
    T = S // P
    KD = D // P
    KC = CW // P
    HH = HD // 2
    SCALE = float(HD) ** -0.5
    assert (S, D, CW, AW, HD, F) == (256, 1024, 512, 512, 64, 256)
    UL = 16 + 3 * NE
    NU = L * UL

    x_v = x.rearrange("a (t p) d -> (a p) t d", p=P)
    out_v = out.rearrange("a (t p) d -> (a p) t d", p=P)
    win_v = w_in.rearrange("l (p k) n -> l p k n", k=KD)
    wout_v = w_out.rearrange("l (s p k) n -> l s p k n", s=2, k=KC)
    ada_v = w_ada.rearrange("l (p k) n -> l p k n", k=KD)
    gate_v = w_gate.rearrange("l e (p k) f -> l e p k f", k=KD)
    up_v = w_up.rearrange("l e (p k) f -> l e p k f", k=KD)
    down_v = w_down.rearrange("l e (p k) d -> l e p k d", k=2)
    IN_ORDER = (3, 4, 5, 0, 1, 2)

    with ExitStack() as ctx:
        def sb(name, shape, dt=F32):
            return ctx.enter_context(nc.sbuf_tensor(name, shape, dt))

        def sem(name):
            return ctx.enter_context(nc.semaphore(name))

        ps = ctx.enter_context(nc.psum_tensor("ps", [P, 8, 512], F32))

        raw = sb("raw", [P, RING, 2048])
        whi = sb("whi", [P, RING, 2048], F32R)
        wlo = sb("wlo", [P, RING, 2048], F32R)
        ada_raw = sb("ada_raw", [P, 2, 4, 512])
        ada_bias = sb("ada_bias", [P, 512])
        mod_rows = sb("mod_rows", [P, D])
        gates = sb("gates", [P, 2, D])
        res = sb("res", [P, T, D])
        act_hi = sb("act_hi", [P, KD, S], F32R)
        act_lo = sb("act_lo", [P, KD, S], F32R)
        tokmaj = sb("tokmaj", [P, T, D])
        qkT = sb("qkT", [P, 2, H // 2, S])
        v_sb = sb("v_sb", [P, T, AW])
        cb = sb("cb", [P, KC, S])
        cc = sb("cc", [P, KC, S])
        cg = sb("cg", [P, KC, S + 2])
        work = sb("work", [P, 2, 4, 384])
        wflat = work[:, :, :, :].rearrange("p a b c -> p (a b c)")
        hf = wflat[:, 0:KD * S].rearrange("p (k s) -> p k s", k=KD)
        slots_i = wflat[:, 1024:1024 + P].bitcast(I32)
        ident = sb("ident", [P, P])
        ones = sb("ones", [P, P])
        rowsel = sb("rowsel", [P, P])
        mask = sb("mask", [P, 384])
        c_col = sb("c_col", [P, KD])
        c_rep = sb("c_rep", [P, KD, 32])
        g_norm = sb("g_norm", [P, 2, L, KD])
        g_qk = sb("g_qk", [P, L, 2, HD])
        g_conv = sb("g_conv", [P, L, KC])
        g_attn = sb("g_attn", [P, L, KC])
        w_conv = sb("w_conv", [P, L, 3, KC])
        r_w = wflat[:, 0:L * KD * NR].rearrange("p (l k n) -> p l k n", l=L, k=KD)
        r_hi = sb("r_hi", [P, L, KD, NR], F32R)
        r_lo = sb("r_lo", [P, L, KD, NR], F32R)
        r_b = sb("r_b", [P, L, NR])
        pos_i = sb("pos_i", [P, T], I32)
        pos_f = sb("pos_f", [P, T])
        invf = sb("invf", [P, HH])
        ang = wflat[:, 512:512 + 3 * T * HH].rearrange("p (a t d) -> p a t d", a=3, t=T)
        sincos = sb("sincos", [P, 2, T, HH])
        trig = sb("trig", [P, 2, T, 2, HD])
        mod_t = sb("mod_t", [P, 2, 2, KD])
        stat = sb("stat", [P, 64])
        rt = sb("rt", [P, 10, T, NR])
        rank = sb("rank", [P, NE])
        combine = sb("combine", [P, T, NE])
        sil = wflat[:, 0:2 * F].rearrange("p (b f) -> p b f", b=2)
        hid = wflat[:, 2 * F:4 * F].rearrange("p (b f) -> p b f", b=2)
        sel = wflat[:, 1024:1024 + NG * T * P].rearrange("p (g t s) -> p g t s", g=NG, t=T)
        selT = cb[:, :, :].rearrange("p k s -> p (k s)").rearrange("p (g t s) -> p g t s", g=NG, t=T)
        hg = cc[:, :, :].rearrange("p k s -> p (k s)").rearrange("p (k s) -> p k s", k=KD)
        y_sb = v_sb[:, :, :].rearrange("p t d -> p (t d)")
        hidT_hi = sb("hidT_hi", [P, 2, 2, P], F32R)
        hidT_lo = sb("hidT_lo", [P, 2, 2, P], F32R)
        before = sb("before", [P, P])
        slots = sb("slots", [P, P])
        slot_of = sb("slot_of", [P, T, NG])
        cw = sb("cw", [P, NE])
        over = sb("over", [P, NG])
        over_any = sb("over_any", [P, 2])
        over_i = sb("over_i", [P, L, 2], I32)
        stage = qkT[:, :, :, :].rearrange("p w c s -> p (w c s)")
        hidT_x = wflat[:, 2048:2048 + 2 * P].rearrange("p (k s) -> p k s", k=2)

        par_in = sem("par_in")
        raw_full = [sem(f"raw_full{r}") for r in range(RING)]
        ada_full = [sem(f"ada_full{r}") for r in range(2)]
        bias_full = sem("bias_full")
        out_done = sem("out_done")
        hi_done = sem("hi_done")
        lo_done = sem("lo_done")
        unit_used = sem("unit_used")
        const_ready = sem("const_ready")
        rowsel_ready = sem("rowsel_ready")
        crep_ready = sem("crep_ready")
        ada_used = sem("ada_used")
        acc_done = sem("acc_done")
        mod_evac = sem("mod_evac")
        mod_used = sem("mod_used")
        mod_ready = sem("mod_ready")
        gate_done = sem("gate_done")
        gate_evac = sem("gate_evac")
        rstd_sum = sem("rstd_sum")
        rstd_root = sem("rstd_root")
        xn_ready = sem("xn_ready")
        xT_done = sem("xT_done")
        hf_ready = sem("hf_ready")
        act_ready = sem("act_ready")
        proj_evac = sem("proj_evac")
        qk_sum = sem("qk_sum")
        qk_root = sem("qk_root")
        rope_done = sem("rope_done")
        qkT_done = sem("qkT_done")
        qkT_ready = sem("qkT_ready")
        gated_done = sem("gated_done")
        scores_done = sem("scores_done")
        max_ready = sem("max_ready")
        exp_done = sem("exp_done")
        pT_done = sem("pT_done")
        pT_ready = sem("pT_ready")
        pv_done = sem("pv_done")
        yconv_ready = sem("yconv_ready")
        csq_ready = sem("csq_ready")
        csum_done = sem("csum_done")
        croot = sem("croot")
        ymc_ready = sem("ymc_ready")
        yatt_raw = sem("yatt_raw")
        yatt_sum = sem("yatt_sum")
        yatt_root = sem("yatt_root")
        yatt_ready = sem("yatt_ready")
        yT_done = sem("yT_done")
        yf_ready = sem("yf_ready")
        yma_ready = sem("yma_ready")
        logit_done = sem("logit_done")
        rexp_in = sem("rexp_in")
        rexp_out = sem("rexp_out")
        rw_ready = sem("rw_ready")
        oh_ready = sem("oh_ready")
        place_done = sem("place_done")
        sel_ready = sem("sel_ready")
        selT_done = sem("selT_done")
        selT_ready = sem("selT_ready")
        comb_ready = sem("comb_ready")
        cw_done = sem("cw_done")
        gather_done = sem("gather_done")
        hg_ready = sem("hg_ready")
        group_ready = sem("group_ready")
        y_ready = sem("y_ready")
        scatter_done = sem("scatter_done")
        scatter_used = sem("scatter_used")
        over_known = sem("over_known")
        x_step = sem("x_step")
        x_sel = sem("x_sel")
        x_in = sem("x_in")
        x_hg = sem("x_hg")
        x_cw = sem("x_cw")
        x_full = sem("x_full")
        x_used = sem("x_used")
        x_sil = sem("x_sil")
        x_hid = sem("x_hid")
        x_hidT = sem("x_hidT")
        x_hidT_out = sem("x_hidT_out")
        x_y = sem("x_y")
        x_back = sem("x_back")
        x_added = sem("x_added")
        sil_done = sem("sil_done")
        hid_ready = sem("hid_ready")
        hidT_done = sem("hidT_done")
        hidT_hi_done = sem("hidT_hi_done")
        hidT_ready = sem("hidT_ready")
        res_ready = sem("res_ready")
        act_step = sem("act_step")
        dve_step = sem("dve_step")
        pool_step = sem("pool_step")

        def gu_unit(e, half):
            return half if e == 0 else 3 * e - 1 + half

        def down_unit(e):
            return 3 * e + 4 if e < NE - 1 else 3 * NE - 1

        X_LOADS = 16 * 5 * EG

        two_dma = {gu_unit(e, half) for e in range(NE) for half in range(2)}

        block = ctx.enter_context(nc.Block())
        NPAR = 11 + 3 * L

        @block.sync
        def _(sp):
            def raw_slot(n):
                if n >= RING:
                    sp.wait_ge(lo_done, n - RING + 1)
                return raw[:, n % RING, :]

            def ada_half(a):
                l, h = a // 2, a % 2
                for b in range(6):
                    B = 6 * a + b
                    cols = slice((h * 6 + b) * 512, (h * 6 + b + 1) * 512)
                    for u in range(2):
                        if B >= 1:
                            sp.wait_ge(ada_used, 2 * (B - 1) + u + 1)
                        sp.dma_start(ada_raw[:, u, :, :], ada_v[l, :, 4 * u:4 * u + 4, cols]
                                     ).then_inc(ada_full[u], 16)
                    if B >= 1:
                        sp.wait_ge(acc_done, B)
                    else:
                        sp.wait_ge(const_ready, 1)
                    sp.dma_start(ada_bias[0:1, :], b_ada[l:l + 1, cols]
                                 ).then_inc(bias_full, 16)

            def in_units(l, i0, i1):
                for i in range(i0, i1):
                    n, blk, half = l * UL + i, IN_ORDER[i // 2], i % 2
                    sp.dma_start(raw_slot(n).rearrange("p (k n) -> p k n", k=4),
                                 win_v[l, :, 4 * half:4 * half + 4, blk * 512:(blk + 1) * 512]
                                 ).then_inc(raw_full[n % RING], 16)

            ada_half(0)
            in_units(0, 0, RING)
            for l in range(L):
                n0 = l * UL
                in_units(l, RING, 12)
                for i in range(4):
                    sp.dma_start(raw_slot(n0 + 12 + i).rearrange("p (k n) -> p k n", k=2),
                                 wout_v[l, i // 2, :, 2 * (i % 2):2 * (i % 2) + 2, :]
                                 ).then_inc(raw_full[(n0 + 12 + i) % RING], 16)
                ada_half(2 * l + 1)
                if l + 1 < L:
                    ada_half(2 * l + 2)
                for e in range(NE + 1):
                    if e < NE:
                        for half in range(2):
                            n = n0 + 16 + gu_unit(e, half)
                            slot = raw_slot(n).rearrange("p (g k f) -> p g k f", g=2, k=4)
                            for g, w in enumerate((gate_v, up_v)):
                                sp.dma_start(slot[:, g, :, :], w[l, e, :, 4 * half:4 * half + 4, :]
                                             ).then_inc(raw_full[n % RING], 16)
                    if e > 0:
                        n = n0 + 16 + down_unit(e - 1)
                        sp.dma_start(raw_slot(n).rearrange("p (k n) -> p k n", k=2), down_v[l, e - 1]
                                     ).then_inc(raw_full[n % RING], 16)
                if l + 1 < L:
                    in_units(l + 1, 0, RING)
                sp.wait_ge(over_known, l + 1)
                with sp.If(sp.value_load(over_i[0:1, l, 0:1], min_val=0, max_val=1) > 0):
                    first = sp.value_load(over_i[0:1, l, 1:2], min_val=0, max_val=NG - 1) * EG
                    sp.wait_ge(unit_used, n0 + 16)
                    for i in range(EG):
                        one = bass.ds(first + i, 1)
                        for part in range(3):
                            sp.wait_ge(x_used, 3 * EG * l + 3 * i + part)
                            if part < 2:
                                dst = stage.rearrange("p (g k f) -> p g k f", g=2, k=4)
                                for g, w in enumerate((gate_v, up_v)):
                                    sp.dma_start(dst[:, g, :, :], w[l, one, :, 4 * part:4 * part + 4, :]
                                                 .rearrange("a p k f -> (a p) k f")).then_inc(x_full, 16)
                            else:
                                sp.dma_start(stage.rearrange("p (k n) -> p k n", k=2), down_v[l, one]
                                             .rearrange("a p k n -> (a p) k n")).then_inc(x_full, 16)
                with sp.Else():
                    sp.sem_inc(x_full, X_LOADS)
            sp.wait_ge(res_ready, 2 * L)
            sp.dma_start(out_v, res[:, :, :]).then_inc(out_done, 16)
            sp.wait_ge(out_done, 16)

        def raw_landed(n):
            total = 0
            for m in range(n % RING, n + 1, RING):
                i = m % UL - 16
                total += 32 if i in two_dma else 16
            return total

        @block.gpsimd
        def _(pool):
            pool.memset(ident[:, :], 0.0).then_inc(pool_step, 1)
            pool.memset(mask[:, :], 0.0).then_inc(pool_step, 1)
            pool.memset(before[:, :], 0.0).then_inc(pool_step, 1)
            pool.memset(ones[:, :], 1.0)
            for i in range(HH):
                pool.memset(invf[:, i:i + 1],
                            float(np.float32(ROPE_THETA) ** (-np.float32(2 * i) / np.float32(HD))))
            for i in range(NE):
                pool.memset(rank[:, i:i + 1], float(NE - i))
            pool.memset(cg[:, :, 0:2], 0.0)
            pool.memset(ada_bias[:, :], 0.0).then_inc(const_ready, 1)
            pool.wait_ge(pool_step, 1)
            pool.affine_select(out=ident[:, :], in_=ident[:, :], compare_op=ALU.not_equal, fill=1.0,
                               base=0, pattern=[[-1, P]], channel_multiplier=1).then_inc(const_ready, 1)
            pool.wait_ge(pool_step, 3)
            pool.affine_select(out=before[:, :], in_=before[:, :], compare_op=ALU.is_ge, fill=1.0,
                               base=0, pattern=[[-1, P]], channel_multiplier=1).then_inc(const_ready, 1)
            pool.iota(slots_i[:, :], pattern=[[1, P]], base=0, channel_multiplier=0).then_inc(const_ready, 1)
            for a in (0, 256):
                last = pool.affine_select(out=mask[:, a:a + P], in_=mask[:, a:a + P], compare_op=ALU.is_ge,
                                          fill=NEG, base=0, pattern=[[-1, P]], channel_multiplier=1)
            last.then_inc(const_ready, 1)

        @block.scalar
        def _(act):
            steps = [0]

            def link(ins):
                steps[0] += 1
                ins.then_inc(act_step, 1)
                act.wait_ge(act_step, steps[0])

            def load(dst, src):
                act.dma_start(dst, src).then_inc(par_in, 16)

            load(c_col[:, :], c.rearrange("a (p k) -> (a p) k", k=KD))
            load(res[:, :, :], x_v)
            with nc.allow_non_contiguous_dma(reason="256 positions, one to a partition"):
                load(pos_i[:, :], positions.rearrange("a (t p) -> (a p) t", p=P))
            load(g_norm[:, 0, :, :], norm1_g.rearrange("l (p k) -> p l k", k=KD))
            load(g_norm[:, 1, :, :], norm2_g.rearrange("l (p k) -> p l k", k=KD))
            load(g_qk[:, :, 0, :], q_norm_g.partition_broadcast(P))
            load(g_qk[:, :, 1, :], k_norm_g.partition_broadcast(P))
            load(g_conv[:, :, :], conv_out_g.rearrange("l (p k) -> p l k", k=KC))
            load(g_attn[:, :, :], attn_out_g.rearrange("l (p k) -> p l k", k=KC))
            for l in range(L):
                load(w_conv[:, l, :, :], conv_w[l].rearrange("r (p k) -> p r k", k=KC))
            load(r_b[:, :, 0:NG], b_rg.partition_broadcast(P))
            load(r_b[:, :, NG:NR], b_re.partition_broadcast(P))
            for l in range(L):
                load(r_w[:, l, :, 0:NG], w_rg[l].rearrange("(p k) n -> p k n", k=KD))
            for l in range(L):
                load(r_w[:, l, :, NG:NR], w_re[l].rearrange("(p k) n -> p k n", k=KD))

            def split(n):
                act.wait_ge(raw_full[n % RING], raw_landed(n))
                if n >= RING:
                    act.wait_ge(unit_used, n - RING + 1)
                act.activation(whi[:, n % RING, :], raw[:, n % RING, :], ACT.Copy).then_inc(hi_done, 1)

            def ahead(n):
                if n < NU:
                    split(n)

            def ada_block(a, b):
                B = 6 * a + b
                act.wait_ge(acc_done, B + 1)
                if b in (2, 4):
                    act.wait_ge(mod_used, 2 * a + b // 2)
                act.activation(mod_rows[:, (b % 2) * 512:(b % 2 + 1) * 512], ps[:, 4 + b % 2, :],
                               ACT.Copy).then_inc(mod_evac, 1)
                if b == 5:
                    if a >= 2:
                        act.wait_ge(res_ready, a - 1)
                    for n in range(2):
                        act.wait_ge(gate_done, 2 * a + n + 1)
                        act.activation(gates[:, a % 2, n * 512:(n + 1) * 512], ps[:, 7, :],
                                       ACT.Copy).then_inc(gate_evac, 1)

            def norm_root(m):
                act.wait_ge(rstd_sum, m + 1)
                act.activation(stat[:, 2:4], stat[:, 0:2], ACT.Sqrt, scale=1.0 / D,
                               bias=eps_col).then_inc(rstd_root, 1)

            def norm_evac(m):
                act.wait_ge(mod_ready, m + 1)
                for bank in range(4):
                    act.wait_ge(xT_done, 4 * m + bank + 1)
                    for j in (2 * bank, 2 * bank + 1):
                        ins = act.activation(hf[:, j, :], ps[:, bank, (j % 2) * S:(j % 2 + 1) * S],
                                             ACT.Identity, scale=mod_t[:, m % 2, 1, j:j + 1],
                                             bias=mod_t[:, m % 2, 0, j:j + 1])
                    ins.then_inc(hf_ready, 1)

            act.wait_ge(par_in, 16)
            act.wait_ge(par_in, 16 * NPAR)
            eps_col = stat[:, 63:64]
            act.wait_ge(crep_ready, 1)
            link(act.activation(stat[:, 40:40 + KD], c_col[:, :], ACT.Silu))
            act.activation(c_rep[:, :, :], stat[:, 40:40 + KD].unsqueeze(2).to_broadcast([P, KD, 32]),
                           ACT.Copy).then_inc(crep_ready, 1)
            act.wait_ge(crep_ready, 3)
            act.activation(sincos[:, :, :, :], ang[:, 0:2, :, :], ACT.Sin).then_inc(crep_ready, 1)
            for b in range(6):
                ada_block(0, b)
            for n in range(RING):
                split(n)
            for l in range(L):
                n0 = l * UL
                m = 2 * l
                norm_root(m)
                norm_evac(m)
                split(n0 + 4)
                split(n0 + 5)
                for w in range(2):
                    act.wait_ge(unit_used, n0 + 2 * w + 2)
                    for t in range(T):
                        ins = act.activation(tokmaj[:, t, w * AW:(w + 1) * AW], ps[:, 4 + 2 * w + t, :],
                                             ACT.Copy)
                    ins.then_inc(proj_evac, 1)
                    if w == 0:
                        split(n0 + 6)
                        split(n0 + 7)
                act.wait_ge(unit_used, n0 + 6)
                act.activation(v_sb[:, :, :], ps[:, 0:2, :], ACT.Copy).then_inc(proj_evac, 1)
                split(n0 + 8)
                split(n0 + 9)
                act.wait_ge(qk_sum, l + 1)
                act.activation(stat[:, 4:36], stat[:, 4:36], ACT.Sqrt, scale=1.0 / HD,
                               bias=eps_col).then_inc(qk_root, 1)
                act.wait_ge(unit_used, n0 + 8)
                act.activation(cb[:, :, :], ps[:, 2:4, :].rearrange("p a (b s) -> p (a b) s", s=S),
                               ACT.Copy).then_inc(proj_evac, 1)
                split(n0 + 10)
                split(n0 + 11)
                act.wait_ge(unit_used, n0 + 10)
                act.activation(cc[:, :, :], ps[:, 4:6, :].rearrange("p a (b s) -> p (a b) s", s=S),
                               ACT.Copy).then_inc(proj_evac, 1)
                for w in range(2):
                    act.wait_ge(qkT_done, 2 * l + w + 1)
                    act.activation(qkT[:, w, :, :],
                                   ps[:, 2 * w:2 * w + 2, :].rearrange("p a (b s) -> p (a b) s", s=S),
                                   ACT.Copy).then_inc(qkT_ready, 1)
                split(n0 + 12)
                split(n0 + 13)

                def exps(g):
                    act.wait_ge(max_ready, 2 * l + g + 1)
                    for h in range(4):
                        for t in range(T):
                            cols = slice(0, P) if t == 0 else slice(P, 384)
                            col = 16 * g + 4 * t + h
                            ins = act.activation(work[:, g, h, cols], work[:, g, h, cols], ACT.Exp,
                                                 bias=stat[:, 4 + col:5 + col],
                                                 accum_out=stat[:, 12 + col:13 + col])
                    ins.then_inc(exp_done, 1)

                a = 2 * l + 1
                exps(0)
                split(n0 + 14)
                split(n0 + 15)
                for b in range(6):
                    ada_block(a, b)
                exps(1)
                for g in range(2):
                    act.wait_ge(pT_done, 2 * l + g + 1)
                    act.activation(work[:, g, :, :], ps[:, 4 * g:4 * g + 4, 0:384], ACT.Copy
                                   ).then_inc(pT_ready, 1)
                act.wait_ge(yconv_ready, l + 1)
                act.activation(cb[:, :, :], cc[:, :, :], ACT.Square).then_inc(csq_ready, 1)
                act.wait_ge(csum_done, l + 1)
                act.activation(cb[:, 0, :], ps[:, 2, 0:S], ACT.Sqrt, scale=1.0 / CW,
                               bias=eps_col).then_inc(croot, 1)
                act.wait_ge(yatt_sum, l + 1)
                act.activation(stat[:, 2:4], stat[:, 0:2], ACT.Sqrt, scale=1.0 / AW,
                               bias=eps_col).then_inc(yatt_root, 1)
                act.wait_ge(yT_done, l + 1)
                for j in range(KC):
                    ins = act.activation(hf[:, KC + j, :], ps[:, j // 2, (j % 2) * S:(j % 2 + 1) * S],
                                         ACT.Copy, scale=g_attn[:, l, j:j + 1])
                ins.then_inc(yf_ready, 1)
                m = 2 * l + 1
                norm_root(m)
                norm_evac(m)
                act.wait_ge(rexp_in, 2 * l + 1)
                act.activation(rt[:, 8, :, 0:NG], rt[:, 8, :, 0:NG], ACT.Exp).then_inc(rexp_out, 1)
                act.wait_ge(rexp_in, 2 * l + 2)
                act.activation(stat[:, 36:38], stat[:, 36:38], ACT.Exp).then_inc(rexp_out, 1)
                if l + 1 < L:
                    for b in range(6):
                        ada_block(2 * l + 2, b)
                for n in range(4):
                    split(n0 + 16 + n)

                def group_in(g):
                    act.wait_ge(gather_done, NG * l + g + 1)
                    if g > 0:
                        act.wait_ge(group_ready, NG * l + g)
                    for k in range(KD):
                        ins = act.activation(hg[:, k, :], ps[:, 6 + k // 4, (k % 4) * P:(k % 4 + 1) * P],
                                             ACT.Identity, scale=mod_t[:, 1, 1, k:k + 1],
                                             bias=mod_t[:, 1, 0, k:k + 1])
                    ins.then_inc(hg_ready, 1)

                group_in(0)
                act.wait_ge(selT_done, l + 1)
                act.activation(selT, ps[:, 4:6, :].rearrange("p a (b s) -> p (a b) s", s=P)
                               .rearrange("p (g t) s -> p g t s", g=NG), ACT.Copy).then_inc(selT_ready, 1)
                split(n0 + 20)
                for e in range(NE):
                    E = l * NE + e
                    act.wait_ge(unit_used, n0 + 16 + gu_unit(e, 1) + 1)
                    if e >= 2:
                        act.wait_ge(hid_ready, E - 1)
                    act.activation(sil[:, e % 2, :], ps[:, e % 2, 0:F], ACT.Silu).then_inc(sil_done, 1)
                    ahead(n0 + 16 + 3 * e + 5)
                    act.wait_ge(hidT_done, E + 1)
                    if e >= 2:
                        act.wait_ge(unit_used, n0 + 16 + down_unit(e - 2) + 1)
                    act.activation(hidT_hi[:, e % 2, :, :], ps[:, 2, 0:2 * P].rearrange("p (k s) -> p k s", k=2),
                                   ACT.Copy).then_inc(hidT_hi_done, 1)
                    if e % EG == 2 and e // EG + 1 < NG:
                        group_in(e // EG + 1)
                    ahead(n0 + 16 + 3 * e + 6)
                    if e < NE - 1:
                        ahead(n0 + 16 + 3 * e + 7)

                act.wait_ge(over_known, l + 1)
                with act.If(act.value_load(over_i[0:1, l, 0:1], min_val=0, max_val=1) > 0):
                    act.wait_ge(x_in, l + 1)
                    for k in range(KD):
                        act.activation(hg[:, k, :], ps[:, 6 + k // 4, (k % 4) * P:(k % 4 + 1) * P],
                                       ACT.Identity, scale=mod_t[:, 1, 1, k:k + 1],
                                       bias=mod_t[:, 1, 0, k:k + 1])
                    act.activation(selT[:, 0, :, :], ps[:, 1, 0:T * P].rearrange("p (t s) -> p t s", t=T),
                                   ACT.Copy).then_inc(x_hg, 1)
                    for i in range(EG):
                        act.wait_ge(x_used, 3 * EG * l + 3 * i + 2)
                        act.activation(sil[:, 0, :], ps[:, 0, 0:F], ACT.Silu).then_inc(x_sil, 1)
                        act.wait_ge(x_hidT, EG * l + i + 1)
                        act.activation(hidT_x, ps[:, 2, 0:2 * P].rearrange("p (k s) -> p k s", k=2),
                                       ACT.Copy).then_inc(x_hidT_out, 1)
                with act.Else():
                    act.sem_inc(x_hg, 1)
                    act.sem_inc(x_sil, EG)
                    act.sem_inc(x_hidT_out, EG)

        @block.vector
        def _(dve):
            steps = [0]

            def link(ins):
                steps[0] += 1
                ins.then_inc(dve_step, 1)
                dve.wait_ge(dve_step, steps[0])

            x_steps = [0]

            def x_link(ins):
                x_steps[0] += 1
                ins.then_inc(x_step, 1)
                dve.wait_ge(x_step, x_steps[0])

            def split(n):
                dve.wait_ge(hi_done, n + 1)
                dve.tensor_tensor(wlo[:, n % RING, :], raw[:, n % RING, :],
                                  whi[:, n % RING, :].bitcast(F32), ALU.subtract).then_inc(lo_done, 1)

            def ahead(n):
                if n < NU:
                    split(n)

            dve.memset(stat[:, 63:64], EPS).then_inc(crep_ready, 1)
            link(dve.memset(rowsel[:, :], 0.0))
            for q in range(4):
                last = dve.memset(rowsel[32 * q:32 * q + 1, :], 1.0)
            last.then_inc(rowsel_ready, 1)
            dve.wait_ge(par_in, 16 * NPAR)
            link(dve.tensor_copy(pos_f[:, :], pos_i[:, :]))
            dve.wait_ge(const_ready, 5)
            dve.tensor_copy(slots[:, :], slots_i)
            for t in range(T):
                last = dve.tensor_scalar(ang[:, 0, t, :], invf[:, :], pos_f[:, t:t + 1], None, ALU.mult)
            link(last)
            link(dve.tensor_scalar(ang[:, 1, :, :], ang[:, 0, :, :], 1.0 / (2 * np.pi), TOP_MAGIC,
                                   ALU.mult, ALU.add))
            link(dve.tensor_scalar(ang[:, 2, :, :], ang[:, 1, :, :], -TOP_MAGIC, None, ALU.add))
            for part in (TWO_PI_A, TWO_PI_B, TWO_PI_C):
                link(dve.scalar_tensor_tensor(out=ang[:, 0, :, :], in0=ang[:, 2, :, :], scalar=-float(part),
                                              in1=ang[:, 0, :, :], op0=ALU.mult, op1=ALU.add))
            link(dve.tensor_scalar(ang[:, 1, :, :], ang[:, 0, :, :], float(np.pi / 2), None, ALU.add))
            link(dve.tensor_scalar(ang[:, 2, :, :], ang[:, 1, :, :], float(np.pi), None, ALU.is_gt))
            link(dve.scalar_tensor_tensor(out=ang[:, 1, :, :], in0=ang[:, 2, :, :], scalar=-float(2 * np.pi),
                                          in1=ang[:, 1, :, :], op0=ALU.mult, op1=ALU.add))
            dve.wait_ge(crep_ready, 2)
            dve.tensor_scalar(ang[:, 0:2, :, :], ang[:, 0:2, :, :], PI_IN, -PI_IN, ALU.min, ALU.max
                              ).then_inc(crep_ready, 1)
            link(dve.tensor_copy(r_hi[:, :, :, :], r_w[:, :, :, :]))
            link(dve.tensor_tensor(r_lo[:, :, :, :], r_w[:, :, :, :], r_hi[:, :, :, :].bitcast(F32),
                                   ALU.subtract))
            dve.wait_ge(crep_ready, 4)

            def modulation(a):
                l, h = a // 2, a % 2
                dve.wait_ge(mod_used, 2 * a + 2)
                if a >= 2:
                    if h == 0:
                        dve.wait_ge(hf_ready, 4 * (a - 1))
                    else:
                        dve.wait_ge(hg_ready, NG * l)
                link(dve.tensor_copy(mod_t[:, h, 0, :], ps[:, 6, 0:KD]))
                dve.scalar_tensor_tensor(out=mod_t[:, h, 1, :], in0=ps[:, 6, KD:2 * KD], scalar=1.0,
                                         in1=g_norm[:, h, l, :], op0=ALU.add, op1=ALU.mult
                                         ).then_inc(mod_ready, 1)

            def token_norm(m):
                for t in range(T):
                    ins = dve.tensor_tensor_reduce(out=tokmaj[:, t, :], in0=res[:, t, :], in1=res[:, t, :],
                                                   scale=1.0, scalar=0.0, op0=ALU.mult, op1=ALU.add,
                                                   accum_out=stat[:, t:t + 1])
                ins.then_inc(rstd_sum, 1)
                dve.wait_ge(rstd_root, m + 1)
                link(dve.reciprocal(stat[:, 0:2], stat[:, 2:4]))
                for t in range(T):
                    dve.tensor_scalar(tokmaj[:, t, :], res[:, t, :], stat[:, t:t + 1], None, ALU.mult
                                      ).then_inc(xn_ready, 1)

            def activation_parts(m):
                for bank in range(4):
                    dve.wait_ge(hf_ready, 4 * m + bank + 1)
                    js = slice(2 * bank, 2 * bank + 2)
                    link(dve.tensor_copy(act_hi[:, js, :], hf[:, js, :]))
                    dve.tensor_tensor(act_lo[:, js, :], hf[:, js, :], act_hi[:, js, :].bitcast(F32),
                                      ALU.subtract).then_inc(act_ready, 1)

            def residual(l, h, banks):
                dve.wait_ge(gate_evac, 2 * (2 * l + h) + 2)
                for t in range(T):
                    link(dve.tensor_tensor(tokmaj[:, t, :].rearrange("p (a b) -> p a b", a=2),
                                           ps[:, banks + 2 * t:banks + 2 * t + 2, :],
                                           gates[:, h, :].rearrange("p (a b) -> p a b", a=2), ALU.mult))
                    ins = dve.tensor_tensor(res[:, t, :], res[:, t, :], tokmaj[:, t, :], ALU.add)
                    if t == T - 1:
                        ins.then_inc(res_ready, 1)
                        dve.wait_ge(res_ready, 2 * l + h + 1)
                    else:
                        link(ins)

            modulation(0)
            for n in range(RING):
                split(n)
            for l in range(L):
                n0 = l * UL
                token_norm(2 * l)
                activation_parts(2 * l)
                for w in range(2):
                    for s in range(2):
                        for half in range(2):
                            hs = slice(half * HH, half * HH + HH)
                            ins = dve.tensor_tensor(
                                trig[:, s, :, w, hs], sincos[:, 1 - s, :, :],
                                g_qk[:, l, w, hs].unsqueeze(1).to_broadcast([P, T, HH]), ALU.mult)
                link(ins)
                split(n0 + 4)
                split(n0 + 5)
                split(n0 + 6)
                split(n0 + 7)
                dve.wait_ge(proj_evac, 5 * l + 2)
                for t in range(T):
                    link(dve.tensor_tensor(wflat[:, t * 1024:(t + 1) * 1024], tokmaj[:, t, :],
                                           tokmaj[:, t, :], ALU.mult))
                dve.tensor_reduce(stat[:, 4:36], wflat[:, 0:2048].rearrange("p (h d) -> p h d", d=HD),
                                  AX.X, ALU.add).then_inc(qk_sum, 1)
                split(n0 + 8)
                split(n0 + 9)
                dve.wait_ge(qk_root, l + 1)
                link(dve.reciprocal(stat[:, 4:36], stat[:, 4:36]))
                for t in range(T):
                    qk = tokmaj[:, t, :].rearrange("p (h d) -> p h d", d=HD)
                    link(dve.tensor_tensor(qk, qk, stat[:, 4 + 16 * t:20 + 16 * t].unsqueeze(2)
                                           .to_broadcast([P, 2 * H, HD]), ALU.mult))
                    parts = [wflat[:, s * 1024:(s + 1) * 1024] for s in range(2)]
                    for s in range(2):
                        for w in range(2):
                            ins = dve.tensor_tensor(
                                parts[s][:, w * AW:(w + 1) * AW].rearrange("p (h d) -> p h d", d=HD),
                                tokmaj[:, t, w * AW:(w + 1) * AW].rearrange("p (h d) -> p h d", d=HD),
                                trig[:, s, t, w, :].unsqueeze(1).to_broadcast([P, H, HD]), ALU.mult)
                    link(ins)
                    xc, xs = (q.rearrange("p (h a d) -> p h a d", a=2, d=HH) for q in parts)
                    q4 = tokmaj[:, t, :].rearrange("p (h a d) -> p h a d", a=2, d=HH)
                    dve.tensor_tensor(q4[:, :, 0, :], xc[:, :, 0, :], xs[:, :, 1, :], ALU.subtract)
                    ins = dve.tensor_tensor(q4[:, :, 1, :], xc[:, :, 1, :], xs[:, :, 0, :], ALU.add)
                    ins.then_inc(rope_done, 1)
                    dve.wait_ge(rope_done, T * l + t + 1)
                split(n0 + 10)
                split(n0 + 11)
                dve.wait_ge(proj_evac, 5 * l + 5)
                dve.wait_ge(unit_used, n0 + 12)
                dve.tensor_tensor(cg[:, :, 2:S + 2], cc[:, :, :],
                                  ps[:, 6:8, :].rearrange("p a (b s) -> p (a b) s", s=S), ALU.mult
                                  ).then_inc(gated_done, 1)
                split(n0 + 12)
                split(n0 + 13)

                def softmax_max(g):
                    dve.wait_ge(scores_done, 2 * l + g + 1)
                    link(dve.scalar_tensor_tensor(out=work[:, g, :, :], in0=ps[:, 4 * g:4 * g + 4, 0:384],
                                                  scalar=SCALE,
                                                  in1=mask[:, :].unsqueeze(1).to_broadcast([P, 4, 384]),
                                                  op0=ALU.mult, op1=ALU.add))
                    for t in range(T):
                        cols = slice(0, P) if t == 0 else slice(P, 384)
                        ins = dve.tensor_reduce(stat[:, 4 + 16 * g + 4 * t:8 + 16 * g + 4 * t],
                                                work[:, g, :, cols], AX.X, ALU.max, negate=True)
                    ins.then_inc(max_ready, 1)

                softmax_max(0)
                split(n0 + 14)
                split(n0 + 15)
                dve.wait_ge(gated_done, l + 1)
                for j in range(KC):
                    taps = [w_conv[:, l, k, j:j + 1] for k in range(3)]
                    link(dve.tensor_scalar(cc[:, j, :], cg[:, j, 0:S], taps[0], None, ALU.mult))
                    for k in (1, 2):
                        link(dve.scalar_tensor_tensor(out=cc[:, j, :], in0=cg[:, j, k:k + S], scalar=taps[k],
                                                      in1=cc[:, j, :], op0=ALU.mult, op1=ALU.add))
                dve.tensor_tensor(cc[:, :, :], cc[:, :, :], cb[:, :, :], ALU.mult).then_inc(yconv_ready, 1)
                modulation(2 * l + 1)
                softmax_max(1)
                dve.wait_ge(croot, l + 1)
                link(dve.reciprocal(cb[:, 1, :], cb[:, 0, :]))
                for j in range(KC):
                    ins = dve.scalar_tensor_tensor(out=cc[:, j, :], in0=cc[:, j, :],
                                                   scalar=g_conv[:, l, j:j + 1], in1=cb[:, 1, :],
                                                   op0=ALU.mult, op1=ALU.mult)
                link(ins)
                link(dve.tensor_copy(act_hi[:, 0:KC, :], cc[:, :, :]))
                dve.tensor_tensor(act_lo[:, 0:KC, :], cc[:, :, :], act_hi[:, 0:KC, :].bitcast(F32),
                                  ALU.subtract).then_inc(ymc_ready, 1)
                dve.wait_ge(exp_done, 2 * l + 2)
                sums = stat[:, 12:36].rearrange("p (a b) -> p a b", b=8)[:, 0:3:2, :]
                link(dve.reciprocal(sums, sums))
                dve.wait_ge(pv_done, l + 1)
                for t in range(T):
                    for g in range(2):
                        ins = dve.tensor_tensor(
                            tokmaj[:, t, g * 256:(g + 1) * 256].rearrange("p (h d) -> p h d", d=HD),
                            ps[:, t, g * 256:(g + 1) * 256].rearrange("p (h d) -> p h d", d=HD),
                            stat[:, 12 + 16 * g + 4 * t:16 + 16 * g + 4 * t].unsqueeze(2)
                            .to_broadcast([P, 4, HD]), ALU.mult)
                link(ins)
                for t in range(T):
                    ins = dve.tensor_tensor_reduce(out=tokmaj[:, t, AW:2 * AW], in0=tokmaj[:, t, 0:AW],
                                                   in1=tokmaj[:, t, 0:AW], scale=1.0, scalar=0.0,
                                                   op0=ALU.mult, op1=ALU.add, accum_out=stat[:, t:t + 1])
                ins.then_inc(yatt_sum, 1)
                dve.wait_ge(yatt_root, l + 1)
                link(dve.reciprocal(stat[:, 0:2], stat[:, 2:4]))
                for t in range(T):
                    ins = dve.tensor_scalar(tokmaj[:, t, 0:AW], tokmaj[:, t, 0:AW], stat[:, t:t + 1], None,
                                            ALU.mult)
                ins.then_inc(yatt_ready, 1)
                dve.wait_ge(yf_ready, l + 1)
                link(dve.tensor_copy(act_hi[:, KC:KD, :], hf[:, KC:KD, :]))
                dve.tensor_tensor(act_lo[:, KC:KD, :], hf[:, KC:KD, :], act_hi[:, KC:KD, :].bitcast(F32),
                                  ALU.subtract).then_inc(yma_ready, 1)
                dve.wait_ge(unit_used, n0 + 16)
                residual(l, 0, 4)
                token_norm(2 * l + 1)
                activation_parts(2 * l + 1)
                dve.wait_ge(logit_done, l + 1)
                lg = rt[:, 0, :, :]
                link(dve.tensor_tensor(lg, ps[:, 0, 0:T * NR].rearrange("p (t n) -> p t n", t=T),
                                       r_b[:, l, :].unsqueeze(1).to_broadcast([P, T, NR]), ALU.add))

                def col(i):
                    return stat[:, i:i + T]

                def wide(ap, n):
                    return ap.unsqueeze(2).to_broadcast([P, T, n])

                def first_max(values, n, top, onehot):
                    link(dve.tensor_reduce(top, values, AX.X, ALU.max))
                    link(dve.tensor_tensor(onehot, values, wide(top, n), ALU.is_equal))
                    link(dve.tensor_tensor(onehot, onehot, rank[:, NE - n:NE].unsqueeze(1)
                                           .to_broadcast([P, T, n]), ALU.mult))
                    link(dve.tensor_reduce(col(50), onehot, AX.X, ALU.max))
                    link(dve.tensor_tensor(onehot, onehot, wide(col(50), n), ALU.is_equal))

                glog = lg[:, :, 0:NG]
                goh_c = rt[:, 6, :, 0:NG]
                goh, oh1, oh2, em = (rt[:, i, :, 0:n] for i, n in ((1, NG), (2, NE), (3, NE), (4, NE)))
                first_max(glog, NG, col(52), goh)
                dve.tensor_copy(goh_c, goh).then_inc(oh_ready, 1)
                dve.tensor_tensor(rt[:, 8, :, 0:NG], glog, wide(col(52), NG), ALU.subtract
                                  ).then_inc(rexp_in, 1)
                link(dve.tensor_scalar(rt[:, 5, :, 0:NG], goh, -1.0, -NEG, ALU.add, ALU.mult))
                for t in range(T):
                    e4 = [rt[:, i, t, 0:NE].rearrange("p (g e) -> p g e", e=EG) for i in (4,)][0]
                    link(dve.tensor_tensor(e4, rt[:, 0, t, NG:NR].rearrange("p (g e) -> p g e", e=EG),
                                           rt[:, 1, t, 0:NG].unsqueeze(2).to_broadcast([P, NG, EG]),
                                           ALU.mult))
                    link(dve.tensor_tensor(e4, e4, rt[:, 5, t, 0:NG].unsqueeze(2)
                                           .to_broadcast([P, NG, EG]), ALU.add))
                first_max(em, NE, col(54), oh1)
                link(dve.scalar_tensor_tensor(out=em, in0=oh1, scalar=10 * NEG, in1=em, op0=ALU.mult,
                                              op1=ALU.add))
                first_max(em, NE, col(56), oh2)
                dve.tensor_tensor(stat[:, 36:38], col(56), col(54), ALU.subtract).then_inc(rexp_in, 1)
                link(dve.tensor_scalar(slot_of[:, :, :], goh_c, -BIG, BIG, ALU.mult, ALU.add))
                dve.wait_ge(place_done, l + 1)
                link(dve.tensor_tensor(slot_of[:, :, :], slot_of[:, :, :],
                                       ps[:, 3, 0:T * NG].rearrange("p (t g) -> p t g", t=T), ALU.add))
                link(dve.tensor_scalar(over[:, :], ps[:, 3, T * NG:(T + 1) * NG], float(P), None, ALU.is_gt))
                dve.tensor_reduce(over_any[:, 0:1], over[:, :], AX.X, ALU.max)
                link(dve.tensor_tensor(rt[:, 7, 0, 0:NG], over[:, :], slots[:, 0:NG], ALU.mult))
                link(dve.tensor_reduce(over_any[:, 1:2], rt[:, 7, 0, 0:NG], AX.X, ALU.add))
                dve.tensor_copy(over_i[:, l, :], over_any[:, :]).then_inc(over_known, 1)
                for g in range(NG):
                    for t in range(T):
                        ins = dve.tensor_scalar(sel[:, g, t, :], slots[:, :], slot_of[:, t, g:g + 1], None,
                                                ALU.is_equal)
                ins.then_inc(sel_ready, 1)
                dve.wait_ge(rexp_out, 2 * l + 1)
                link(dve.tensor_reduce(col(58), rt[:, 8, :, 0:NG], AX.X, ALU.add))
                dve.wait_ge(rexp_out, 2 * l + 2)
                link(dve.tensor_scalar(col(60), stat[:, 36:38], 1.0, None, ALU.add))
                link(dve.tensor_tensor(col(60), col(60), col(58), ALU.mult))
                link(dve.reciprocal(col(60), col(60)))
                link(dve.tensor_tensor(stat[:, 38:40], stat[:, 36:38], col(60), ALU.mult))
                link(dve.tensor_tensor(oh1, oh1, wide(col(60), NE), ALU.mult))
                link(dve.tensor_tensor(oh2, oh2, wide(stat[:, 38:40], NE), ALU.mult))
                dve.tensor_tensor(combine[:, :, :], oh1, oh2, ALU.add).then_inc(comb_ready, 1)
                if l + 1 < L:
                    modulation(2 * l + 2)
                for n in range(4):
                    split(n0 + 16 + n)

                def group_parts(g):
                    dve.wait_ge(hg_ready, NG * l + g + 1)
                    if g >= 2:
                        dve.wait_ge(unit_used, n0 + 16 + gu_unit(EG * (g - 1) - 1, 1) + 1)
                    half = slice((g % 2) * P, (g % 2 + 1) * P)
                    link(dve.tensor_copy(act_hi[:, :, half], hg))
                    dve.tensor_tensor(act_lo[:, :, half], hg, act_hi[:, :, half].bitcast(F32),
                                      ALU.subtract).then_inc(group_ready, 1)

                def group_out(g):
                    dve.wait_ge(unit_used, n0 + 16 + down_unit(EG * g + EG - 1) + 1)
                    if g > 0:
                        dve.wait_ge(scatter_done, T * (NG * l + g))
                    dve.tensor_tensor(y_sb.rearrange("p (a b) -> p a b", a=2), ps[:, 4:6, :],
                                      gates[:, 1, :].rearrange("p (a b) -> p a b", a=2), ALU.mult
                                      ).then_inc(y_ready, 1)

                def spread_in(g, t):
                    dve.wait_ge(scatter_done, T * (NG * l + g) + t + 1)
                    row = res[:, t, :].rearrange("p (a b) -> p a b", a=2)
                    dve.tensor_tensor(row, row, ps[:, 6:8, :], ALU.add).then_inc(scatter_used, 1)

                group_parts(0)
                dve.wait_ge(cw_done, l + 1)
                link(dve.tensor_copy(cw[:, :], ps[:, 3, 16:16 + NE]))
                split(n0 + 20)
                dve.wait_ge(gate_evac, 2 * (2 * l + 1) + 2)
                for e in range(NE):
                    E = l * NE + e
                    g = e // EG
                    dve.wait_ge(sil_done, E + 1)
                    if e >= 2:
                        dve.wait_ge(hidT_done, E - 1)
                    dve.scalar_tensor_tensor(out=hid[:, e % 2, :], in0=ps[:, e % 2, F:2 * F],
                                             scalar=cw[:, e:e + 1], in1=sil[:, e % 2, :],
                                             op0=ALU.mult, op1=ALU.mult).then_inc(hid_ready, 1)
                    if e % EG == 0 and g > 0:
                        group_out(g - 1)
                    ahead(n0 + 16 + 3 * e + 5)
                    dve.wait_ge(hidT_hi_done, E + 1)
                    dve.tensor_tensor(hidT_lo[:, e % 2, :, :], ps[:, 2, 0:2 * P].rearrange("p (k s) -> p k s", k=2),
                                      hidT_hi[:, e % 2, :, :].bitcast(F32), ALU.subtract).then_inc(hidT_ready, 1)
                    if e % EG < T and g > 0:
                        spread_in(g - 1, e % EG)
                    ahead(n0 + 16 + 3 * e + 6)
                    if e < NE - 1:
                        ahead(n0 + 16 + 3 * e + 7)
                    if e % EG == 2 and g + 1 < NG:
                        group_parts(g + 1)
                group_out(NG - 1)
                for t in range(T):
                    spread_in(NG - 1, t)
                dve.wait_ge(over_known, l + 1)
                with dve.If(dve.value_load(over_i[0:1, l, 0:1], min_val=0, max_val=1) > 0):
                    dve.wait_ge(scatter_used, T * NG * (l + 1))
                    dve.wait_ge(selT_ready, l + 1)
                    for t in range(T):
                        x_link(dve.tensor_tensor(rt[:, 7, t, 0:NG], slot_of[:, t, :], over[:, :], ALU.mult))
                    x_link(dve.tensor_scalar(rt[:, 9, 0, 0:NG], over[:, :], -BIG, BIG, ALU.mult, ALU.add))
                    for t in range(T):
                        x_link(dve.tensor_tensor(rt[:, 7, t, 0:NG], rt[:, 7, t, 0:NG], rt[:, 9, 0, 0:NG], ALU.add))
                    x_link(dve.tensor_reduce(over_any[:, 0:T], rt[:, 7, :, 0:NG], AX.X, ALU.min))
                    for t in range(T):
                        x_link(dve.tensor_scalar(sel[:, 0, t, :], slots[:, :], over_any[:, t:t + 1], -float(P),
                                               ALU.subtract, ALU.is_equal))
                        x_link(dve.tensor_tensor(rt[:, 9, t, 0:NE].rearrange("p (e g) -> p e g", g=NG),
                                               combine[:, t, :].rearrange("p (g e) -> p e g", g=NG),
                                               over[:, :].unsqueeze(1).to_broadcast([P, EG, NG]), ALU.mult))
                        ins = dve.tensor_reduce(rt[:, 7, t, 0:EG],
                                                rt[:, 9, t, 0:NE].rearrange("p (e g) -> p e g", g=NG),
                                                AX.X, ALU.add)
                    ins.then_inc(x_sel, 1)
                    dve.wait_ge(x_in, l + 1)
                    dve.tensor_copy(cw[:, 0:EG], ps[:, 3, 0:EG]).then_inc(x_cw, 1)
                    dve.wait_ge(x_cw, l + 1)
                    for i in range(EG):
                        dve.wait_ge(x_sil, EG * l + i + 1)
                        dve.scalar_tensor_tensor(out=hid[:, 0, :], in0=ps[:, 0, F:2 * F], scalar=cw[:, i:i + 1],
                                                 in1=sil[:, 0, :], op0=ALU.mult, op1=ALU.mult
                                                 ).then_inc(x_hid, 1)
                    dve.wait_ge(x_used, 3 * EG * (l + 1))
                    dve.tensor_tensor(y_sb.rearrange("p (a b) -> p a b", a=2), ps[:, 4:6, :],
                                      gates[:, 1, :].rearrange("p (a b) -> p a b", a=2), ALU.mult
                                      ).then_inc(x_y, 1)
                    for t in range(T):
                        dve.wait_ge(x_back, T * l + t + 1)
                        row = res[:, t, :].rearrange("p (a b) -> p a b", a=2)
                        dve.tensor_tensor(row, row, ps[:, 6:8, :], ALU.add).then_inc(x_added, 1)
                with dve.Else():
                    dve.sem_inc(x_step, x_steps[0] // (l + 1))
                    dve.sem_inc(x_sel, 1)
                    dve.sem_inc(x_cw, 1)
                    dve.sem_inc(x_hid, EG)
                    dve.sem_inc(x_y, 1)
                    dve.sem_inc(x_added, T)
                dve.drain().then_inc(res_ready, 1)


        @block.tensor
        def _(pe):
            def wait_unit(n):
                pe.wait_ge(lo_done, n + 1)
                r = n % RING
                return whi[:, r, :], wlo[:, r, :]

            def ada_half(a):
                for b in range(6):
                    B = 6 * a + b
                    bank = 4 + b % 2
                    if b >= 2:
                        pe.wait_ge(mod_evac, B - 1)
                    for k in range(KD):
                        if k % 4 == 0:
                            pe.wait_ge(ada_full[k // 4], 16 * (B + 1))
                        q = k % 4
                        ins = pe.matmul(ps[32 * q:32 * q + 32, bank, :], c_rep[:, k, :],
                                        ada_raw[:, k // 4, k % 4, :], start=(k < 4), stop=(k >= 4 and q > 0),
                                        skip_group_check=True)
                        if k % 4 == 3:
                            ins.then_inc(ada_used, 1)
                    pe.wait_ge(bias_full, 16 * (B + 1))
                    pe.matmul(ps[0:32, bank, :], ones[:, 0:32], ada_bias[:, :], start=False, stop=True,
                              skip_group_check=True).then_inc(acc_done, 1)
                    if b % 2 == 0:
                        continue
                    v = b // 2
                    pe.wait_ge(mod_evac, B + 1)
                    if v < 2:
                        for j in range(KD):
                            ins = pe.matmul(ps[:, 6, v * KD + j:v * KD + j + 1], mod_rows[:, j::KD],
                                            rowsel[:, 0:1], start=True, stop=True)
                            if j == KD - 1:
                                ins.then_inc(mod_used, 1)
                    else:
                        for n in range(2):
                            if n == 1:
                                pe.wait_ge(gate_evac, 2 * a + 1)
                            pe.matmul(ps[:, 7, :], rowsel[:, :], mod_rows[:, n * 512:(n + 1) * 512],
                                      start=True, stop=True).then_inc(gate_done, 1)

            def transposes(m):
                pe.wait_ge(xn_ready, T * (m + 1))
                for bank in range(4):
                    for j in (2 * bank, 2 * bank + 1):
                        for t in range(T):
                            ins = pe.transpose(ps[:, bank, (j % 2) * S + t * P:(j % 2) * S + (t + 1) * P],
                                               tokmaj[:, t, j::KD], ident[:, :])
                    ins.then_inc(xT_done, 1)

            acts = (act_hi, act_lo)

            pe.wait_ge(const_ready, 5)
            pe.wait_ge(rowsel_ready, 1)
            pe.wait_ge(crep_ready, 2)
            ada_half(0)
            for l in range(L):
                n0 = l * UL
                transposes(2 * l)
                for i in range(3):
                    bank = (4, 6, 0)[i]
                    for half in range(2):
                        w = wait_unit(n0 + 2 * i + half)
                        pe.wait_ge(act_ready, 4 * 2 * l + (4 if i else 2 * half + 2))
                        for kk in range(4):
                            k = 4 * half + kk
                            for t in range(T):
                                for p, (pa, pw) in enumerate(PASSES):
                                    ins = pe.matmul(ps[:, bank + t, :], acts[pa][:, k, t * P:(t + 1) * P],
                                                    w[pw][:, kk * 512:(kk + 1) * 512],
                                                    start=(k == 0 and p == 0), stop=(k == KD - 1 and p == 2))
                        ins.then_inc(unit_used, 1)

                def conv_block(i, bank):
                    for half in range(2):
                        w = wait_unit(n0 + 6 + 2 * i + half)
                        for kk in range(4):
                            k = 4 * half + kk
                            for j in range(KC):
                                for p, (pa, pw) in enumerate(PASSES):
                                    ins = pe.matmul(ps[:, bank + j // 2, (j % 2) * S:(j % 2 + 1) * S],
                                                    w[pw][:, kk * 512 + j:(kk + 1) * 512:KC],
                                                    acts[pa][:, k, :], start=(k == 0 and p == 0 and j % 2 == 0),
                                                    stop=(k == KD - 1 and p == 2), skip_group_check=True)
                        ins.then_inc(unit_used, 1)

                conv_block(0, 2)
                pe.wait_ge(proj_evac, 5 * l + 1)
                conv_block(1, 4)
                pe.wait_ge(rope_done, T * (l + 1))
                for w in range(2):
                    pe.wait_ge(proj_evac, 5 * l + 3 + w)
                    for cpair in range(H // 2):
                        for t in range(T):
                            a0 = (cpair % 2) * S + t * P
                            ins = pe.transpose(ps[:, 2 * w + cpair // 2, a0:a0 + P],
                                               tokmaj[:, t, w * AW + cpair * P:w * AW + (cpair + 1) * P],
                                               ident[:, :])
                    ins.then_inc(qkT_done, 1)
                pe.wait_ge(proj_evac, 5 * l + 2)
                conv_block(2, 6)

                def scores(g):
                    for hh in range(4):
                        h = 4 * g + hh
                        rows = slice((h % 2) * HD, (h % 2) * HD + HD)
                        for t in range(T):
                            cols = slice(0, P) if t == 0 else slice(P, 384)
                            ins = pe.matmul(ps[:, 4 * g + hh, cols], qkT[rows, 0, h // 2, t * P:(t + 1) * P],
                                            qkT[rows, 1, h // 2, 0:(t + 1) * P], start=True, stop=True)
                    ins.then_inc(scores_done, 1)

                pe.wait_ge(qkT_ready, 2 * l + 2)
                scores(0)
                pe.wait_ge(proj_evac, 5 * l + 5)
                pe.wait_ge(gated_done, l + 1)
                ada_half(2 * l + 1)
                pe.wait_ge(gate_evac, 2 * (2 * l + 1) + 2)
                pe.wait_ge(mod_ready, 2 * l + 2)
                scores(1)
                for g in range(2):
                    pe.wait_ge(exp_done, 2 * l + g + 1)
                    for hh in range(4):
                        for q in range(3):
                            ins = pe.transpose(ps[:, 4 * g + hh, q * P:(q + 1) * P],
                                               work[:, g, hh, q * P:(q + 1) * P], ident[:, :])
                    ins.then_inc(pT_done, 1)
                for g in range(2):
                    if g == 0:
                        pe.wait_ge(pT_ready, 2 * l + 1)
                    else:
                        pe.wait_ge(pT_ready, 2 * l + 2)
                    for hh in range(4):
                        h = 4 * g + hh
                        vs = slice(h * HD, (h + 1) * HD)
                        pe.matmul(ps[:, 0, vs], work[:, g, hh, 0:P], v_sb[:, 0, vs], start=True, stop=True)
                        pe.matmul(ps[:, 1, vs], work[:, g, hh, P:2 * P], v_sb[:, 0, vs], start=True, stop=False)
                        ins = pe.matmul(ps[:, 1, vs], work[:, g, hh, 2 * P:3 * P], v_sb[:, 1, vs],
                                        start=False, stop=True)
                ins.then_inc(pv_done, 1)
                pe.wait_ge(csq_ready, l + 1)
                for j in range(KC):
                    ins = pe.matmul(ps[:, 2, 0:S], ones[:, :], cb[:, j, :], start=(j == 0), stop=(j == KC - 1))
                ins.then_inc(csum_done, 1)

                def out_proj(s):
                    for half in range(2):
                        w = wait_unit(n0 + 12 + 2 * s + half)
                        for kk in range(2):
                            k = 4 * s + 2 * half + kk
                            for t in range(T):
                                for p, (pa, pw) in enumerate(PASSES):
                                    for n in range(2):
                                        c0 = kk * D + n * 512
                                        ins = pe.matmul(ps[:, 4 + 2 * t + n, :],
                                                        acts[pa][:, k, t * P:(t + 1) * P],
                                                        w[pw][:, c0:c0 + 512], start=(k == 0 and p == 0),
                                                        stop=(k == KD - 1 and p == 2))
                        ins.then_inc(unit_used, 1)

                pe.wait_ge(ymc_ready, l + 1)
                out_proj(0)
                pe.wait_ge(yatt_ready, l + 1)
                for j in range(KC):
                    for t in range(T):
                        a0 = (j % 2) * S + t * P
                        ins = pe.transpose(ps[:, j // 2, a0:a0 + P], tokmaj[:, t, j:AW:KC], ident[:, :])
                ins.then_inc(yT_done, 1)
                pe.wait_ge(yma_ready, l + 1)
                out_proj(1)
                transposes(2 * l + 1)
                pe.wait_ge(act_ready, 4 * (2 * l + 2))
                rw = (r_hi, r_lo)
                for t in range(T):
                    for k in range(KD):
                        for p, (pa, pw) in enumerate(PASSES):
                            ins = pe.matmul(ps[:, 0, t * NR:(t + 1) * NR], acts[pa][:, k, t * P:(t + 1) * P],
                                            rw[pw][:, l, k, :], start=(k == 0 and p == 0),
                                            stop=(k == KD - 1 and p == 2))
                ins.then_inc(logit_done, 1)
                pe.wait_ge(oh_ready, l + 1)
                goh = rt[:, 6, :, 0:NG]
                pe.matmul(ps[:, 3, 0:NG], before[:, :], goh[:, 0, :], start=True, stop=True)
                pe.matmul(ps[:, 3, NG:2 * NG], before[:, :], goh[:, 1, :], start=True, stop=False)
                pe.matmul(ps[:, 3, NG:2 * NG], ones[:, :], goh[:, 0, :], start=False, stop=True)
                for t in range(T):
                    ins = pe.matmul(ps[:, 3, 2 * NG:3 * NG], ones[:, :], goh[:, t, :], start=(t == 0),
                                    stop=(t == T - 1))
                ins.then_inc(place_done, 1)
                if l + 1 < L:
                    ada_half(2 * l + 2)
                    pe.wait_ge(gate_evac, 2 * (2 * l + 2) + 2)
                    pe.wait_ge(mod_ready, 2 * l + 3)

                def gather(g):
                    if g > 0:
                        pe.wait_ge(scatter_used, T * (NG * l + g - 1))
                        pe.wait_ge(hg_ready, NG * l + g)
                    for k in range(KD):
                        for t in range(T):
                            ins = pe.matmul(ps[:, 6 + k // 4, (k % 4) * P:(k % 4 + 1) * P],
                                            tokmaj[:, t, k::KD], sel[:, g, t, :],
                                            start=(t == 0), stop=(t == T - 1))
                    ins.then_inc(gather_done, 1)

                def scatter(g, t):
                    pe.wait_ge(y_ready, NG * l + g + 1)
                    if g < NG - 1:
                        pe.wait_ge(hg_ready, NG * l + g + 1)
                    if t > 0:
                        pe.wait_ge(scatter_used, T * (NG * l + g) + t)
                    for n in range(2):
                        ins = pe.matmul(ps[:, 6 + n, :], selT[:, g, t, :], y_sb[:, n * 512:(n + 1) * 512],
                                        start=True, stop=True)
                    ins.then_inc(scatter_done, 1)

                def gate_up(e, half):
                    E = l * NE + e
                    g = e // EG
                    if half == 0:
                        pe.wait_ge(group_ready, NG * l + g + 1)
                        if e >= 2:
                            pe.wait_ge(hid_ready, E - 1)
                    w = wait_unit(n0 + 16 + gu_unit(e, half))
                    cols = slice((g % 2) * P, (g % 2 + 1) * P)
                    for kk in range(4):
                        k = 4 * half + kk
                        for p, (pa, pw) in enumerate(PASSES):
                            ins = pe.matmul(
                                ps[:, e % 2, :], acts[pa][:, k, cols],
                                w[pw].rearrange("p (g k f) -> p g k f", g=2, k=4)[:, :, kk, :],
                                start=(k == 0 and p == 0), stop=(k == KD - 1 and p == 2))
                    return ins

                def hid_transpose(e):
                    E = l * NE + e
                    pe.wait_ge(hid_ready, E + 1)
                    if E > 0:
                        pe.wait_ge(hidT_ready, E)
                    for kk in range(2):
                        ins = pe.transpose(ps[:, 2, kk * P:(kk + 1) * P], hid[:, e % 2, kk::2], ident[:, :])
                    ins.then_inc(hidT_done, 1)

                def down(e):
                    E = l * NE + e
                    g, i = e // EG, e % EG
                    w = wait_unit(n0 + 16 + down_unit(e))
                    pe.wait_ge(hidT_ready, E + 1)
                    if i == 0 and g > 0:
                        pe.wait_ge(y_ready, NG * l + g)
                    hT = (hidT_hi, hidT_lo)
                    for kk in range(2):
                        for p, (pa, pw) in enumerate(PASSES):
                            for n in range(2):
                                c0 = kk * D + n * 512
                                ins = pe.matmul(ps[:, 4 + n, :], hT[pa][:, e % 2, kk, :],
                                                w[pw][:, c0:c0 + 512], start=(i == 0 and kk == 0 and p == 0),
                                                stop=(i == EG - 1 and kk == 1 and p == 2))
                    ins.then_inc(unit_used, 1)

                pe.wait_ge(sel_ready, l + 1)
                gather(0)
                for g in range(NG):
                    for t in range(T):
                        i = T * g + t
                        ins = pe.transpose(ps[:, 4 + i // 4, (i % 4) * P:(i % 4 + 1) * P], sel[:, g, t, :],
                                           ident[:, :])
                ins.then_inc(selT_done, 1)
                pe.wait_ge(comb_ready, l + 1)
                for g in range(NG):
                    for t in range(T):
                        ins = pe.matmul(ps[:, 3, 16 + EG * g:16 + EG * (g + 1)], sel[:, g, t, :],
                                        combine[:, t, EG * g:EG * (g + 1)], start=(t == 0), stop=(t == T - 1))
                ins.then_inc(cw_done, 1)
                gate_up(0, 0).then_inc(unit_used, 1)
                pe.wait_ge(selT_ready, l + 1)
                gate_up(0, 1).then_inc(unit_used, 1)
                for e in range(NE):
                    g, i = e // EG, e % EG
                    if e + 1 < NE:
                        gate_up(e + 1, 0).then_inc(unit_used, 1)
                    hid_transpose(e)
                    if i == 2 and g + 1 < NG:
                        gather(g + 1)
                    if e + 1 < NE:
                        gate_up(e + 1, 1).then_inc(unit_used, 1)
                    if i < T and g > 0:
                        scatter(g - 1, i)
                    down(e)
                for t in range(T):
                    scatter(NG - 1, t)
                pe.wait_ge(over_known, l + 1)
                with pe.If(pe.value_load(over_i[0:1, l, 0:1], min_val=0, max_val=1) > 0):
                    pe.wait_ge(x_sel, l + 1)
                    pe.wait_ge(scatter_used, T * NG * (l + 1))
                    for k in range(KD):
                        for t in range(T):
                            pe.matmul(ps[:, 6 + k // 4, (k % 4) * P:(k % 4 + 1) * P], tokmaj[:, t, k::KD],
                                      sel[:, 0, t, :], start=(t == 0), stop=(t == T - 1))
                    for t in range(T):
                        pe.transpose(ps[:, 1, t * P:(t + 1) * P], sel[:, 0, t, :], ident[:, :])
                    for t in range(T):
                        ins = pe.matmul(ps[:, 3, 0:EG], sel[:, 0, t, :], rt[:, 7, t, 0:EG], start=(t == 0),
                                        stop=(t == T - 1))
                    ins.then_inc(x_in, 1)
                    pe.wait_ge(x_hg, l + 1)
                    pe.wait_ge(x_cw, l + 1)
                    for i in range(EG):
                        loads = X_LOADS * l + 16 * 5 * i
                        if i > 0:
                            pe.wait_ge(x_hid, EG * l + i)
                        for half in range(2):
                            pe.wait_ge(x_full, loads + 32 * (half + 1))
                            w = stage.rearrange("p (g k f) -> p g k f", g=2, k=4)
                            for kk in range(4):
                                k = 4 * half + kk
                                ins = pe.matmul(ps[:, 0, :], hg[:, k, :], w[:, :, kk, :], start=(k == 0),
                                                stop=(k == KD - 1))
                            ins.then_inc(x_used, 1)
                        pe.wait_ge(x_hid, EG * l + i + 1)
                        for kk in range(2):
                            ins = pe.transpose(ps[:, 2, kk * P:(kk + 1) * P], hid[:, 0, kk::2], ident[:, :])
                        ins.then_inc(x_hidT, 1)
                        pe.wait_ge(x_full, loads + 80)
                        pe.wait_ge(x_hidT_out, EG * l + i + 1)
                        for kk in range(2):
                            for n in range(2):
                                c0 = kk * D + n * 512
                                ins = pe.matmul(ps[:, 4 + n, :], hidT_x[:, kk, :], stage[:, c0:c0 + 512],
                                                start=(i == 0 and kk == 0), stop=(i == EG - 1 and kk == 1))
                        ins.then_inc(x_used, 1)
                    pe.wait_ge(x_y, l + 1)
                    for t in range(T):
                        if t > 0:
                            pe.wait_ge(x_added, T * l + t)
                        for n in range(2):
                            ins = pe.matmul(ps[:, 6 + n, :], selT[:, 0, t, :], y_sb[:, n * 512:(n + 1) * 512],
                                            start=True, stop=True)
                        ins.then_inc(x_back, 1)
                with pe.Else():
                    pe.sem_inc(x_in, 1)
                    pe.sem_inc(x_used, 3 * EG)
                    pe.sem_inc(x_hidT, EG)
                    pe.sem_inc(x_back, T)


_INS = ["x", "c", "positions", "norm1_g", "norm2_g", "w_ada", "b_ada", "w_in", "conv_w", "q_norm_g",
        "k_norm_g", "conv_out_g", "attn_out_g", "w_out", "w_router_group", "b_router_group",
        "w_router_expert", "b_router_expert", "w_gate", "w_up", "w_down"]


def kernel(**inputs):
    import concourse.bacc as _bacc
    from concourse.bass_utils import run_bass_kernel_spmd as _run

    nc = _bacc.Bacc("TRN2", target_bir_lowering=False, num_devices=1, dynamic_dma_scratch_size=4096)
    arrays, args = {}, []
    for name in _INS:
        a = np.ascontiguousarray(inputs[name])
        arrays[f"in_{name}_dram"] = a
        args.append(nc.dram_tensor(f"in_{name}_dram", a.shape, mybir.dt.from_np(a.dtype),
                                   kind="ExternalInput").ap())
    shape = tuple(inputs["x"].shape)
    args.append(nc.dram_tensor("out_0_dram", shape, F32, kind="ExternalOutput").ap())
    trunk(nc, *args)
    r = _run(nc, [arrays], core_ids=[0])
    return r.results[0]["out_0_dram"]
```

```python
from contextlib import ExitStack

import concourse.bass as bass
import numpy as np
from concourse import mybir

ALU = mybir.AluOpType
ACT = mybir.ActivationFunctionType
AX = mybir.AxisListType
F32 = mybir.dt.float32
F32R = mybir.dt.float32r
I32 = mybir.dt.int32

P = 128
EPS = 1e-6
NEG = -1e30
ROPE_THETA = 10000.0
TOP_MAGIC = 12582912.0
TWO_PI_A = 6.28125
TWO_PI_B = 0.00193500518798828125
TWO_PI_C = 2 * np.pi - TWO_PI_A - TWO_PI_B
PI_IN = 3.1415925
BIG = 4096.0
RING = 4
RAW = 7
PAIR_BANK = (0, 4, 2, 0)
PASSES = ((0, 0), (0, 1), (1, 0))


def trunk(nc, x, c, positions, norm1_g, norm2_g, w_ada, b_ada, w_in, conv_w, q_norm_g, k_norm_g,
          conv_out_g, attn_out_g, w_out, w_rg, b_rg, w_re, b_re, w_gate, w_up, w_down, out):
    _, S, D = x.shape
    L = norm1_g.shape[0]
    CW = conv_out_g.shape[1]
    AW = attn_out_g.shape[1]
    HD = q_norm_g.shape[1]
    H = AW // HD
    NE, _, F = w_gate.shape[1:]
    NG = w_rg.shape[2]
    EG = NE // NG
    NR = NG + NE
    T = S // P
    KD = D // P
    KC = CW // P
    HH = HD // 2
    SCALE = float(HD) ** -0.5
    assert (S, D, CW, AW, HD, F) == (256, 1024, 512, 512, 64, 256)
    UL = 16 + 3 * NE
    NU = L * UL

    x_v = x.rearrange("a (t p) d -> (a p) t d", p=P)
    out_v = out.rearrange("a (t p) d -> (a p) t d", p=P)
    win_v = w_in.rearrange("l (p k) n -> l p k n", k=KD)
    wout_v = w_out.rearrange("l (s p k) n -> l s p k n", s=2, k=KC)
    ada_v = w_ada.rearrange("l (p k) n -> l p k n", k=KD)
    gate_v = w_gate.rearrange("l e (p k) f -> l e p k f", k=KD)
    up_v = w_up.rearrange("l e (p k) f -> l e p k f", k=KD)
    down_v = w_down.rearrange("l e (p k) d -> l e p k d", k=2)
    IN_ORDER = (3, 4, 5, 0, 1, 2)

    with ExitStack() as ctx:
        def sb(name, shape, dt=F32):
            return ctx.enter_context(nc.sbuf_tensor(name, shape, dt))

        def sem(name):
            return ctx.enter_context(nc.semaphore(name))

        ps = ctx.enter_context(nc.psum_tensor("ps", [P, 8, 512], F32))

        raw = sb("raw", [P, RAW, 2048])
        whi = sb("whi", [P, RING, 2048], F32R)
        wlo = sb("wlo", [P, RING, 2048], F32R)
        mod_rows = sb("mod_rows", [P, D])
        gates = sb("gates", [P, 2, D])
        res = sb("res", [P, T, D])
        act_hi = sb("act_hi", [P, KD, S], F32R)
        act_lo = sb("act_lo", [P, KD, S], F32R)
        tokmaj = sb("tokmaj", [P, T, D])
        qkT = sb("qkT", [P, 2, H // 2, S])
        v_sb = sb("v_sb", [P, T, AW])
        cb = sb("cb", [P, KC, S])
        cc = sb("cc", [P, KC, S])
        cg = sb("cg", [P, KC, S + 2])
        work = sb("work", [P, 2, 4, 384])
        wflat = work[:, :, :, :].rearrange("p a b c -> p (a b c)")
        hf = wflat[:, 0:KD * S].rearrange("p (k s) -> p k s", k=KD)
        slots_i = wflat[:, 1024:1024 + P].bitcast(I32)
        ident = sb("ident", [P, P])
        ones = sb("ones", [P, P])
        rowsel = sb("rowsel", [P, P])
        mask = sb("mask", [P, 384])
        c_col = sb("c_col", [P, KD])
        c_rep = sb("c_rep", [P, KD, 32])
        g_norm = sb("g_norm", [P, 2, L, KD])
        g_qk = sb("g_qk", [P, L, 2, HD])
        g_conv = sb("g_conv", [P, L, KC])
        g_attn = sb("g_attn", [P, L, KC])
        w_conv = sb("w_conv", [P, L, 3, KC])
        r_w = wflat[:, 0:L * KD * NR].rearrange("p (l k n) -> p l k n", l=L, k=KD)
        r_hi = sb("r_hi", [P, L, KD, NR], F32R)
        r_lo = sb("r_lo", [P, L, KD, NR], F32R)
        r_b = sb("r_b", [P, L, NR])
        pos_i = sb("pos_i", [P, T], I32)
        pos_f = sb("pos_f", [P, T])
        invf = sb("invf", [P, HH])
        ang = wflat[:, 512:512 + 3 * T * HH].rearrange("p (a t d) -> p a t d", a=3, t=T)
        sincos = sb("sincos", [P, 2, T, HH])
        trig = sb("trig", [P, 2, T, 2, HD])
        mod_t = sb("mod_t", [P, 2, 2, KD])
        mod_b = sb("mod_b", [P, L, 6, KD])
        stat = sb("stat", [P, 64])
        rt = sb("rt", [P, 10, T, NR])
        rank = sb("rank", [P, NE])
        combine = sb("combine", [P, T, NE])
        sil = wflat[:, 0:2 * F].rearrange("p (b f) -> p b f", b=2)
        hid = wflat[:, 2 * F:4 * F].rearrange("p (b f) -> p b f", b=2)
        sel = wflat[:, 1024:1024 + NG * T * P].rearrange("p (g t s) -> p g t s", g=NG, t=T)
        selT = cb[:, :, :].rearrange("p k s -> p (k s)").rearrange("p (g t s) -> p g t s", g=NG, t=T)
        hg = cc[:, :, :].rearrange("p k s -> p (k s)").rearrange("p (k s) -> p k s", k=KD)
        logitT = v_sb[0:NR, 0, 0:S]
        y_sb = v_sb[:, :, :].rearrange("p t d -> p (t d)")
        hidT_hi = sb("hidT_hi", [P, 2, 2, P], F32R)
        hidT_lo = sb("hidT_lo", [P, 2, 2, P], F32R)
        before = sb("before", [P, P])
        slots = sb("slots", [P, P])
        slot_of = sb("slot_of", [P, T, NG])
        cw = sb("cw", [P, NE])
        over = sb("over", [P, NG])
        over_any = sb("over_any", [P, 2])
        over_i = sb("over_i", [P, L, 2], I32)
        stage = qkT[:, :, :, :].rearrange("p w c s -> p (w c s)")
        hidT_x = wflat[:, 2048:2048 + 2 * P].rearrange("p (k s) -> p k s", k=2)

        c_landed = sem("c_landed")
        x_landed = sem("x_landed")
        par_in = sem("par_in")
        raw_full = [sem(f"raw_full{r}") for r in range(RAW)]
        gate_bias = sem("gate_bias")
        out_done = sem("out_done")
        hi_done = sem("hi_done")
        lo_done = sem("lo_done")
        unit_used = sem("unit_used")
        const_ready = sem("const_ready")
        rowsel_ready = sem("rowsel_ready")
        crep_ready = sem("crep_ready")
        ada_used = sem("ada_used")
        acc_done = sem("acc_done")
        mod_evac = sem("mod_evac")
        mod_used = sem("mod_used")
        mod_ready = sem("mod_ready")
        shift_ready = sem("shift_ready")
        gate_ready = sem("gate_ready")
        rstd_sum = sem("rstd_sum")
        rstd_root = sem("rstd_root")
        xn_ready = sem("xn_ready")
        xT_done = sem("xT_done")
        hf_ready = sem("hf_ready")
        act_ready = sem("act_ready")
        proj_evac = sem("proj_evac")
        qk_sum = sem("qk_sum")
        qk_root = sem("qk_root")
        rope_done = sem("rope_done")
        qkT_done = sem("qkT_done")
        qkT_ready = sem("qkT_ready")
        gated_done = sem("gated_done")
        scores_done = sem("scores_done")
        max_ready = sem("max_ready")
        exp_done = sem("exp_done")
        pT_done = sem("pT_done")
        pT_ready = sem("pT_ready")
        pv_done = sem("pv_done")
        yconv_ready = sem("yconv_ready")
        csq_ready = sem("csq_ready")
        csum_done = sem("csum_done")
        croot = sem("croot")
        ymc_ready = sem("ymc_ready")
        yatt_raw = sem("yatt_raw")
        yatt_sum = sem("yatt_sum")
        yatt_root = sem("yatt_root")
        yatt_ready = sem("yatt_ready")
        row_done = sem("row_done")
        yT_done = sem("yT_done")
        yf_ready = sem("yf_ready")
        yma_ready = sem("yma_ready")
        logitT_done = sem("logitT_done")
        logitT_ready = sem("logitT_ready")
        logit_done = sem("logit_done")
        rexp_in = sem("rexp_in")
        rexp_out = sem("rexp_out")
        oh_ready = sem("oh_ready")
        place_done = sem("place_done")
        count_done = sem("count_done")
        sel_ready = sem("sel_ready")
        selT_done = sem("selT_done")
        selT_ready = sem("selT_ready")
        comb_ready = sem("comb_ready")
        cw_done = sem("cw_done")
        gather_done = sem("gather_done")
        hg_ready = sem("hg_ready")
        group_ready = sem("group_ready")
        y_ready = sem("y_ready")
        scatter_done = sem("scatter_done")
        scatter_used = sem("scatter_used")
        over_known = sem("over_known")
        x_step = sem("x_step")
        x_sel = sem("x_sel")
        x_in = sem("x_in")
        x_hg = sem("x_hg")
        x_cw = sem("x_cw")
        x_full = sem("x_full")
        x_used = sem("x_used")
        x_sil = sem("x_sil")
        x_hid = sem("x_hid")
        x_hidT = sem("x_hidT")
        x_hidT_out = sem("x_hidT_out")
        x_y = sem("x_y")
        x_back = sem("x_back")
        x_added = sem("x_added")
        sil_done = sem("sil_done")
        hid_ready = sem("hid_ready")
        hidT_done = sem("hidT_done")
        hidT_hi_done = sem("hidT_hi_done")
        hidT_ready = sem("hidT_ready")
        res_ready = sem("res_ready")
        act_step = sem("act_step")
        dve_step = sem("dve_step")
        pool_step = sem("pool_step")

        def gu_unit(e, half):
            return half if e == 0 else 3 * e - 1 + half

        def down_unit(e):
            return 3 * e + 4 if e < NE - 1 else 3 * NE - 1

        def spread_bank(g, t):
            return 0 if g == NG - 1 and t == T - 1 else 6

        X_LOADS = 16 * 5 * EG

        two_dma = {gu_unit(e, half) for e in range(NE) for half in range(2)}

        vectors = [(0, 0), (0, 1)]
        for l in range(L):
            vectors += [(l, 2), (l, 3), (l, 4), (l, 5)] + ([(l + 1, 0), (l + 1, 1)] if l + 1 < L else [])
        place_of = {v: q for q, v in enumerate(vectors)}

        stream = [("a", j) for j in range(8)] + [("w", n) for n in range(RING)]
        quarters = 8
        for l in range(L):
            runs = [(2, 2), (2, 2), (2, 2), (2, 2), (4, 2), (4, 2)]
            if l + 1 < L:
                runs += [(4, 2), (4, 0)]
            n = l * UL + RING
            for quarter_run, weight_run in runs:
                stream += [("a", quarters + j) for j in range(quarter_run)]
                stream += [("w", n + i) for i in range(weight_run)]
                quarters += quarter_run
                n += weight_run
            stream += [("w", i) for i in range(n, (l + 1) * UL)]
            if l + 1 < L:
                stream += [("w", (l + 1) * UL + n) for n in range(RING)]
            stream.append(("x", l))
        slot_of_unit, landed = {}, {}
        counts, pos = [0] * RAW, 0
        for unit in stream:
            if unit[0] == "x":
                continue
            r = pos % RAW
            two = unit[0] == "w" and unit[1] % UL - 16 in two_dma
            counts[r] += 32 if two else 16
            slot_of_unit[unit], landed[unit] = r, counts[r]
            pos += 1

        block = ctx.enter_context(nc.Block())
        NPAR = 9 + 4 * L

        @block.sync
        def _(sp):
            def weight(n):
                l, i = n // UL, n % UL
                raw_n = raw[:, slot_of_unit[("w", n)], :]
                if i < 12:
                    blk, half = IN_ORDER[i // 2], i % 2
                    return [(raw_n.rearrange("p (k n) -> p k n", k=4),
                             win_v[l, :, 4 * half:4 * half + 4, blk * 512:(blk + 1) * 512])]
                if i < 16:
                    i -= 12
                    return [(raw_n.rearrange("p (k n) -> p k n", k=2),
                             wout_v[l, i // 2, :, 2 * (i % 2):2 * (i % 2) + 2, :])]
                for e in range(NE):
                    if i - 16 == down_unit(e):
                        return [(raw_n.rearrange("p (k n) -> p k n", k=2), down_v[l, e])]
                    for half in range(2):
                        if i - 16 == gu_unit(e, half):
                            dst = raw_n.rearrange("p (g k f) -> p g k f", g=2, k=4)
                            return [(dst[:, g, :, :], w[l, e, :, 4 * half:4 * half + 4, :])
                                    for g, w in enumerate((gate_v, up_v))]

            def quarter(j):
                (l, which), b, u = vectors[j // 4], j // 2 % 2, j % 2
                c0 = which * D + b * 512
                return [(raw[:, slot_of_unit[("a", j)], :].rearrange("p (k n) -> p k n", k=4),
                         ada_v[l, :, 4 * u:4 * u + 4, c0:c0 + 512])]

            def extra_loads(l):
                sp.wait_ge(over_known, l + 1)
                with sp.If(sp.value_load(over_i[0:1, l, 0:1], min_val=0, max_val=1) > 0):
                    first = sp.value_load(over_i[0:1, l, 1:2], min_val=0, max_val=NG - 1) * EG
                    sp.wait_ge(unit_used, l * UL + 16)
                    for i in range(EG):
                        one = bass.ds(first + i, 1)
                        for part in range(3):
                            sp.wait_ge(x_used, 3 * EG * l + 3 * i + part)
                            if part < 2:
                                dst = stage.rearrange("p (g k f) -> p g k f", g=2, k=4)
                                for g, w in enumerate((gate_v, up_v)):
                                    sp.dma_start(dst[:, g, :, :], w[l, one, :, 4 * part:4 * part + 4, :]
                                                 .rearrange("a p k f -> (a p) k f")).then_inc(x_full, 16)
                            else:
                                sp.dma_start(stage.rearrange("p (k n) -> p k n", k=2), down_v[l, one]
                                             .rearrange("a p k n -> (a p) k n")).then_inc(x_full, 16)
                with sp.Else():
                    sp.sem_inc(x_full, X_LOADS)

            holder = [None] * RAW
            for kind, n in stream:
                if kind == "x":
                    extra_loads(n)
                    continue
                r = slot_of_unit[(kind, n)]
                if holder[r] is not None:
                    was, m = holder[r]
                    if was == "w":
                        sp.wait_ge(lo_done, m + 1)
                    else:
                        sp.wait_ge(acc_done if m % 2 else ada_used, m // 2 + 1)
                holder[r] = (kind, n)
                for dst, src in (weight(n) if kind == "w" else quarter(n)):
                    sp.dma_start(dst, src).then_inc(raw_full[r], 16)
            sp.wait_ge(res_ready, L)
            sp.dma_start(out_v, res[:, :, :]).then_inc(out_done, 16)
            sp.wait_ge(out_done, 16)

        @block.gpsimd
        def _(pool):
            pool.memset(ident[:, :], 0.0).then_inc(pool_step, 1)
            pool.memset(mask[:, :], 0.0).then_inc(pool_step, 1)
            pool.memset(before[:, :], 0.0).then_inc(pool_step, 1)
            pool.memset(ones[:, :], 1.0)
            for i in range(HH):
                pool.memset(invf[:, i:i + 1],
                            float(np.float32(ROPE_THETA) ** (-np.float32(2 * i) / np.float32(HD))))
            for i in range(NE):
                pool.memset(rank[:, i:i + 1], float(NE - i))
            pool.memset(cg[:, :, 0:2], 0.0).then_inc(const_ready, 1)
            pool.wait_ge(pool_step, 1)
            pool.affine_select(out=ident[:, :], in_=ident[:, :], compare_op=ALU.not_equal, fill=1.0,
                               base=0, pattern=[[-1, P]], channel_multiplier=1).then_inc(const_ready, 1)
            pool.wait_ge(pool_step, 3)
            pool.affine_select(out=before[:, :], in_=before[:, :], compare_op=ALU.is_ge, fill=1.0,
                               base=0, pattern=[[-1, P]], channel_multiplier=1).then_inc(const_ready, 1)
            pool.iota(slots_i[:, :], pattern=[[1, P]], base=0, channel_multiplier=0).then_inc(const_ready, 1)
            for a in (0, 256):
                last = pool.affine_select(out=mask[:, a:a + P], in_=mask[:, a:a + P], compare_op=ALU.is_ge,
                                          fill=NEG, base=0, pattern=[[-1, P]], channel_multiplier=1)
            last.then_inc(const_ready, 1)

        @block.scalar
        def _(act):
            steps = [0]

            def link(ins):
                steps[0] += 1
                ins.then_inc(act_step, 1)
                act.wait_ge(act_step, steps[0])

            def load(dst, src):
                act.dma_start(dst, src).then_inc(par_in, 16)

            act.dma_start(c_col[:, :], c.rearrange("a (p k) -> (a p) k", k=KD)).then_inc(c_landed, 16)
            act.dma_start(res[:, :, :], x_v).then_inc(x_landed, 16)
            with nc.allow_non_contiguous_dma(reason="256 positions, one to a partition"):
                load(pos_i[:, :], positions.rearrange("a (t p) -> (a p) t", p=P))
            load(g_norm[:, 0, :, :], norm1_g.rearrange("l (p k) -> p l k", k=KD))
            load(g_norm[:, 1, :, :], norm2_g.rearrange("l (p k) -> p l k", k=KD))
            load(g_qk[:, :, 0, :], q_norm_g.partition_broadcast(P))
            load(g_qk[:, :, 1, :], k_norm_g.partition_broadcast(P))
            load(g_conv[:, :, :], conv_out_g.rearrange("l (p k) -> p l k", k=KC))
            load(g_attn[:, :, :], attn_out_g.rearrange("l (p k) -> p l k", k=KC))
            for l in range(L):
                load(w_conv[:, l, :, :], conv_w[l].rearrange("r (p k) -> p r k", k=KC))
            for l in range(L):
                load(mod_b[:, l, :, :], b_ada[l].rearrange("(v p k) -> p v k", p=P, k=KD))
            load(r_b[:, :, 0:NG], b_rg.partition_broadcast(P))
            load(r_b[:, :, NG:NR], b_re.partition_broadcast(P))
            for l in range(L):
                load(r_w[:, l, :, 0:NG], w_rg[l].rearrange("(p k) n -> p k n", k=KD))
            for l in range(L):
                load(r_w[:, l, :, NG:NR], w_re[l].rearrange("(p k) n -> p k n", k=KD))

            def split(n):
                r = slot_of_unit[("w", n)]
                act.wait_ge(raw_full[r], landed[("w", n)])
                if n >= RING:
                    act.wait_ge(unit_used, n - RING + 1)
                act.activation(whi[:, n % RING, :], raw[:, r, :], ACT.Copy).then_inc(hi_done, 1)

            def ahead(n):
                if n < NU:
                    split(n)

            def ada_out(v, b):
                q = place_of[v]
                act.wait_ge(acc_done, 2 * q + b + 1)
                if b == 0 and q > 0:
                    act.wait_ge(mod_used, q)
                act.activation(mod_rows[:, b * 512:(b + 1) * 512], ps[:, 6, :], ACT.Copy
                               ).then_inc(mod_evac, 1)

            def gate_biases(l):
                if l > 0:
                    act.wait_ge(res_ready, l)
                for h in range(2):
                    c0 = (3 * h + 2) * D
                    act.dma_start(gates[:, h, :], b_ada[l, c0:c0 + D].partition_broadcast(P)
                                  ).then_inc(gate_bias, 16)

            def norm_root(m):
                for t in range(T):
                    act.wait_ge(rstd_sum, T * m + t + 1)
                    act.activation(stat[:, 2 + t:3 + t], stat[:, t:t + 1], ACT.Sqrt, scale=1.0 / D,
                                   bias=eps_col).then_inc(rstd_root, 1)

            def norm_evac(m, with_ada=False):
                act.wait_ge(mod_ready, m + 1)
                for bank in range(4):
                    act.wait_ge(xT_done, 4 * m + bank + 1)
                    for j in (2 * bank, 2 * bank + 1):
                        ins = act.activation(hf[:, j, :], ps[:, bank, (j % 2) * S:(j % 2 + 1) * S],
                                             ACT.Identity, scale=mod_t[:, m % 2, 1, j:j + 1],
                                             bias=mod_t[:, m % 2, 0, j:j + 1])
                    ins.then_inc(hf_ready, 1)
                    if with_ada and bank == 1:
                        ada_out((m // 2 + 1, 1), 0)

            act.wait_ge(c_landed, 16)
            eps_col = stat[:, 63:64]
            act.wait_ge(crep_ready, 1)
            link(act.activation(stat[:, 40:40 + KD], c_col[:, :], ACT.Silu))
            act.activation(c_rep[:, :, :], stat[:, 40:40 + KD].unsqueeze(2).to_broadcast([P, KD, 32]),
                           ACT.Copy).then_inc(crep_ready, 1)
            norm_root(0)
            for b in range(2):
                ada_out((0, 0), b)
            act.wait_ge(crep_ready, 3)
            act.activation(sincos[:, :, :, :], ang[:, 0:2, :, :], ACT.Sin).then_inc(crep_ready, 1)
            ada_out((0, 1), 0)
            split(0)
            ada_out((0, 1), 1)
            norm_evac(0)
            for n in range(1, RING):
                split(n)
            for l in range(L):
                n0 = l * UL
                m = 2 * l
                if l > 0:
                    norm_root(m)
                    norm_evac(m)
                gate_biases(l)
                split(n0 + 4)
                split(n0 + 5)
                for w in range(2):
                    act.wait_ge(unit_used, n0 + 2 * w + 2)
                    bank = (4, 0)[w]
                    for t in range(T):
                        ins = act.activation(tokmaj[:, t, w * AW:(w + 1) * AW], ps[:, bank + t, :],
                                             ACT.Copy)
                    ins.then_inc(proj_evac, 1)
                    ada_out((l, 2), w)
                    if w == 0:
                        split(n0 + 6)
                        split(n0 + 7)
                split(n0 + 8)
                split(n0 + 9)
                act.wait_ge(unit_used, n0 + 6)
                act.activation(v_sb[:, :, :], ps[:, 2:4, :], ACT.Copy).then_inc(proj_evac, 1)
                act.wait_ge(qk_sum, l + 1)
                act.activation(stat[:, 4:36], stat[:, 4:36], ACT.Sqrt, scale=1.0 / HD,
                               bias=eps_col).then_inc(qk_root, 1)
                act.wait_ge(unit_used, n0 + 8)
                act.activation(cb[:, :, :], ps[:, 4:6, :].rearrange("p a (b s) -> p (a b) s", s=S),
                               ACT.Copy).then_inc(proj_evac, 1)
                split(n0 + 10)
                split(n0 + 11)
                ada_out((l, 3), 0)
                act.wait_ge(unit_used, n0 + 10)
                act.activation(cc[:, :, :], ps[:, 0:2, :].rearrange("p a (b s) -> p (a b) s", s=S),
                               ACT.Copy).then_inc(proj_evac, 1)
                ada_out((l, 3), 1)
                for w in range(2):
                    act.wait_ge(qkT_done, 2 * l + w + 1)
                    bank = (4, 0)[w]
                    act.activation(qkT[:, w, :, :],
                                   ps[:, bank:bank + 2, :].rearrange("p a (b s) -> p (a b) s", s=S),
                                   ACT.Copy).then_inc(qkT_ready, 1)
                    split(n0 + 12 + w)

                def exps(u):
                    act.wait_ge(max_ready, 4 * l + u + 1)
                    for h in (2 * u, 2 * u + 1):
                        for t in range(T):
                            cols = slice(0, P) if t == 0 else slice(P, 384)
                            ins = act.activation(work[:, h // 4, h % 4, cols], work[:, h // 4, h % 4, cols],
                                                 ACT.Exp, bias=stat[:, 4 + 8 * t + h:5 + 8 * t + h],
                                                 accum_out=stat[:, 20 + 8 * t + h:21 + 8 * t + h])
                    ins.then_inc(exp_done, 1)

                def pT_out(u):
                    act.wait_ge(pT_done, 4 * l + u + 1)
                    b0 = PAIR_BANK[u]
                    act.activation(work[:, u // 2, 2 * (u % 2):2 * (u % 2) + 2, :], ps[:, b0:b0 + 2, 0:384],
                                   ACT.Copy).then_inc(pT_ready, 1)

                exps(0)
                exps(1)
                ada_out((l, 4), 0)
                pT_out(0)
                exps(2)
                pT_out(1)
                ada_out((l, 4), 1)
                pT_out(2)
                exps(3)
                split(n0 + 14)
                pT_out(3)
                act.wait_ge(yconv_ready, l + 1)
                act.activation(cb[:, :, :], cc[:, :, :], ACT.Square).then_inc(csq_ready, 1)
                ada_out((l, 5), 0)
                act.wait_ge(csum_done, l + 1)
                act.activation(cb[:, 0, :], ps[:, 4, 0:S], ACT.Sqrt, scale=1.0 / CW,
                               bias=eps_col).then_inc(croot, 1)
                ada_out((l, 5), 1)
                split(n0 + 15)
                act.wait_ge(yatt_sum, l + 1)
                act.activation(stat[:, 2:4], stat[:, 0:2], ACT.Sqrt, scale=1.0 / AW,
                               bias=eps_col).then_inc(yatt_root, 1)
                act.wait_ge(yT_done, l + 1)
                for j in range(KC):
                    ins = act.activation(hf[:, KC + j, :], ps[:, 4 + j // 2, (j % 2) * S:(j % 2 + 1) * S],
                                         ACT.Copy, scale=g_attn[:, l, j:j + 1])
                ins.then_inc(yf_ready, 1)
                if l + 1 < L:
                    ada_out((l + 1, 0), 0)
                    ada_out((l + 1, 0), 1)
                m = 2 * l + 1
                norm_root(m)
                norm_evac(m, l + 1 < L)
                if l + 1 < L:
                    ada_out((l + 1, 1), 1)
                split(n0 + 16)
                split(n0 + 17)

                def group_in(g):
                    if g > 0:
                        act.wait_ge(group_ready, 2 * (NG * l + g))
                    for k in range(KD):
                        if k % 4 == 0:
                            act.wait_ge(gather_done, 2 * (NG * l + g) + k // 4 + 1)
                        ins = act.activation(hg[:, k, :], ps[:, 6 + k // 4, (k % 4) * P:(k % 4 + 1) * P],
                                             ACT.Identity, scale=mod_t[:, 1, 1, k:k + 1],
                                             bias=mod_t[:, 1, 0, k:k + 1])
                        if k % 4 == 3:
                            ins.then_inc(hg_ready, 1)

                group_in(0)
                split(n0 + 18)
                act.wait_ge(rexp_in, 2 * l + 1)
                act.activation(rt[:, 8, :, 0:NG], rt[:, 8, :, 0:NG], ACT.Exp).then_inc(rexp_out, 1)
                act.wait_ge(rexp_in, 2 * l + 2)
                act.activation(stat[:, 36:38], stat[:, 36:38], ACT.Exp).then_inc(rexp_out, 1)
                split(n0 + 19)
                for e in range(NE):
                    E = l * NE + e
                    act.wait_ge(unit_used, n0 + 16 + gu_unit(e, 1) + 1)
                    if e >= 2:
                        act.wait_ge(hid_ready, E - 1)
                    act.activation(sil[:, e % 2, :], ps[:, e % 2, 0:F], ACT.Silu).then_inc(sil_done, 1)
                    if e == 0:
                        act.wait_ge(selT_done, l + 1)
                        act.activation(selT, ps[:, 4:6, :].rearrange("p a (b s) -> p (a b) s", s=P)
                                       .rearrange("p (g t) s -> p g t s", g=NG), ACT.Copy).then_inc(selT_ready, 1)
                        split(n0 + 20)
                    if e % EG == 2 and e // EG + 1 < NG:
                        group_in(e // EG + 1)
                    ahead(n0 + 16 + 3 * e + 5)
                    act.wait_ge(hidT_done, E + 1)
                    if e >= 2:
                        act.wait_ge(unit_used, n0 + 16 + down_unit(e - 2) + 1)
                    act.activation(hidT_hi[:, e % 2, :, :], ps[:, 2, 0:2 * P].rearrange("p (k s) -> p k s", k=2),
                                   ACT.Copy).then_inc(hidT_hi_done, 1)
                    ahead(n0 + 16 + 3 * e + 6)
                    if e < NE - 1:
                        ahead(n0 + 16 + 3 * e + 7)

                act.wait_ge(over_known, l + 1)
                with act.If(act.value_load(over_i[0:1, l, 0:1], min_val=0, max_val=1) > 0):
                    act.wait_ge(x_in, l + 1)
                    for k in range(KD):
                        act.activation(hg[:, k, :], ps[:, 6 + k // 4, (k % 4) * P:(k % 4 + 1) * P],
                                       ACT.Identity, scale=mod_t[:, 1, 1, k:k + 1],
                                       bias=mod_t[:, 1, 0, k:k + 1])
                    act.activation(selT[:, 0, :, :], ps[:, 1, 0:T * P].rearrange("p (t s) -> p t s", t=T),
                                   ACT.Copy).then_inc(x_hg, 1)
                    for i in range(EG):
                        act.wait_ge(x_used, 3 * EG * l + 3 * i + 2)
                        act.activation(sil[:, 0, :], ps[:, 0, 0:F], ACT.Silu).then_inc(x_sil, 1)
                        act.wait_ge(x_hidT, EG * l + i + 1)
                        act.activation(hidT_x, ps[:, 2, 0:2 * P].rearrange("p (k s) -> p k s", k=2),
                                       ACT.Copy).then_inc(x_hidT_out, 1)
                with act.Else():
                    act.sem_inc(x_hg, 1)
                    act.sem_inc(x_sil, EG)
                    act.sem_inc(x_hidT_out, EG)

        @block.vector
        def _(dve):
            steps = [0]

            def link(ins):
                steps[0] += 1
                ins.then_inc(dve_step, 1)
                dve.wait_ge(dve_step, steps[0])

            x_steps = [0]

            def x_link(ins):
                x_steps[0] += 1
                ins.then_inc(x_step, 1)
                dve.wait_ge(x_step, x_steps[0])

            def split(n):
                dve.wait_ge(hi_done, n + 1)
                dve.tensor_tensor(wlo[:, n % RING, :], raw[:, slot_of_unit[("w", n)], :],
                                  whi[:, n % RING, :].bitcast(F32), ALU.subtract).then_inc(lo_done, 1)

            def ahead(n):
                if n < NU:
                    split(n)

            def token_stat(m, t):
                dve.tensor_tensor_reduce(out=tokmaj[:, t, :], in0=res[:, t, :], in1=res[:, t, :],
                                         scale=1.0, scalar=0.0, op0=ALU.mult, op1=ALU.add,
                                         accum_out=stat[:, t:t + 1]).then_inc(rstd_sum, 1)

            def token_scale(m):
                for t in range(T):
                    dve.wait_ge(rstd_root, T * m + t + 1)
                    link(dve.reciprocal(stat[:, t:t + 1], stat[:, 2 + t:3 + t]))
                    dve.tensor_scalar(tokmaj[:, t, :], res[:, t, :], stat[:, t:t + 1], None, ALU.mult
                                      ).then_inc(xn_ready, 1)

            dve.memset(stat[:, 63:64], EPS).then_inc(crep_ready, 1)
            link(dve.memset(rowsel[:, :], 0.0))
            for q in range(4):
                last = dve.memset(rowsel[32 * q:32 * q + 1, :], 1.0)
            last.then_inc(rowsel_ready, 1)
            dve.wait_ge(x_landed, 16)
            for t in range(T):
                token_stat(0, t)
            token_scale(0)
            dve.wait_ge(par_in, 16 * NPAR)
            link(dve.tensor_copy(pos_f[:, :], pos_i[:, :]))
            dve.wait_ge(const_ready, 5)
            dve.tensor_copy(slots[:, :], slots_i)
            for t in range(T):
                last = dve.tensor_scalar(ang[:, 0, t, :], invf[:, :], pos_f[:, t:t + 1], None, ALU.mult)
            link(last)
            link(dve.tensor_scalar(ang[:, 1, :, :], ang[:, 0, :, :], 1.0 / (2 * np.pi), TOP_MAGIC,
                                   ALU.mult, ALU.add))
            link(dve.tensor_scalar(ang[:, 2, :, :], ang[:, 1, :, :], -TOP_MAGIC, None, ALU.add))
            for part in (TWO_PI_A, TWO_PI_B, TWO_PI_C):
                link(dve.scalar_tensor_tensor(out=ang[:, 0, :, :], in0=ang[:, 2, :, :], scalar=-float(part),
                                              in1=ang[:, 0, :, :], op0=ALU.mult, op1=ALU.add))
            link(dve.tensor_scalar(ang[:, 1, :, :], ang[:, 0, :, :], float(np.pi / 2), None, ALU.add))
            link(dve.tensor_scalar(ang[:, 2, :, :], ang[:, 1, :, :], float(np.pi), None, ALU.is_gt))
            link(dve.scalar_tensor_tensor(out=ang[:, 1, :, :], in0=ang[:, 2, :, :], scalar=-float(2 * np.pi),
                                          in1=ang[:, 1, :, :], op0=ALU.mult, op1=ALU.add))
            dve.wait_ge(crep_ready, 2)
            dve.tensor_scalar(ang[:, 0:2, :, :], ang[:, 0:2, :, :], PI_IN, -PI_IN, ALU.min, ALU.max
                              ).then_inc(crep_ready, 1)
            link(dve.tensor_copy(r_hi[:, :, :, :], r_w[:, :, :, :]))
            link(dve.tensor_tensor(r_lo[:, :, :, :], r_w[:, :, :, :], r_hi[:, :, :, :].bitcast(F32),
                                   ALU.subtract))
            dve.wait_ge(crep_ready, 4)

            def modulation(a):
                l, h = a // 2, a % 2
                dve.wait_ge(mod_used, place_of[(l, 3 * h + 1)] + 1)
                if a >= 2:
                    dve.wait_ge(hg_ready, 2 * NG * l)
                link(dve.tensor_tensor(mod_t[:, h, :, :], ps[:, 7, 0:2 * KD].rearrange("p (v k) -> p v k", v=2),
                                       mod_b[:, l, 3 * h:3 * h + 2, :], ALU.add))
                scaled(l, h)

            def scaled(l, h):
                dve.scalar_tensor_tensor(out=mod_t[:, h, 1, :], in0=mod_t[:, h, 1, :], scalar=1.0,
                                         in1=g_norm[:, h, l, :], op0=ALU.add, op1=ALU.mult
                                         ).then_inc(mod_ready, 1)

            def next_shift(l):
                dve.wait_ge(mod_used, place_of[(l + 1, 0)] + 1)
                dve.tensor_tensor(mod_t[:, 0, 0, :], ps[:, 7, 0:KD], mod_b[:, l + 1, 0, :], ALU.add
                                  ).then_inc(shift_ready, 1)

            def next_scale(l):
                dve.wait_ge(mod_used, place_of[(l + 1, 1)] + 1)
                link(dve.tensor_tensor(mod_t[:, 0, 1, :], ps[:, 2, 0:KD], mod_b[:, l + 1, 1, :], ALU.add))
                scaled(l + 1, 0)

            def gate_add(l, h):
                dve.wait_ge(mod_used, place_of[(l, 3 * h + 2)] + 1)
                dve.wait_ge(gate_bias, 32 * (l + 1))
                g2 = gates[:, h, :].rearrange("p (a b) -> p a b", a=2)
                dve.tensor_tensor(g2, g2, ps[:, 6:8, :], ALU.add).then_inc(gate_ready, 1)

            def activation_parts(m, banks):
                for bank in banks:
                    dve.wait_ge(hf_ready, 4 * m + bank + 1)
                    js = slice(2 * bank, 2 * bank + 2)
                    link(dve.tensor_copy(act_hi[:, js, :], hf[:, js, :]))
                    dve.tensor_tensor(act_lo[:, js, :], hf[:, js, :], act_hi[:, js, :].bitcast(F32),
                                      ALU.subtract).then_inc(act_ready, 1)

            def residual(l, t, n):
                cols = slice(n * 512, (n + 1) * 512)
                link(dve.tensor_tensor(tokmaj[:, t, cols], ps[:, 2 * t + n, :], gates[:, 0, cols], ALU.mult))
                link(dve.tensor_tensor(res[:, t, cols], res[:, t, cols], tokmaj[:, t, cols], ALU.add))

            def half_stat(t, n, out):
                cols = slice(n * 512, (n + 1) * 512)
                return dve.tensor_tensor_reduce(out=tokmaj[:, t, cols], in0=res[:, t, cols], in1=res[:, t, cols],
                                                scale=1.0, scalar=0.0, op0=ALU.mult, op1=ALU.add,
                                                accum_out=out)

            split(0)
            modulation(0)
            for l in range(L):
                n0 = l * UL
                if l > 0:
                    for t in range(T):
                        token_stat(2 * l, t)
                    token_scale(2 * l)
                activation_parts(2 * l, range(0, 2))
                activation_parts(2 * l, range(2, 4))
                for n in range(1 if l == 0 else RING - 1, RING):
                    split(n0 + n)
                for w in range(2):
                    for s in range(2):
                        for half in range(2):
                            hs = slice(half * HH, half * HH + HH)
                            ins = dve.tensor_tensor(
                                trig[:, s, :, w, hs], sincos[:, 1 - s, :, :],
                                g_qk[:, l, w, hs].unsqueeze(1).to_broadcast([P, T, HH]), ALU.mult)
                link(ins)
                split(n0 + 4)
                split(n0 + 5)
                split(n0 + 6)
                split(n0 + 7)
                dve.wait_ge(proj_evac, 5 * l + 2)
                for t in range(T):
                    link(dve.tensor_tensor(wflat[:, t * 1024:(t + 1) * 1024], tokmaj[:, t, :],
                                           tokmaj[:, t, :], ALU.mult))
                dve.tensor_reduce(stat[:, 4:36], wflat[:, 0:2048].rearrange("p (h d) -> p h d", d=HD),
                                  AX.X, ALU.add).then_inc(qk_sum, 1)
                split(n0 + 8)
                split(n0 + 9)
                gate_add(l, 0)
                dve.wait_ge(qk_root, l + 1)
                link(dve.reciprocal(stat[:, 4:36], stat[:, 4:36]))
                for t in range(T):
                    qk = tokmaj[:, t, :].rearrange("p (h d) -> p h d", d=HD)
                    link(dve.tensor_tensor(qk, qk, stat[:, 4 + 16 * t:20 + 16 * t].unsqueeze(2)
                                           .to_broadcast([P, 2 * H, HD]), ALU.mult))
                    parts = [wflat[:, s * 1024:(s + 1) * 1024] for s in range(2)]
                    for s in range(2):
                        for w in range(2):
                            ins = dve.tensor_tensor(
                                parts[s][:, w * AW:(w + 1) * AW].rearrange("p (h d) -> p h d", d=HD),
                                tokmaj[:, t, w * AW:(w + 1) * AW].rearrange("p (h d) -> p h d", d=HD),
                                trig[:, s, t, w, :].unsqueeze(1).to_broadcast([P, H, HD]), ALU.mult)
                    link(ins)
                    xc, xs = (q.rearrange("p (h a d) -> p h a d", a=2, d=HH) for q in parts)
                    q4 = tokmaj[:, t, :].rearrange("p (h a d) -> p h a d", a=2, d=HH)
                    dve.tensor_tensor(q4[:, :, 0, :], xc[:, :, 0, :], xs[:, :, 1, :], ALU.subtract)
                    ins = dve.tensor_tensor(q4[:, :, 1, :], xc[:, :, 1, :], xs[:, :, 0, :], ALU.add)
                    ins.then_inc(rope_done, 1)
                    dve.wait_ge(rope_done, T * l + t + 1)
                split(n0 + 10)
                split(n0 + 11)
                dve.wait_ge(proj_evac, 5 * l + 5)
                dve.wait_ge(unit_used, n0 + 12)
                dve.tensor_tensor(cg[:, :, 2:S + 2], cc[:, :, :],
                                  ps[:, 2:4, :].rearrange("p a (b s) -> p (a b) s", s=S), ALU.mult
                                  ).then_inc(gated_done, 1)
                split(n0 + 12)
                split(n0 + 13)

                def softmax_max(u):
                    dve.wait_ge(scores_done, 4 * l + u + 1)
                    b0 = PAIR_BANK[u]
                    rows = work[:, u // 2, 2 * (u % 2):2 * (u % 2) + 2, :]
                    link(dve.scalar_tensor_tensor(out=rows, in0=ps[:, b0:b0 + 2, 0:384], scalar=SCALE,
                                                  in1=mask[:, :].unsqueeze(1).to_broadcast([P, 2, 384]),
                                                  op0=ALU.mult, op1=ALU.add))
                    for t in range(T):
                        cols = slice(0, P) if t == 0 else slice(P, 384)
                        ins = dve.tensor_reduce(stat[:, 4 + 8 * t + 2 * u:6 + 8 * t + 2 * u],
                                                rows[:, :, cols], AX.X, ALU.max, negate=True)
                    ins.then_inc(max_ready, 1)

                def heads_out(u):
                    b0 = PAIR_BANK[u]
                    dve.wait_ge(exp_done, 4 * l + u + 1)
                    sums = stat[:, 20:36].rearrange("p (t h) -> p t h", t=T)[:, :, 2 * u:2 * u + 2]
                    link(dve.reciprocal(sums, sums))
                    dve.wait_ge(pv_done, 4 * l + u + 1)
                    for t in range(T):
                        ins = dve.tensor_tensor(
                            tokmaj[:, t, 2 * u * HD:2 * (u + 1) * HD].rearrange("p (h d) -> p h d", d=HD),
                            ps[:, b0:b0 + 2, 384 + t * HD:384 + (t + 1) * HD],
                            stat[:, 20 + 8 * t + 2 * u:22 + 8 * t + 2 * u].unsqueeze(2)
                            .to_broadcast([P, 2, HD]), ALU.mult)
                    ins.then_inc(yatt_raw, 1)

                softmax_max(0)
                softmax_max(1)
                softmax_max(2)
                dve.wait_ge(gated_done, l + 1)
                for j in range(KC):
                    if j == KC - 1:
                        heads_out(0)
                    taps = [w_conv[:, l, k, j:j + 1] for k in range(3)]
                    link(dve.tensor_scalar(cc[:, j, :], cg[:, j, 0:S], taps[0], None, ALU.mult))
                    for k in (1, 2):
                        link(dve.scalar_tensor_tensor(out=cc[:, j, :], in0=cg[:, j, k:k + S], scalar=taps[k],
                                                      in1=cc[:, j, :], op0=ALU.mult, op1=ALU.add))
                softmax_max(3)
                dve.tensor_tensor(cc[:, :, :], cc[:, :, :], cb[:, :, :], ALU.mult).then_inc(yconv_ready, 1)
                heads_out(1)
                heads_out(2)
                split(n0 + 14)
                modulation(2 * l + 1)
                dve.wait_ge(croot, l + 1)
                link(dve.reciprocal(cb[:, 1, :], cb[:, 0, :]))
                for j in range(KC):
                    ins = dve.scalar_tensor_tensor(out=cc[:, j, :], in0=cc[:, j, :],
                                                   scalar=g_conv[:, l, j:j + 1], in1=cb[:, 1, :],
                                                   op0=ALU.mult, op1=ALU.mult)
                link(ins)
                link(dve.tensor_copy(act_hi[:, 0:KC, :], cc[:, :, :]))
                dve.tensor_tensor(act_lo[:, 0:KC, :], cc[:, :, :], act_hi[:, 0:KC, :].bitcast(F32),
                                  ALU.subtract).then_inc(ymc_ready, 1)
                heads_out(3)
                dve.wait_ge(yatt_raw, 4 * (l + 1))
                for t in range(T):
                    ins = dve.tensor_tensor_reduce(out=tokmaj[:, t, AW:2 * AW], in0=tokmaj[:, t, 0:AW],
                                                   in1=tokmaj[:, t, 0:AW], scale=1.0, scalar=0.0,
                                                   op0=ALU.mult, op1=ALU.add, accum_out=stat[:, t:t + 1])
                ins.then_inc(yatt_sum, 1)
                dve.wait_ge(yatt_root, l + 1)
                link(dve.reciprocal(stat[:, 0:2], stat[:, 2:4]))
                for t in range(T):
                    ins = dve.tensor_scalar(tokmaj[:, t, 0:AW], tokmaj[:, t, 0:AW], stat[:, t:t + 1], None,
                                            ALU.mult)
                ins.then_inc(yatt_ready, 1)
                gate_add(l, 1)
                split(n0 + 15)
                dve.wait_ge(yf_ready, l + 1)
                link(dve.tensor_copy(act_hi[:, KC:KD, :], hf[:, KC:KD, :]))
                dve.tensor_tensor(act_lo[:, KC:KD, :], hf[:, KC:KD, :], act_hi[:, KC:KD, :].bitcast(F32),
                                  ALU.subtract).then_inc(yma_ready, 1)
                dve.wait_ge(gate_ready, 2 * l + 1)
                dve.wait_ge(row_done, 2 * l + 1)
                for n in range(2):
                    residual(l, 0, n)
                token_stat(2 * l + 1, 0)
                dve.wait_ge(row_done, 2 * l + 2)
                residual(l, 1, 0)
                half_stat(1, 0, stat[:, 1:2])
                dve.wait_ge(unit_used, l * UL + 16)
                residual(l, 1, 1)
                link(half_stat(1, 1, stat[:, 60:61]))
                dve.tensor_tensor(stat[:, 1:2], stat[:, 1:2], stat[:, 60:61], ALU.add).then_inc(rstd_sum, 1)
                token_scale(2 * l + 1)
                activation_parts(2 * l + 1, range(4))
                if l + 1 < L:
                    next_shift(l)
                dve.wait_ge(logitT_done, l + 1)
                dve.tensor_copy(logitT, ps[0:NR, 0, 0:S]).then_inc(logitT_ready, 1)
                dve.wait_ge(logit_done, l + 1)
                lg = rt[:, 0, :, :]
                link(dve.tensor_tensor(lg, ps[:, 0, S:S + T * NR].rearrange("p (t n) -> p t n", t=T),
                                       r_b[:, l, :].unsqueeze(1).to_broadcast([P, T, NR]), ALU.add))

                def col(i):
                    return stat[:, i:i + T]

                def wide(ap, n):
                    return ap.unsqueeze(2).to_broadcast([P, T, n])

                def first_max(values, n, top, onehot):
                    link(dve.tensor_reduce(top, values, AX.X, ALU.max))
                    link(dve.tensor_tensor(onehot, values, wide(top, n), ALU.is_equal))
                    link(dve.tensor_tensor(onehot, onehot, rank[:, NE - n:NE].unsqueeze(1)
                                           .to_broadcast([P, T, n]), ALU.mult))
                    link(dve.tensor_reduce(col(50), onehot, AX.X, ALU.max))
                    link(dve.tensor_tensor(onehot, onehot, wide(col(50), n), ALU.is_equal))

                glog = lg[:, :, 0:NG]
                goh_c = rt[:, 6, :, 0:NG]
                goh, oh1, oh2, em = (rt[:, i, :, 0:n] for i, n in ((1, NG), (2, NE), (3, NE), (4, NE)))
                first_max(glog, NG, col(52), goh)
                dve.tensor_copy(goh_c, goh).then_inc(oh_ready, 1)
                dve.tensor_tensor(rt[:, 8, :, 0:NG], glog, wide(col(52), NG), ALU.subtract
                                  ).then_inc(rexp_in, 1)
                link(dve.tensor_scalar(slot_of[:, :, :], goh, -BIG, BIG, ALU.mult, ALU.add))
                dve.wait_ge(place_done, l + 1)
                link(dve.tensor_tensor(slot_of[:, :, :], slot_of[:, :, :],
                                       ps[:, 3, 0:T * NG].rearrange("p (t g) -> p t g", t=T), ALU.add))
                for g in range(NG):
                    for t in range(T):
                        ins = dve.tensor_scalar(sel[:, g, t, :], slots[:, :], slot_of[:, t, g:g + 1], None,
                                                ALU.is_equal)
                    ins.then_inc(sel_ready, 1)
                split(n0 + 16)
                dve.wait_ge(count_done, l + 1)
                link(dve.tensor_scalar(over[:, :], ps[:, 1, 0:NG], float(P), None, ALU.is_gt))
                dve.tensor_reduce(over_any[:, 0:1], over[:, :], AX.X, ALU.max)
                link(dve.tensor_tensor(rt[:, 7, 0, 0:NG], over[:, :], slots[:, 0:NG], ALU.mult))
                link(dve.tensor_reduce(over_any[:, 1:2], rt[:, 7, 0, 0:NG], AX.X, ALU.add))
                dve.tensor_copy(over_i[:, l, :], over_any[:, :]).then_inc(over_known, 1)
                link(dve.tensor_scalar(rt[:, 5, :, 0:NG], goh, -1.0, -NEG, ALU.add, ALU.mult))
                for t in range(T):
                    e4 = rt[:, 4, t, 0:NE].rearrange("p (g e) -> p g e", e=EG)
                    link(dve.tensor_tensor(e4, rt[:, 0, t, NG:NR].rearrange("p (g e) -> p g e", e=EG),
                                           rt[:, 1, t, 0:NG].unsqueeze(2).to_broadcast([P, NG, EG]),
                                           ALU.mult))
                    link(dve.tensor_tensor(e4, e4, rt[:, 5, t, 0:NG].unsqueeze(2)
                                           .to_broadcast([P, NG, EG]), ALU.add))
                first_max(em, NE, col(54), oh1)

                def group_parts(g):
                    if g >= 2:
                        dve.wait_ge(unit_used, n0 + 16 + gu_unit(EG * (g - 1) - 1, 1) + 1)
                    cols = slice((g % 2) * P, (g % 2 + 1) * P)
                    for half in range(2):
                        dve.wait_ge(hg_ready, 2 * (NG * l + g) + half + 1)
                        ks = slice(4 * half, 4 * half + 4)
                        link(dve.tensor_copy(act_hi[:, ks, cols], hg[:, ks, :]))
                        dve.tensor_tensor(act_lo[:, ks, cols], hg[:, ks, :], act_hi[:, ks, cols].bitcast(F32),
                                          ALU.subtract).then_inc(group_ready, 1)

                def group_out(g):
                    dve.wait_ge(unit_used, n0 + 16 + down_unit(EG * g + EG - 1) + 1)
                    if g > 0:
                        dve.wait_ge(scatter_done, T * (NG * l + g))
                    dve.tensor_tensor(y_sb.rearrange("p (a b) -> p a b", a=2), ps[:, 4:6, :],
                                      gates[:, 1, :].rearrange("p (a b) -> p a b", a=2), ALU.mult
                                      ).then_inc(y_ready, 1)

                def spread_in(g, t):
                    dve.wait_ge(scatter_done, T * (NG * l + g) + t + 1)
                    row = res[:, t, :].rearrange("p (a b) -> p a b", a=2)
                    bank = spread_bank(g, t)
                    dve.tensor_tensor(row, row, ps[:, bank:bank + 2, :], ALU.add).then_inc(scatter_used, 1)

                group_parts(0)
                split(n0 + 17)
                link(dve.scalar_tensor_tensor(out=em, in0=oh1, scalar=10 * NEG, in1=em, op0=ALU.mult,
                                              op1=ALU.add))
                first_max(em, NE, col(56), oh2)
                dve.tensor_tensor(stat[:, 36:38], col(56), col(54), ALU.subtract).then_inc(rexp_in, 1)
                dve.wait_ge(rexp_out, 2 * l + 1)
                link(dve.tensor_reduce(col(58), rt[:, 8, :, 0:NG], AX.X, ALU.add))
                dve.wait_ge(rexp_out, 2 * l + 2)
                link(dve.tensor_scalar(col(60), stat[:, 36:38], 1.0, None, ALU.add))
                link(dve.tensor_tensor(col(60), col(60), col(58), ALU.mult))
                link(dve.reciprocal(col(60), col(60)))
                link(dve.tensor_tensor(stat[:, 38:40], stat[:, 36:38], col(60), ALU.mult))
                link(dve.tensor_tensor(oh1, oh1, wide(col(60), NE), ALU.mult))
                link(dve.tensor_tensor(oh2, oh2, wide(stat[:, 38:40], NE), ALU.mult))
                dve.tensor_tensor(combine[:, :, :], oh1, oh2, ALU.add).then_inc(comb_ready, 1)
                split(n0 + 18)
                if l + 1 < L:
                    next_scale(l)
                dve.wait_ge(cw_done, l + 1)
                link(dve.tensor_copy(cw[:, :], ps[:, 3, 16:16 + NE]))
                dve.wait_ge(gate_ready, 2 * l + 2)
                for e in range(NE):
                    E = l * NE + e
                    g = e // EG
                    dve.wait_ge(sil_done, E + 1)
                    if e >= 2:
                        dve.wait_ge(hidT_done, E - 1)
                    dve.scalar_tensor_tensor(out=hid[:, e % 2, :], in0=ps[:, e % 2, F:2 * F],
                                             scalar=cw[:, e:e + 1], in1=sil[:, e % 2, :],
                                             op0=ALU.mult, op1=ALU.mult).then_inc(hid_ready, 1)
                    if e == 0:
                        split(n0 + 19)
                        split(n0 + 20)
                    if e % EG == 0 and g > 0:
                        group_out(g - 1)
                    if e % EG == 2 and g + 1 < NG:
                        group_parts(g + 1)
                    if e < NE - 1:
                        ahead(n0 + 16 + 3 * e + 5)
                    dve.wait_ge(hidT_hi_done, E + 1)
                    dve.tensor_tensor(hidT_lo[:, e % 2, :, :], ps[:, 2, 0:2 * P].rearrange("p (k s) -> p k s", k=2),
                                      hidT_hi[:, e % 2, :, :].bitcast(F32), ALU.subtract).then_inc(hidT_ready, 1)
                    if e % EG < T and g > 0:
                        spread_in(g - 1, e % EG)
                    if e < NE - 1:
                        ahead(n0 + 16 + 3 * e + 6)
                        ahead(n0 + 16 + 3 * e + 7)
                ahead((l + 1) * UL + 2)
                group_out(NG - 1)
                for t in range(T):
                    spread_in(NG - 1, t)
                dve.wait_ge(over_known, l + 1)
                with dve.If(dve.value_load(over_i[0:1, l, 0:1], min_val=0, max_val=1) > 0):
                    dve.wait_ge(scatter_used, T * NG * (l + 1))
                    dve.wait_ge(selT_ready, l + 1)
                    for t in range(T):
                        x_link(dve.tensor_tensor(rt[:, 7, t, 0:NG], slot_of[:, t, :], over[:, :], ALU.mult))
                    x_link(dve.tensor_scalar(rt[:, 9, 0, 0:NG], over[:, :], -BIG, BIG, ALU.mult, ALU.add))
                    for t in range(T):
                        x_link(dve.tensor_tensor(rt[:, 7, t, 0:NG], rt[:, 7, t, 0:NG], rt[:, 9, 0, 0:NG], ALU.add))
                    x_link(dve.tensor_reduce(over_any[:, 0:T], rt[:, 7, :, 0:NG], AX.X, ALU.min))
                    for t in range(T):
                        x_link(dve.tensor_scalar(sel[:, 0, t, :], slots[:, :], over_any[:, t:t + 1], -float(P),
                                               ALU.subtract, ALU.is_equal))
                        x_link(dve.tensor_tensor(rt[:, 9, t, 0:NE].rearrange("p (e g) -> p e g", g=NG),
                                               combine[:, t, :].rearrange("p (g e) -> p e g", g=NG),
                                               over[:, :].unsqueeze(1).to_broadcast([P, EG, NG]), ALU.mult))
                        ins = dve.tensor_reduce(rt[:, 7, t, 0:EG],
                                                rt[:, 9, t, 0:NE].rearrange("p (e g) -> p e g", g=NG),
                                                AX.X, ALU.add)
                    ins.then_inc(x_sel, 1)
                    dve.wait_ge(x_in, l + 1)
                    dve.tensor_copy(cw[:, 0:EG], ps[:, 3, 0:EG]).then_inc(x_cw, 1)
                    dve.wait_ge(x_cw, l + 1)
                    for i in range(EG):
                        dve.wait_ge(x_sil, EG * l + i + 1)
                        dve.scalar_tensor_tensor(out=hid[:, 0, :], in0=ps[:, 0, F:2 * F], scalar=cw[:, i:i + 1],
                                                 in1=sil[:, 0, :], op0=ALU.mult, op1=ALU.mult
                                                 ).then_inc(x_hid, 1)
                    dve.wait_ge(x_used, 3 * EG * (l + 1))
                    dve.tensor_tensor(y_sb.rearrange("p (a b) -> p a b", a=2), ps[:, 4:6, :],
                                      gates[:, 1, :].rearrange("p (a b) -> p a b", a=2), ALU.mult
                                      ).then_inc(x_y, 1)
                    for t in range(T):
                        dve.wait_ge(x_back, T * l + t + 1)
                        row = res[:, t, :].rearrange("p (a b) -> p a b", a=2)
                        dve.tensor_tensor(row, row, ps[:, 6:8, :], ALU.add).then_inc(x_added, 1)
                with dve.Else():
                    dve.sem_inc(x_step, x_steps[0] // (l + 1))
                    dve.sem_inc(x_sel, 1)
                    dve.sem_inc(x_cw, 1)
                    dve.sem_inc(x_hid, EG)
                    dve.sem_inc(x_y, 1)
                    dve.sem_inc(x_added, T)
                dve.drain().then_inc(res_ready, 1)


        @block.tensor
        def _(pe):
            def wait_unit(n):
                pe.wait_ge(lo_done, n + 1)
                r = n % RING
                return whi[:, r, :], wlo[:, r, :]

            def ada_acc(v, b):
                q = place_of[v]
                if q > 0 or b > 0:
                    pe.wait_ge(mod_evac, 2 * q + b)
                if b == 0 and q > 0 and vectors[q - 1][1] % 3 == 2:
                    pe.wait_ge(gate_ready, 2 * vectors[q - 1][0] + vectors[q - 1][1] // 3 + 1)
                for k in range(KD):
                    unit = ("a", 4 * q + 2 * b + k // 4)
                    if k % 4 == 0:
                        pe.wait_ge(raw_full[slot_of_unit[unit]], landed[unit])
                    w = raw[:, slot_of_unit[unit], (k % 4) * 512:(k % 4 + 1) * 512]
                    ins = pe.matmul(ps[32 * (k % 4):32 * (k % 4) + 32, 6, :], c_rep[:, k, :], w,
                                    start=(k < 4), stop=(k >= 4), skip_group_check=True)
                    if k == 3:
                        ins.then_inc(ada_used, 1)
                ins.then_inc(acc_done, 1)

            def ada_sum(v):
                q = place_of[v]
                kind = v[1] % 3
                pe.wait_ge(mod_evac, 2 * q + 2)
                if kind < 2:
                    bank, c0 = (2, 0) if v[0] > 0 and v[1] == 1 else (7, kind * KD)
                    for j in range(KD):
                        ins = pe.matmul(ps[:, bank, c0 + j:c0 + j + 1], mod_rows[:, j::KD],
                                        rowsel[:, 0:1], start=True, stop=True)
                else:
                    pe.wait_ge(mod_ready, 2 * v[0] + v[1] // 3 + 1)
                    for n in range(2):
                        ins = pe.matmul(ps[:, 6 + n, :], rowsel[:, :], mod_rows[:, n * 512:(n + 1) * 512],
                                        start=True, stop=True)
                ins.then_inc(mod_used, 1)

            def transposes(m):
                for t in range(T):
                    pe.wait_ge(xn_ready, T * m + t + 1)
                    for bank in range(4):
                        for j in (2 * bank, 2 * bank + 1):
                            ins = pe.transpose(ps[:, bank, (j % 2) * S + t * P:(j % 2) * S + (t + 1) * P],
                                               tokmaj[:, t, j::KD], ident[:, :])
                        if t == T - 1:
                            ins.then_inc(xT_done, 1)

            acts = (act_hi, act_lo)

            pe.wait_ge(const_ready, 5)
            pe.wait_ge(rowsel_ready, 1)
            pe.wait_ge(crep_ready, 2)
            ada_acc((0, 0), 0)
            ada_acc((0, 0), 1)
            ada_sum((0, 0))
            transposes(0)
            ada_acc((0, 1), 0)
            ada_acc((0, 1), 1)
            ada_sum((0, 1))
            for l in range(L):
                n0 = l * UL
                if l > 0:
                    transposes(2 * l)
                for i in range(3):
                    bank = (4, 0, 2)[i]
                    for half in range(2):
                        w = wait_unit(n0 + 2 * i + half)
                        pe.wait_ge(act_ready, 4 * 2 * l + (4 if i else 2 * half + 2))
                        for kk in range(4):
                            k = 4 * half + kk
                            for t in range(T):
                                for p, (pa, pw) in enumerate(PASSES):
                                    ins = pe.matmul(ps[:, bank + t, :], acts[pa][:, k, t * P:(t + 1) * P],
                                                    w[pw][:, kk * 512:(kk + 1) * 512],
                                                    start=(k == 0 and p == 0), stop=(k == KD - 1 and p == 2))
                        ins.then_inc(unit_used, 1)
                    if i < 2:
                        ada_acc((l, 2), i)
                ada_sum((l, 2))

                def conv_block(i, bank):
                    for half in range(2):
                        w = wait_unit(n0 + 6 + 2 * i + half)
                        for kk in range(4):
                            k = 4 * half + kk
                            for j in range(KC):
                                for p, (pa, pw) in enumerate(PASSES):
                                    ins = pe.matmul(ps[:, bank + j // 2, (j % 2) * S:(j % 2 + 1) * S],
                                                    w[pw][:, kk * 512 + j:(kk + 1) * 512:KC],
                                                    acts[pa][:, k, :], start=(k == 0 and p == 0 and j % 2 == 0),
                                                    stop=(k == KD - 1 and p == 2), skip_group_check=True)
                        ins.then_inc(unit_used, 1)

                def qk_transposes(w):
                    bank = (4, 0)[w]
                    pe.wait_ge(proj_evac, 5 * l + 4 + w)
                    for cpair in range(H // 2):
                        for t in range(T):
                            a0 = (cpair % 2) * S + t * P
                            ins = pe.transpose(ps[:, bank + cpair // 2, a0:a0 + P],
                                               tokmaj[:, t, w * AW + cpair * P:w * AW + (cpair + 1) * P],
                                               ident[:, :])
                    ins.then_inc(qkT_done, 1)

                pe.wait_ge(proj_evac, 5 * l + 1)
                conv_block(0, 4)
                ada_acc((l, 3), 0)
                pe.wait_ge(proj_evac, 5 * l + 2)
                conv_block(1, 0)
                ada_acc((l, 3), 1)
                pe.wait_ge(rope_done, T * (l + 1))
                qk_transposes(0)
                qk_transposes(1)
                pe.wait_ge(proj_evac, 5 * l + 3)
                conv_block(2, 2)
                ada_sum((l, 3))

                def heads(u):
                    for h in (2 * u, 2 * u + 1):
                        yield h, PAIR_BANK[u] + h % 2, work[:, h // 4, h % 4, :]

                def scores(u):
                    for h, bank, _ in heads(u):
                        rows = slice((h % 2) * HD, (h % 2) * HD + HD)
                        for t in range(T):
                            cols = slice(0, P) if t == 0 else slice(P, 384)
                            ins = pe.matmul(ps[:, bank, cols], qkT[rows, 0, h // 2, t * P:(t + 1) * P],
                                            qkT[rows, 1, h // 2, 0:(t + 1) * P], start=True, stop=True)
                    ins.then_inc(scores_done, 1)

                def probs_T(u):
                    pe.wait_ge(exp_done, 4 * l + u + 1)
                    for h, bank, p in heads(u):
                        for q in range(3):
                            ins = pe.transpose(ps[:, bank, q * P:(q + 1) * P], p[:, q * P:(q + 1) * P],
                                               ident[:, :])
                    ins.then_inc(pT_done, 1)

                def values(u):
                    pe.wait_ge(pT_ready, 4 * l + u + 1)
                    for h, bank, p in heads(u):
                        vs = slice(h * HD, (h + 1) * HD)
                        y0, y1 = slice(384, 384 + HD), slice(384 + HD, 384 + 2 * HD)
                        pe.matmul(ps[:, bank, y0], p[:, 0:P], v_sb[:, 0, vs], start=True, stop=True)
                        pe.matmul(ps[:, bank, y1], p[:, P:2 * P], v_sb[:, 0, vs], start=True, stop=False)
                        ins = pe.matmul(ps[:, bank, y1], p[:, 2 * P:3 * P], v_sb[:, 1, vs], start=False,
                                        stop=True)
                    ins.then_inc(pv_done, 1)

                pe.wait_ge(qkT_ready, 2 * l + 2)
                scores(0)
                scores(1)
                ada_acc((l, 4), 0)
                pe.wait_ge(gated_done, l + 1)
                scores(2)
                probs_T(0)
                probs_T(1)
                ada_acc((l, 4), 1)
                values(0)
                probs_T(2)
                values(1)
                pe.wait_ge(yatt_raw, 4 * l + 1)
                scores(3)
                values(2)
                ada_sum((l, 4))
                probs_T(3)
                ada_acc((l, 5), 0)
                pe.wait_ge(csq_ready, l + 1)
                pe.wait_ge(yatt_raw, 4 * l + 2)
                for j in range(KC):
                    ins = pe.matmul(ps[:, 4, 0:S], ones[:, :], cb[:, j, :], start=(j == 0), stop=(j == KC - 1))
                ins.then_inc(csum_done, 1)
                values(3)
                ada_acc((l, 5), 1)
                ada_sum((l, 5))

                def out_proj(s, t, ns=range(2), last=True):
                    for half in range(2):
                        w = wait_unit(n0 + 12 + 2 * s + half)
                        for kk in range(2):
                            k = 4 * s + 2 * half + kk
                            for p, (pa, pw) in enumerate(PASSES):
                                for n in ns:
                                    c0 = kk * D + n * 512
                                    ins = pe.matmul(ps[:, 2 * t + n, :], acts[pa][:, k, t * P:(t + 1) * P],
                                                    w[pw][:, c0:c0 + 512], start=(k == 0 and p == 0),
                                                    stop=(k == KD - 1 and p == 2))
                        if t == T - 1 and last:
                            ins.then_inc(unit_used, 1)
                    return ins

                pe.wait_ge(ymc_ready, l + 1)
                pe.wait_ge(yatt_raw, 4 * (l + 1))
                for t in range(T):
                    out_proj(0, t)
                pe.wait_ge(yatt_ready, l + 1)
                for j in range(KC):
                    for t in range(T):
                        a0 = (j % 2) * S + t * P
                        ins = pe.transpose(ps[:, 4 + j // 2, a0:a0 + P], tokmaj[:, t, j:AW:KC], ident[:, :])
                ins.then_inc(yT_done, 1)
                if l + 1 < L:
                    ada_acc((l + 1, 0), 0)
                    ada_acc((l + 1, 0), 1)
                pe.wait_ge(yma_ready, l + 1)
                out_proj(1, 0).then_inc(row_done, 1)
                for n in range(2):
                    ins = out_proj(1, 1, range(n, n + 1), last=(n == 1))
                    if n == 0:
                        ins.then_inc(row_done, 1)
                if l + 1 < L:
                    ada_sum((l + 1, 0))
                transposes(2 * l + 1)
                if l + 1 < L:
                    ada_acc((l + 1, 1), 0)
                    ada_acc((l + 1, 1), 1)
                rw = (r_hi, r_lo)
                pe.wait_ge(xT_done, 4 * (2 * l + 2))
                pe.wait_ge(hf_ready, 4 * (2 * l + 1) + 1)
                for k in range(KD):
                    if k % 2 == 0:
                        pe.wait_ge(act_ready, 4 * (2 * l + 1) + k // 2 + 1)
                    for p, (pa, pw) in enumerate(PASSES):
                        ins = pe.matmul(ps[0:NR, 0, 0:S], rw[pw][:, l, k, :], acts[pa][:, k, :],
                                        start=(k == 0 and p == 0), stop=(k == KD - 1 and p == 2))
                ins.then_inc(logitT_done, 1)
                pe.wait_ge(logitT_ready, l + 1)
                for t in range(T):
                    ins = pe.transpose(ps[:, 0, S + t * NR:S + (t + 1) * NR], logitT[:, t * P:(t + 1) * P],
                                       ident[0:NR, 0:NR])
                ins.then_inc(logit_done, 1)
                pe.wait_ge(oh_ready, l + 1)
                goh = rt[:, 6, :, 0:NG]
                pe.matmul(ps[:, 3, 0:T * NG], before[:, :], goh, start=True, stop=False, skip_group_check=True)
                pe.matmul(ps[:, 3, NG:2 * NG], ones[:, :], goh[:, 0, :], start=False, stop=True,
                          skip_group_check=True).then_inc(place_done, 1)
                for t in range(T):
                    ins = pe.matmul(ps[:, 1, 0:NG], ones[:, :], goh[:, t, :], start=(t == 0),
                                    stop=(t == T - 1))
                ins.then_inc(count_done, 1)

                def gather(g):
                    if g == 0 and l + 1 < L:
                        pe.wait_ge(mod_evac, 2 * place_of[(l + 1, 1)] + 2)
                        pe.wait_ge(shift_ready, l + 1)
                    if g > 0:
                        pe.wait_ge(scatter_used, T * (NG * l + g - 1))
                        pe.wait_ge(hg_ready, 2 * (NG * l + g))
                    for k in range(KD):
                        for t in range(T):
                            ins = pe.matmul(ps[:, 6 + k // 4, (k % 4) * P:(k % 4 + 1) * P],
                                            tokmaj[:, t, k::KD], sel[:, g, t, :],
                                            start=(t == 0), stop=(t == T - 1))
                        if k % 4 == 3:
                            ins.then_inc(gather_done, 1)

                def scatter(g, t):
                    pe.wait_ge(y_ready, NG * l + g + 1)
                    if g < NG - 1:
                        pe.wait_ge(hg_ready, 2 * (NG * l + g + 1))
                    bank = spread_bank(g, t)
                    if t > 0 and bank == 6:
                        pe.wait_ge(scatter_used, T * (NG * l + g) + t)
                    for n in range(2):
                        ins = pe.matmul(ps[:, bank + n, :], selT[:, g, t, :], y_sb[:, n * 512:(n + 1) * 512],
                                        start=True, stop=True)
                    ins.then_inc(scatter_done, 1)

                def gate_up(e, half):
                    E = l * NE + e
                    g = e // EG
                    if e % EG == 0:
                        pe.wait_ge(group_ready, 2 * (NG * l + g) + half + 1)
                    if half == 0:
                        if e >= 2:
                            pe.wait_ge(hid_ready, E - 1)
                    w = wait_unit(n0 + 16 + gu_unit(e, half))
                    cols = slice((g % 2) * P, (g % 2 + 1) * P)
                    for kk in range(4):
                        k = 4 * half + kk
                        for p, (pa, pw) in enumerate(PASSES):
                            ins = pe.matmul(
                                ps[:, e % 2, :], acts[pa][:, k, cols],
                                w[pw].rearrange("p (g k f) -> p g k f", g=2, k=4)[:, :, kk, :],
                                start=(k == 0 and p == 0), stop=(k == KD - 1 and p == 2))
                    return ins

                def hid_transpose(e):
                    E = l * NE + e
                    pe.wait_ge(hid_ready, E + 1)
                    if E > 0:
                        pe.wait_ge(hidT_ready, E)
                    for kk in range(2):
                        ins = pe.transpose(ps[:, 2, kk * P:(kk + 1) * P], hid[:, e % 2, kk::2], ident[:, :])
                    ins.then_inc(hidT_done, 1)

                def down(e):
                    E = l * NE + e
                    g, i = e // EG, e % EG
                    w = wait_unit(n0 + 16 + down_unit(e))
                    pe.wait_ge(hidT_ready, E + 1)
                    if e == 0:
                        pe.wait_ge(selT_ready, l + 1)
                    if i == 0 and g > 0:
                        pe.wait_ge(y_ready, NG * l + g)
                    hT = (hidT_hi, hidT_lo)
                    for kk in range(2):
                        for p, (pa, pw) in enumerate(PASSES):
                            for n in range(2):
                                c0 = kk * D + n * 512
                                ins = pe.matmul(ps[:, 4 + n, :], hT[pa][:, e % 2, kk, :],
                                                w[pw][:, c0:c0 + 512], start=(i == 0 and kk == 0 and p == 0),
                                                stop=(i == EG - 1 and kk == 1 and p == 2))
                    ins.then_inc(unit_used, 1)

                pe.wait_ge(sel_ready, NG * l + 1)
                gather(0)
                pe.wait_ge(sel_ready, NG * (l + 1))
                for g in range(NG):
                    for t in range(T):
                        i = T * g + t
                        ins = pe.transpose(ps[:, 4 + i // 4, (i % 4) * P:(i % 4 + 1) * P], sel[:, g, t, :],
                                           ident[:, :])
                ins.then_inc(selT_done, 1)
                if l + 1 < L:
                    ada_sum((l + 1, 1))
                gate_up(0, 0).then_inc(unit_used, 1)
                gate_up(0, 1).then_inc(unit_used, 1)
                pe.wait_ge(comb_ready, l + 1)
                for g in range(NG):
                    for t in range(T):
                        ins = pe.matmul(ps[:, 3, 16 + EG * g:16 + EG * (g + 1)], sel[:, g, t, :],
                                        combine[:, t, EG * g:EG * (g + 1)], start=(t == 0), stop=(t == T - 1))
                ins.then_inc(cw_done, 1)
                for e in range(NE):
                    g, i = e // EG, e % EG
                    if e + 1 < NE:
                        gate_up(e + 1, 0).then_inc(unit_used, 1)
                    hid_transpose(e)
                    if e + 1 < NE:
                        gate_up(e + 1, 1).then_inc(unit_used, 1)
                    if i < T and g > 0:
                        scatter(g - 1, i)
                    down(e)
                    if i == 1 and g + 1 < NG:
                        gather(g + 1)
                for t in range(T):
                    scatter(NG - 1, t)
                pe.wait_ge(over_known, l + 1)
                with pe.If(pe.value_load(over_i[0:1, l, 0:1], min_val=0, max_val=1) > 0):
                    pe.wait_ge(x_sel, l + 1)
                    pe.wait_ge(scatter_used, T * NG * (l + 1))
                    for k in range(KD):
                        for t in range(T):
                            pe.matmul(ps[:, 6 + k // 4, (k % 4) * P:(k % 4 + 1) * P], tokmaj[:, t, k::KD],
                                      sel[:, 0, t, :], start=(t == 0), stop=(t == T - 1))
                    for t in range(T):
                        pe.transpose(ps[:, 1, t * P:(t + 1) * P], sel[:, 0, t, :], ident[:, :])
                    for t in range(T):
                        ins = pe.matmul(ps[:, 3, 0:EG], sel[:, 0, t, :], rt[:, 7, t, 0:EG], start=(t == 0),
                                        stop=(t == T - 1))
                    ins.then_inc(x_in, 1)
                    pe.wait_ge(x_hg, l + 1)
                    pe.wait_ge(x_cw, l + 1)
                    for i in range(EG):
                        loads = X_LOADS * l + 16 * 5 * i
                        if i > 0:
                            pe.wait_ge(x_hid, EG * l + i)
                        for half in range(2):
                            pe.wait_ge(x_full, loads + 32 * (half + 1))
                            w = stage.rearrange("p (g k f) -> p g k f", g=2, k=4)
                            for kk in range(4):
                                k = 4 * half + kk
                                ins = pe.matmul(ps[:, 0, :], hg[:, k, :], w[:, :, kk, :], start=(k == 0),
                                                stop=(k == KD - 1))
                            ins.then_inc(x_used, 1)
                        pe.wait_ge(x_hid, EG * l + i + 1)
                        for kk in range(2):
                            ins = pe.transpose(ps[:, 2, kk * P:(kk + 1) * P], hid[:, 0, kk::2], ident[:, :])
                        ins.then_inc(x_hidT, 1)
                        pe.wait_ge(x_full, loads + 80)
                        pe.wait_ge(x_hidT_out, EG * l + i + 1)
                        for kk in range(2):
                            for n in range(2):
                                c0 = kk * D + n * 512
                                ins = pe.matmul(ps[:, 4 + n, :], hidT_x[:, kk, :], stage[:, c0:c0 + 512],
                                                start=(i == 0 and kk == 0), stop=(i == EG - 1 and kk == 1))
                        ins.then_inc(x_used, 1)
                    pe.wait_ge(x_y, l + 1)
                    for t in range(T):
                        if t > 0:
                            pe.wait_ge(x_added, T * l + t)
                        for n in range(2):
                            ins = pe.matmul(ps[:, 6 + n, :], selT[:, 0, t, :], y_sb[:, n * 512:(n + 1) * 512],
                                            start=True, stop=True)
                        ins.then_inc(x_back, 1)
                with pe.Else():
                    pe.sem_inc(x_in, 1)
                    pe.sem_inc(x_used, 3 * EG)
                    pe.sem_inc(x_hidT, EG)
                    pe.sem_inc(x_back, T)


_INS = ["x", "c", "positions", "norm1_g", "norm2_g", "w_ada", "b_ada", "w_in", "conv_w", "q_norm_g",
        "k_norm_g", "conv_out_g", "attn_out_g", "w_out", "w_router_group", "b_router_group",
        "w_router_expert", "b_router_expert", "w_gate", "w_up", "w_down"]


def kernel(**inputs):
    import concourse.bacc as _bacc
    from concourse.bass_utils import run_bass_kernel_spmd as _run

    nc = _bacc.Bacc("TRN2", target_bir_lowering=False, num_devices=1, dynamic_dma_scratch_size=4096)
    arrays, args = {}, []
    for name in _INS:
        a = np.ascontiguousarray(inputs[name])
        arrays[f"in_{name}_dram"] = a
        args.append(nc.dram_tensor(f"in_{name}_dram", a.shape, mybir.dt.from_np(a.dtype),
                                   kind="ExternalInput").ap())
    shape = tuple(inputs["x"].shape)
    args.append(nc.dram_tensor("out_0_dram", shape, F32, kind="ExternalOutput").ap())
    trunk(nc, *args)
    r = _run(nc, [arrays], core_ids=[0])
    return r.results[0]["out_0_dram"]
```
